# Optimizing a Trainium2 kernel written in Bass

```python
import jax
import jax.numpy as jnp
from jax import lax
import numpy as np

D_MODEL = 1024
BATCH = 1
SEQ = 512
DEPTH = 2
DEC_BATCH = 1
DEC_SEQ = 512
PAST_LEN = 128

GRID_W = 64
HEAD_DIM = 64
EPS = 1e-6

ATTN_HEADS = 8
ATTN_KV_HEADS = 2
Q_BLOCK = 128
ROPE_THETA = 10000.0

GLA_HEADS = 4
GLA_RANK = 16
GLA_TAU = 16.0
GLA_CHUNK = 64

MLSTM_HEADS = 4
MLSTM_CHUNK = 64

ATTN_W = ATTN_HEADS * HEAD_DIM
KV_W = ATTN_KV_HEADS * HEAD_DIM
GLA_W = GLA_HEADS * HEAD_DIM
MLSTM_W = MLSTM_HEADS * HEAD_DIM
MIX_W = ATTN_W + GLA_W + MLSTM_W

D_FF = 2816
CONV_WIDTH = 3

IN_SPLITS = (ATTN_W, KV_W, KV_W,
             GLA_W, GLA_W, GLA_W, GLA_W, 2 * GLA_RANK,
             MLSTM_W, MLSTM_W, MLSTM_W, MLSTM_W, 4 * MLSTM_HEADS)
IN_DIM = sum(IN_SPLITS)

kernel_name = "hybrid_bidir_encoder_heads"

def rms_norm(x, g):
    xf = x.astype(jnp.float32)
    y = xf * lax.rsqrt(jnp.mean(xf * xf, axis=-1, keepdims=True) + EPS)
    return (y * g.astype(jnp.float32)).astype(x.dtype)

def axial_rope_tables(seq):
    n_rows = seq // GRID_W
    row = jnp.repeat(jnp.arange(n_rows, dtype=jnp.float32), GRID_W)
    col = jnp.tile(jnp.arange(GRID_W, dtype=jnp.float32), n_rows)
    n_freq = HEAD_DIM // 4
    inv_freq = jnp.power(ROPE_THETA, -jnp.arange(n_freq, dtype=jnp.float32) / n_freq)
    ang = jnp.stack([row[:, None] * inv_freq, col[:, None] * inv_freq], axis=1)
    return jnp.cos(ang), jnp.sin(ang)

def apply_axial_rope(x, cos, sin):
    b, s, h, d = x.shape
    xr = x.astype(jnp.float32).reshape(b, s, h, 2, 2, d // 4)
    x1, x2 = xr[..., 0, :], xr[..., 1, :]
    c = cos[None, :, None]
    sn = sin[None, :, None]
    out = jnp.stack([x1 * c - x2 * sn, x1 * sn + x2 * c], axis=-2)
    return out.reshape(b, s, h, d).astype(x.dtype)

def axial_gqa_attention(q, k, v, qn_g, kn_g, cos, sin):
    b, s = q.shape[:2]
    grp = ATTN_HEADS // ATTN_KV_HEADS
    q = apply_axial_rope(rms_norm(q, qn_g), cos, sin)
    k = apply_axial_rope(rms_norm(k, kn_g), cos, sin)
    n_blk = s // Q_BLOCK
    qb = jnp.moveaxis(q.reshape(b, n_blk, Q_BLOCK, ATTN_KV_HEADS, grp, HEAD_DIM), 1, 0)
    scale = HEAD_DIM ** -0.5

    def block(qi):
        sc = jnp.einsum('bqhgd,bkhd->bhgqk', qi, k, preferred_element_type=jnp.float32) * scale
        p = jax.nn.softmax(sc, axis=-1).astype(v.dtype)
        return jnp.einsum('bhgqk,bkhd->bqhgd', p, v)

    o = lax.map(block, qb)
    return jnp.moveaxis(o, 0, 1).reshape(b, s, ATTN_W)

def gla_direction(q, k, v, log_a):
    b, h, s, d = q.shape
    n_c = s // GLA_CHUNK
    to_chunks = lambda t: jnp.moveaxis(t.reshape(b, h, n_c, GLA_CHUNK, d), 2, 0)
    mask = jnp.tril(jnp.ones((GLA_CHUNK, GLA_CHUNK), dtype=bool))

    def step(state, inp):
        qc, kc, vc, gc = inp
        cum = jnp.cumsum(gc, axis=2)
        o_inter = jnp.einsum('bhtd,bhde->bhte', qc * jnp.exp(cum), state)
        diff = cum[:, :, :, None, :] - cum[:, :, None, :, :]
        decay = jnp.exp(jnp.where(mask[:, :, None], diff, -jnp.inf))
        att = jnp.einsum('bhtd,bhsd,bhtsd->bhts', qc, kc, decay)
        o_intra = jnp.einsum('bhts,bhse->bhte', att, vc)
        last = cum[:, :, -1:, :]
        new_state = (jnp.exp(last[:, :, 0, :])[..., None] * state
                     + jnp.einsum('bhsd,bhse->bhde', kc * jnp.exp(last - cum), vc))
        return new_state, o_inter + o_intra

    init = jnp.zeros((b, h, d, d), jnp.float32)
    _, o = lax.scan(step, init, (to_chunks(q), to_chunks(k), to_chunks(v), to_chunks(log_a)))
    return jnp.moveaxis(o, 0, 2).reshape(b, h, s, d)

def gla_mixer(q, k, v, g, a_lr, w2, a_b, norm_g):
    b, s, _ = q.shape
    f32 = jnp.float32
    heads = lambda t: t.astype(f32).reshape(b, s, GLA_HEADS, HEAD_DIM).transpose(0, 2, 1, 3)
    qh = heads(q) * HEAD_DIM ** -0.5
    kh = heads(k)
    vh = heads(v)
    a_lr = a_lr.astype(f32).reshape(b, s, 2, GLA_RANK)
    z = jnp.einsum('bsnr,nrk->nbsk', a_lr, w2.astype(f32)) + a_b.astype(f32)[:, None, None, :]
    log_a = jax.nn.log_sigmoid(z) / GLA_TAU
    flip = lambda t: t[:, :, ::-1]
    o_f = gla_direction(qh, kh, vh, heads(log_a[0]))
    o_b = flip(gla_direction(flip(qh), flip(kh), flip(vh), flip(heads(log_a[1]))))
    o = (o_f + o_b).transpose(0, 2, 1, 3)
    gate = jax.nn.silu(g.astype(f32).reshape(b, s, GLA_HEADS, HEAD_DIM))
    return (rms_norm(o, norm_g) * gate).reshape(b, s, GLA_W)

def mlstm_direction(q, k, v, i_pre, logf):
    b, h, s, d = q.shape
    L = MLSTM_CHUNK
    n_c = s // L
    chunk = lambda t: jnp.moveaxis(t.reshape(b, h, n_c, L, *t.shape[3:]), 2, 0)
    mask = jnp.tril(jnp.ones((L, L), dtype=bool))

    def step(carry, inp):
        c_st, n_st, m_st = carry
        qc, kc, vc, ic, fc = inp
        fcum = jnp.cumsum(fc, axis=-1)
        log_d = jnp.where(mask, fcum[..., :, None] - fcum[..., None, :] + ic[..., None, :], -jnp.inf)
        inter = fcum + m_st[..., None]
        m_t = jnp.maximum(inter, jnp.max(log_d, axis=-1))
        w_inter = jnp.exp(inter - m_t)
        qk = jnp.einsum('bhtd,bhsd->bhts', qc, kc) * jnp.exp(log_d - m_t[..., None])
        num = (w_inter[..., None] * jnp.einsum('bhed,bhtd->bhte', c_st, qc)
               + jnp.einsum('bhts,bhse->bhte', qk, vc))
        den = w_inter * jnp.einsum('bhd,bhtd->bht', n_st, qc) + jnp.sum(qk, axis=-1)
        hc = num / jnp.maximum(jnp.abs(den), jnp.exp(-m_t))[..., None]
        f_tot = fcum[..., -1]
        log_w = f_tot[..., None] - fcum + ic
        m_new = jnp.maximum(f_tot + m_st, jnp.max(log_w, axis=-1))
        decay = jnp.exp(f_tot + m_st - m_new)
        wk = kc * jnp.exp(log_w - m_new[..., None])[..., None]
        c_new = decay[..., None, None] * c_st + jnp.einsum('bhse,bhsd->bhed', vc, wk)
        n_new = decay[..., None] * n_st + jnp.sum(wk, axis=2)
        return (c_new, n_new, m_new), hc

    init = (jnp.zeros((b, h, d, d), jnp.float32), jnp.zeros((b, h, d), jnp.float32),
            jnp.zeros((b, h), jnp.float32))
    _, hs = lax.scan(step, init, (chunk(q), chunk(k), chunk(v), chunk(i_pre), chunk(logf)))
    return jnp.moveaxis(hs, 0, 2).reshape(b, h, s, d)

def mlstm_mixer(q, k, v, o_pre, gates, gate_b, norm_g):
    b, s, _ = q.shape
    f32 = jnp.float32
    heads = lambda t: t.astype(f32).reshape(b, s, MLSTM_HEADS, HEAD_DIM).transpose(0, 2, 1, 3)
    qh = heads(q)
    kh = heads(k) * HEAD_DIM ** -0.5
    vh = heads(v)
    gp = (gates.astype(f32).reshape(b, s, 4, MLSTM_HEADS) + gate_b.astype(f32)).transpose(2, 0, 3, 1)
    lf_f = jax.nn.log_sigmoid(gp[2])
    lf_b = jax.nn.log_sigmoid(gp[3])
    flip = lambda t: t[:, :, ::-1]
    h_f = mlstm_direction(qh, kh, vh, gp[0], lf_f)
    h_b = flip(mlstm_direction(flip(qh), flip(kh), flip(vh), flip(gp[1]), flip(lf_b)))
    h = jax.nn.sigmoid(heads(o_pre)) * (h_f + h_b)
    return rms_norm(h.transpose(0, 2, 1, 3), norm_g).reshape(b, s, MLSTM_W)

def centred_dwconv(u, w, bias):
    s = u.shape[1]
    pad = CONV_WIDTH // 2
    up = jnp.pad(u, ((0, 0), (pad, CONV_WIDTH - 1 - pad), (0, 0)))
    out = up[:, 0:s] * w[0]
    for j in range(1, CONV_WIDTH):
        out = out + up[:, j:j + s] * w[j]
    return out + bias

def encoder_layer(x, cos, sin, norm_mix_g, w_in, attn_qn_g, attn_kn_g, gla_gate_w2, gla_gate_b,
                  gla_norm_g, mlstm_gate_b, mlstm_norm_g, w_out, norm_ffn_g, w_up, conv_w, conv_b,
                  w_down):
    b, s, _ = x.shape
    h = rms_norm(x, norm_mix_g)
    proj = h @ w_in
    offsets = np.cumsum(IN_SPLITS)[:-1].tolist()
    aq, ak, av, bq, bk, bv, bg, ba, cq, ck, cv, co, cg = jnp.split(proj, offsets, axis=-1)
    attn = axial_gqa_attention(aq.reshape(b, s, ATTN_HEADS, HEAD_DIM),
                               ak.reshape(b, s, ATTN_KV_HEADS, HEAD_DIM),
                               av.reshape(b, s, ATTN_KV_HEADS, HEAD_DIM),
                               attn_qn_g, attn_kn_g, cos, sin)
    gla = gla_mixer(bq, bk, bv, bg, ba, gla_gate_w2, gla_gate_b, gla_norm_g)
    mls = mlstm_mixer(cq, ck, cv, co, cg, mlstm_gate_b, mlstm_norm_g)
    mixed = jnp.concatenate([attn.astype(x.dtype), gla.astype(x.dtype), mls.astype(x.dtype)], axis=-1)
    x = x + mixed @ w_out
    u = centred_dwconv(rms_norm(x, norm_ffn_g) @ w_up, conv_w, conv_b)
    gate, val = jnp.split(u, 2, axis=-1)
    return x + (jax.nn.silu(gate) * val) @ w_down

def setup_inputs(seed: int = 0) -> dict:
    key = jax.random.key(seed)
    ks = jax.random.split(key, 20)
    f32 = jnp.float32
    nrm = lambda k, shape, scale: scale * jax.random.normal(k, shape, f32)
    gain = lambda k, shape: 1.0 + 0.02 * jax.random.normal(k, shape, f32)
    f_bias = jnp.linspace(3.0, 6.0, MLSTM_HEADS, dtype=f32)
    mlstm_gate_b = jnp.concatenate([nrm(ks[9], (DEPTH, 2, MLSTM_HEADS), 0.1),
                                    f_bias + nrm(ks[10], (DEPTH, 2, MLSTM_HEADS), 0.1)], axis=1)
    return {
        'x_prompt': jax.random.normal(ks[0], (BATCH, SEQ, D_MODEL), f32),
        'x_sample': jax.random.normal(ks[1], (DEC_BATCH, DEC_SEQ, D_MODEL), f32),
        'norm_mix_g': gain(ks[2], (DEPTH, D_MODEL)),
        'w_in': nrm(ks[3], (DEPTH, D_MODEL, IN_DIM), D_MODEL ** -0.5),
        'attn_qn_g': gain(ks[4], (DEPTH, HEAD_DIM)),
        'attn_kn_g': gain(ks[5], (DEPTH, HEAD_DIM)),
        'gla_gate_w2': nrm(ks[6], (DEPTH, 2, GLA_RANK, GLA_W), GLA_RANK ** -0.5),
        'gla_gate_b': nrm(ks[7], (DEPTH, 2, GLA_W), 0.1),
        'gla_norm_g': gain(ks[8], (DEPTH, HEAD_DIM)),
        'mlstm_gate_b': mlstm_gate_b,
        'mlstm_norm_g': gain(ks[11], (DEPTH, HEAD_DIM)),
        'w_out': nrm(ks[12], (DEPTH, MIX_W, D_MODEL), MIX_W ** -0.5),
        'norm_ffn_g': gain(ks[13], (DEPTH, D_MODEL)),
        'w_up': nrm(ks[14], (DEPTH, D_MODEL, 2 * D_FF), D_MODEL ** -0.5),
        'conv_w': nrm(ks[15], (DEPTH, CONV_WIDTH, 2 * D_FF), CONV_WIDTH ** -0.5),
        'conv_b': nrm(ks[16], (DEPTH, 2 * D_FF), 0.02),
        'w_down': nrm(ks[17], (DEPTH, D_FF, D_MODEL), D_FF ** -0.5),
    }

def reference(x_prompt, x_sample, norm_mix_g, w_in, attn_qn_g, attn_kn_g, gla_gate_w2, gla_gate_b,
              gla_norm_g, mlstm_gate_b, mlstm_norm_g, w_out, norm_ffn_g, w_up, conv_w, conv_b,
              w_down):
    def run(x):
        cos, sin = axial_rope_tables(x.shape[1])
        for l in range(DEPTH):
            x = encoder_layer(x, cos, sin, norm_mix_g[l], w_in[l], attn_qn_g[l], attn_kn_g[l],
                              gla_gate_w2[l], gla_gate_b[l], gla_norm_g[l], mlstm_gate_b[l],
                              mlstm_norm_g[l], w_out[l], norm_ffn_g[l], w_up[l], conv_w[l],
                              conv_b[l], w_down[l])
        return x

    y_prompt = run(x_prompt)
    y_sample = run(x_sample)
    return (y_prompt, y_sample)


_drawn_inputs = setup_inputs


def setup_inputs(seed=0):
    import zlib

    import numpy as np

    out = dict(_drawn_inputs(seed))
    spreads = {}
    factors = {'attn_qn_g': 8.0,
     'attn_kn_g': 8.0,
     'gla_gate_b': 2.803,
     'gla_norm_g': 5.219,
     'mlstm_norm_g': 3.19,
     'norm_ffn_g': 2.768,
     'conv_b': 2.809}
    for name, (base, spread) in spreads.items():
        noise = np.random.default_rng([zlib.crc32(name.encode()), seed]).standard_normal(out[name].shape)
        drawn = base * np.exp(spread * noise) if base else spread * noise
        out[name] = jnp.asarray(drawn.astype(out[name].dtype))
    for name, factor in factors.items():
        out[name] = (out[name] * factor).astype(out[name].dtype)
    return out
```

```python
from contextlib import ExitStack

import numpy as np

import concourse.bass as bass
from concourse import mybir
from concourse.alu_op_type import AluOpType as ALU

F32 = mybir.dt.float32
F32R = mybir.dt.float32r
U32 = mybir.dt.uint32
ACT = mybir.ActivationFunctionType
AX_X = mybir.AxisListType.X

P = 128
DEPTH = 2
D = 1024
SEQ = 512
NSEQ = 2
T = NSEQ * SEQ
KT = D // P
TT = T // P
SB = SEQ // P
HD = 64
EPS = 1e-6
GRID_W = 64
ROPE_THETA = 10000.0
AH, KVH = 8, 2
NQK = AH + KVH
GH = MH = 4
GLA_TAU = 16.0
DFF = 2816
FT = DFF // P
CH = 32
NCH = SEQ // CH
UNIT = KT * P

AQ, AK, AV = 0, 512, 640
BQ, BK, BV, BG, BA = 768, 1024, 1280, 1536, 1792
CQ, CK, CV, CO, CG = 1824, 2080, 2336, 2592, 2848

TOK_COLS = [AQ, AQ + 256, AK, BV, BG, CV, CO]
FEAT_COLS = [CQ, CQ + 128, CK, CK + 128, BQ, BQ + 128, BK, BK + 128]
N_TOK = 2 * len(TOK_COLS)
N_IN = N_TOK + len(FEAT_COLS) + 1
N_OUT = KT
N_UNITS = N_IN + N_OUT
RAW, SPLIT = 3, 4
E_TOK = len(TOK_COLS) * TT
E_ALL = E_TOK + 2 * (N_IN - N_TOK)

BA_ROW = (4, 36)
GROWS = 36

V_MIX, V_FFN, V_GLAN, V_MLN, V_GB, V_GBI, V_GBF = 0, 8, 16, 17, 18, 22, 23
NVEC = 24


def build(nc, x_in, w_units, w_ffn, vecs, w2p, qkg, convp, rope, gmask, chunkmask, lmask, sel,
          ident_in, x_out):
    ctx = ExitStack()
    with ctx:
        def fixed(name, shape, dt=F32):
            return ctx.enter_context(nc.sbuf_tensor(name, shape, dt))

        def region(size, specs):
            assert sum(int(np.prod(shape[1:])) * 4 + 31 & ~31 for _, shape, _ in specs) <= size, specs[0][0]
            with ExitStack() as phase:
                return [phase.enter_context(nc.sbuf_tensor(n, s, d)) for n, s, d in specs]

        W_BYTES = 2 * SPLIT * UNIT * 4
        H_BYTES = 2 * KT * T * 4
        Q_BYTES = 4 * (2 * 4 * T + TT * (768 + 3 * 256 + MH * (HD + 1)) + T)
        ident = fixed("ident", [P, P])
        ones = fixed("ones", [P, P])
        eps = fixed("eps", [P, 1])
        vec = fixed("vec", [P, NVEC])
        raw = fixed("raw", [P, RAW, UNIT])

        with ExitStack() as w_region:
            whi = w_region.enter_context(nc.sbuf_tensor("whi", [P, SPLIT, KT, P], F32R))
            wlo = w_region.enter_context(nc.sbuf_tensor("wlo", [P, SPLIT, KT, P], F32R))
        st, oacc, ktok = region(W_BYTES, [
            ("states", [P, NCH, NSEQ, 2, HD], F32), ("oacc", [P, TT, 256], F32), ("ktok", [P, TT, 256], F32)])
        w_hold = ctx.enter_context(nc.sbuf_tensor("w_region", [P, W_BYTES // 4], F32))

        hh, hl = region(H_BYTES, [("hh", [P, KT, T], F32R), ("hl", [P, KT, T], F32R)])
        (ropec, ropes, tabc, tabs, t1, t2, kdup, qkgain, ssq, rqk, qT, kT, prob, pT, nmx, rsum,
         rinvp) = region(H_BYTES, [
            ("ropec", [P, SB, HD], F32), ("ropes", [P, SB, HD], F32),
            ("tabc", [P, SB, NQK, HD], F32), ("tabs", [P, SB, NQK, HD], F32),
            ("t1", [P, NQK * HD], F32), ("t2", [P, NQK * HD], F32),
            ("kdup", [P, 2, KVH, 2, HD], F32), ("qkgain", [P, 2, HD], F32),
            ("ssq", [P, TT, NQK], F32), ("rqk", [P, TT, NQK], F32),
            ("qT", [P, AH // 2, T], F32), ("kT", [P, KVH, T], F32),
            ("prob", [P, 2, SEQ], F32), ("pT", [P, 2, SB, P], F32),
            ("nmx", [P, 64], F32), ("rsum", [P, 64], F32), ("rinvp", [P, 64], F32)])
        (G, gx, dml, qhat, khat, qtil, ktil, attT, gam, cmask, aL, w2s, gss,
         gtmp) = region(H_BYTES, [
            ("G", [P, 2, T], F32), ("gx", [P, 2, T], F32), ("dml", [P, T], F32),
            ("qhat", [P, 2, T], F32), ("khat", [P, 2, T], F32), ("qtil", [P, 2, T], F32),
            ("ktil", [P, T], F32), ("attT", [P, 2, 2, 2, P], F32),
            ("gam", [P, 2, P], U32), ("cmask", [P, SEQ], F32), ("aL", [P, 2, NSEQ * NCH], F32),
            ("w2s", [P, 2, 256], F32), ("gss", [P, 2, TT * GH], F32), ("gtmp", [P, 256], F32)])
        ee = ktil[:].rearrange("p (a t) -> p a t", a=2)
        (yf, ri, fl, Fc, mm_rows, Rr, Cr, zr, sels, mmask, CT, EM, mR, Dt, rc, dn, t12, hs,
         mss) = region(H_BYTES, [
            ("yf", [GROWS, T], F32), ("ri", [GROWS, T], F32), 
            ("fl", [GROWS, T], F32), ("Fc", [GROWS, T], F32), ("mm_rows", [GROWS, T], F32),
            ("Rr", [GROWS, T], F32), ("Cr", [GROWS, T], F32), ("zr", [GROWS, SEQ], F32),
            ("sels", [GROWS, 2 * MH, P], F32), ("mmask", [P, 2, P], F32),
            ("CT", [P, TT, GROWS], F32), ("EM", [P, TT, GROWS], F32),
            ("mR", [P, 2, SEQ], F32), ("Dt", [P, 2, SB, SEQ], F32),
            ("rc", [P, 2, SB], F32), ("dn", [P, 2, SB], F32), ("t12", [P, 2, SB, HD], F32),
            ("hs", [P, SB, HD], F32), ("mss", [P, 2, TT * MH], F32)])
        h_hold = ctx.enter_context(nc.sbuf_tensor("h_region", [P, H_BYTES // 4], F32))

        (qkM, qkG, tokA, gv, gg, vaug, co, small) = region(Q_BYTES, [
            ("qkM", [P, 4, T], F32), ("qkG", [P, 4, T], F32), ("tokA", [P, TT, 768], F32),
            ("gv", [P, TT, 256], F32), ("gg", [P, TT, 256], F32),
            ("vaug", [P, TT, MH, HD + 1], F32), ("co", [P, TT, 256], F32),
            ("small", [P, T], F32)])
        (x, sq, hf, rms, rinv, accg, accv, sil, acth, actl, convs, cw) = region(Q_BYTES, [
            ("x", [P, KT, T], F32), ("sq", [P, 4, SEQ], F32), ("hf", [P, 2, SEQ], F32),
            ("rms", [P, NSEQ, SEQ], F32), ("rinv", [P, NSEQ, SEQ], F32),
            ("accg", [P, NSEQ, SEQ], F32), ("accv", [P, NSEQ, SEQ], F32),
            ("sil", [P, NSEQ, SEQ], F32), ("acth", [P, NSEQ, SEQ], F32R),
            ("actl", [P, NSEQ, SEQ], F32R), ("convs", [P, FT, 8], F32), ("cw", [P, 8], F32)])
        q_hold = ctx.enter_context(nc.sbuf_tensor("q_region", [P, Q_BYTES // 4], F32))

        ps = ctx.enter_context(nc.psum_tensor("ps", [P, 8, 512], F32))
        x_spill = nc.dram_tensor("x_spill", [P, KT * T], F32, kind="Internal").ap()

        def sem(name):
            return ctx.enter_context(nc.semaphore(name))

        per_layer = []

        def lsem(name):
            s = sem(name)
            per_layer.append(s)
            return s

        x_loaded, consts_loaded, ones_set = sem("x_loaded"), sem("consts_loaded"), sem("ones_set")
        layer_end, layer_go, out_done = lsem("layer_end"), sem("layer_go"), sem("out_done")
        vec_loaded, spilled, reloaded = lsem("vec_loaded"), lsem("spilled"), lsem("reloaded")
        act_chain, dve_chain = lsem("act_chain"), lsem("dve_chain")
        sq_ready, sq_used = lsem("sq_ready"), lsem("sq_used")
        rms_ready, hf_ready = lsem("rms_ready"), lsem("hf_ready")
        hh_ready, h_ready = lsem("hh_ready"), lsem("h_ready")
        raw_full = [lsem(f"raw_full{i}") for i in range(RAW)]
        hi_ready, lo_ready, unit_used = lsem("hi_ready"), lsem("lo_ready"), lsem("unit_used")
        proj_ready, act_evac, dve_evac = lsem("proj_ready"), lsem("act_evac"), lsem("dve_evac")
        att_consts, tab_done = lsem("att_consts"), lsem("tab_done")
        qk_sums, qk_rms, rot_ready = lsem("qk_sums"), lsem("qk_rms"), lsem("rot_ready")
        qkT_psum, qkT_ready = lsem("qkT_psum"), lsem("qkT_ready")
        sc_ready, nmx_ready, prob_ready = lsem("sc_ready"), lsem("nmx_ready"), lsem("prob_ready")
        pT_psum, pT_ready = lsem("pT_psum"), lsem("pT_ready")
        ao_psum, ao_done = lsem("ao_psum"), lsem("ao_done")
        gla_consts, z_psum, ln_ready = lsem("gla_consts"), lsem("z_psum"), lsem("ln_ready")
        la_ready, cum_ready, dml_ready = lsem("la_ready"), lsem("cum_ready"), lsem("dml_ready")
        gx_ready, gx_used = lsem("gx_ready"), lsem("gx_used")
        ktil_psum, ktok_ready, aL_ready = lsem("ktil_psum"), lsem("ktok_ready"), lsem("aL_ready")
        kv_psum, state_ready = lsem("kv_psum"), lsem("state_ready")
        gat_psum, gat_ready = lsem("gat_psum"), lsem("gat_ready")
        go_psum, go_evac = lsem("go_psum"), lsem("go_evac")
        gsq_ready, gss_ready, grms_ready = lsem("gsq_ready"), lsem("gss_ready"), lsem("grms_ready")
        gsig_ready, gla_done = lsem("gsig_ready"), lsem("gla_done")
        ml_consts, yf_ready, fl_ready = lsem("ml_consts"), lsem("yf_ready"), lsem("fl_ready")
        rc_ready, ct_psum, ct_ready = lsem("rc_ready"), lsem("ct_psum"), lsem("ct_ready")
        qk_psum, rb_psum, mr_ready = lsem("qk_psum"), lsem("rb_psum"), lsem("mr_ready")
        dt_ready, wt_ready, num_psum = lsem("dt_ready"), lsem("wt_ready"), lsem("num_psum")
        heads_gated, ml_evac = lsem("heads_gated"), lsem("ml_evac")
        msq_ready, mss_ready, mrms_ready = lsem("msq_ready"), lsem("mss_ready"), lsem("mrms_ready")
        msig_ready, ml_done = lsem("msig_ready"), lsem("ml_done")
        mix_psum, mixh_ready, mixl_ready = lsem("mix_psum"), lsem("mixh_ready"), lsem("mixl_ready")
        wo_psum, wo_done = lsem("wo_psum"), lsem("wo_done")
        f_full = [lsem(f"f_full_{k}") for k in "gvd"]
        f_hi = [lsem(f"f_hi_{k}") for k in "gvd"]
        f_lo = [lsem(f"f_lo_{k}") for k in "gvd"]
        f_used = [lsem(f"f_used_{k}") for k in "gvd"]
        conv_loaded, cw_ready = lsem("conv_loaded"), lsem("cw_ready")
        g_init, v_init = lsem("g_init"), lsem("v_init")
        g_half, v_half = lsem("g_half"), lsem("v_half")
        g_conv, v_conv = lsem("g_conv"), lsem("v_conv")
        sil_ready, act_ready = lsem("sil_ready"), lsem("act_ready")
        acth_ready, actl_ready = lsem("acth_ready"), lsem("actl_ready")
        d_psum, d_done = lsem("d_psum"), lsem("d_done")

        def evac_target(e):
            if e < E_TOK:
                c, tt = divmod(e, TT)
                col = TOK_COLS[c]
                if col < BQ:
                    return tokA[:, tt, col:col + 256], 256
                if col == CV:
                    return vaug[:, tt, :, 0:HD], 256
                return {BV: gv, BG: gg, CO: co}[col][:, tt, :], 256
            f, s = divmod(e - E_TOK, NSEQ)
            cols = slice(s * SEQ, (s + 1) * SEQ)
            if f < 4:
                return qkM[:, f, cols], SEQ
            if f < 8:
                return qkG[:, f - 4, cols], SEQ
            return small[:, cols], SEQ

        def evac_source(e):
            dst, n = evac_target(e)
            src = ps[:, e % 8, 0:n]
            if e < E_TOK and TOK_COLS[e // TT] == CV:
                src = src.rearrange("p (h d) -> p h d", h=MH)
            return dst, src

        def fwd_or_bwd_range(d, i):
            return (i * P, SEQ) if d == 0 else (0, (i + 1) * P)

        def step_of(d, ci):
            return ci if d == 0 else NCH - 1 - ci

        block = ctx.enter_context(nc.Block())

        @block.sync
        def _(sp):
            for k in range(KT):
                sp.dma_start(x[:, k, :], x_in[:, k, :]).then_inc(x_loaded, 16)
            sp.dma_start(ident[:], ident_in).then_inc(consts_loaded, 16)
            sp.wait_ge(x_loaded, 16 * KT)
            with sp.Fori(0, DEPTH) as l:
                sp.dma_start(vec[:], vecs[l]).then_inc(vec_loaded, 16)

                def load_unit(n):
                    if n >= RAW:
                        sp.wait_ge(lo_ready, n - RAW + 1)
                    sp.dma_start(raw[:, n % RAW, :], w_units[l, n]).then_inc(raw_full[n % RAW], 16)

                load_unit(0)
                load_unit(1)
                sp.dma_start(x_spill, x[:].rearrange("p k t -> p (k t)")).then_inc(spilled, 16)
                for n in range(2, N_IN + RAW):
                    load_unit(n)
                sp.wait_ge(proj_ready, E_ALL)
                sp.dma_start(ropec[:], rope[0]).then_inc(att_consts, 16)
                sp.dma_start(ropes[:], rope[1]).then_inc(att_consts, 16)
                sp.dma_start(qkgain[:], qkg[l]).then_inc(att_consts, 16)
                sp.wait_ge(ao_done, 64)
                sp.dma_start(gam[:], gmask).then_inc(gla_consts, 16)
                sp.dma_start(cmask[:], chunkmask).then_inc(gla_consts, 16)
                sp.dma_start(w2s[:], w2p[l]).then_inc(gla_consts, 16)
                sp.wait_ge(gla_done, 1)
                sp.dma_start(sels[:], sel).then_inc(ml_consts, 16)
                sp.dma_start(mmask[:], lmask).then_inc(ml_consts, 16)
                sp.wait_ge(ml_done, 1)
                sp.wait_ge(spilled, 16)
                sp.dma_start(x[:].rearrange("p k t -> p (k t)"), x_spill).then_inc(reloaded, 16)
                for n in range(N_IN + RAW, N_UNITS):
                    load_unit(n)

                sp.wait_ge(mix_psum, 2 * TT)
                sp.dma_start(convs[:], convp[l]).then_inc(conv_loaded, 16)

                def load_ffn(j):
                    for kind in range(3):
                        if isinstance(j, int) and j == 0:
                            sp.wait_ge(lo_ready, N_UNITS)
                        else:
                            sp.wait_ge(f_lo[kind], j)
                        sp.dma_start(raw[:, kind, :], w_ffn[l, j, kind]).then_inc(f_full[kind], 16)

                load_ffn(0)
                with sp.Fori(1, FT) as j:
                    load_ffn(j)
                sp.wait_ge(d_done, FT * KT)
                sp.wait_ge(layer_end, 3)
                for s in per_layer:
                    sp.sem_clear(s)
                sp.sem_inc(layer_go, 1)
            sp.dma_start(x_out, x[:]).then_inc(out_done, 16)
            sp.wait_ge(out_done, 16)

        @block.tensor
        def _(pe):
            pe.wait_ge(consts_loaded, 16)
            pe.wait_ge(ones_set, 2)
            with pe.Fori(0, DEPTH) as l:
                def norm_sums(n):
                    for s in range(NSEQ):
                        for k in range(KT):
                            i = (n * NSEQ + s) * KT + k
                            pe.wait_ge(sq_ready, i + 1)
                            pe.matmul(ps[:, s, :], ones[:], sq[:, i % 4, :], start=(k == 0),
                                      stop=(k == KT - 1)).then_inc(sq_used, 1)

                def passes3(out, stat, mov, first, last):
                    pe.matmul(out, stat[1], mov[0], start=first, stop=False)
                    pe.matmul(out, stat[0], mov[1], start=False, stop=False)
                    return pe.matmul(out, stat[0], mov[0], start=False, stop=last)

                norm_sums(0)

                def bank_free(e):
                    if e >= 8:
                        pe.wait_ge((act_evac, dve_evac)[e % 2], e // 2 - 3)

                for c in range(len(TOK_COLS)):
                    pe.wait_ge(lo_ready, 2 * c + 2)
                    slot = 2 * c % SPLIT
                    for tt in range(TT):
                        e = c * TT + tt
                        bank_free(e)
                        if c == 0 and tt == 0:
                            pe.wait_ge(rms_ready, 2)
                        for k in range(KT):
                            if c == 0 and tt % SB == 0:
                                pe.wait_ge(h_ready, tt // SB * KT + k + 1)
                            tok = slice(tt * P, (tt + 1) * P)
                            mm3 = passes3(ps[:, e % 8, 0:256], (hh[:, k, tok], hl[:, k, tok]),
                                          (whi[:, slot:slot + 2, k, :], wlo[:, slot:slot + 2, k, :]),
                                          k == 0, k == KT - 1)
                        mm3.then_inc(proj_ready, 1)
                        if tt == TT - 1:
                            pe.wait_ge(proj_ready, e + 1)
                            pe.sem_inc(unit_used, 2)

                for u in range(N_TOK, N_IN):
                    pe.wait_ge(lo_ready, u + 1)
                    for s in range(NSEQ):
                        e = E_TOK + 2 * (u - N_TOK) + s
                        bank_free(e)
                        tok = slice(s * SEQ, (s + 1) * SEQ)
                        for k in range(KT):
                            mm3 = passes3(ps[:, e % 8, :], (whi[:, u % SPLIT, k, :], wlo[:, u % SPLIT, k, :]),
                                          (hh[:, k, tok], hl[:, k, tok]), k == 0, k == KT - 1)
                        mm3.then_inc(proj_ready, 1)
                    pe.wait_ge(proj_ready, e + 1)
                    pe.sem_inc(unit_used, 1)

                pe.wait_ge(act_evac, E_ALL // 2)
                pe.wait_ge(dve_evac, E_ALL // 2)
                for tt in range(TT):
                    bank = tt % 2 * 2
                    pe.wait_ge(rot_ready, tt + 1)
                    if tt >= 2:
                        pe.wait_ge(qkT_ready, 2 * (tt - 2) + 2)
                    for b in range(AH // 2):
                        tr = pe.transpose(ps[:, bank, b * P:(b + 1) * P],
                                          tokA[:, tt, b * P:(b + 1) * P], ident[:])
                    tr.then_inc(qkT_psum, 1)
                    for g in range(KVH):
                        tr = pe.transpose(ps[:, bank + 1, g * P:(g + 1) * P],
                                          kdup[:, tt % 2, g, :, :].rearrange("p r d -> p (r d)"), ident[:])
                    tr.then_inc(qkT_psum, 1)
                n_att = NSEQ * AH * SB
                for i in range(n_att + 2):
                    if i < n_att:
                        s, h, qt = i // (AH * SB), i // SB % AH, i % SB
                        rows = slice(h % 2 * HD, (h % 2 + 1) * HD)
                        if i == 0:
                            pe.wait_ge(qkT_ready, 2 * TT)
                        if i >= 2:
                            pe.wait_ge(prob_ready, i - 1)
                        q0 = s * SEQ + qt * P
                        pe.matmul(ps[:, 4 + i % 2, :], qT[rows, h // 2, q0:q0 + P],
                                  kT[rows, h // 4, s * SEQ:(s + 1) * SEQ], start=True,
                                  stop=True).then_inc(sc_ready, 1)
                    if 1 <= i <= n_att:
                        v = i - 1
                        pe.wait_ge(prob_ready, v + 1)
                        if v >= 2:
                            pe.wait_ge(pT_ready, v - 1)
                        for kt in range(SB):
                            tr = pe.transpose(ps[:, 6 + v % 2, kt * P:(kt + 1) * P],
                                              prob[:, v % 2, kt * P:(kt + 1) * P], ident[:])
                        tr.then_inc(pT_psum, 1)
                    if i >= 2:
                        v = i - 2
                        s, h = v // (AH * SB), v // SB % AH
                        pe.wait_ge(pT_ready, v + 1)
                        if v >= 2:
                            pe.wait_ge(ao_done, v - 1)
                        c0 = AV + h // 4 * HD
                        for kt in range(SB):
                            mm = pe.matmul(ps[:, v % 2, 0:HD], pT[:, v % 2, kt, :],
                                           tokA[:, s * SB + kt, c0:c0 + HD], start=(kt == 0), stop=(kt == SB - 1))
                        mm.then_inc(ao_psum, 1)

                pe.wait_ge(ao_done, n_att)
                pe.wait_ge(gla_consts, 48)
                for d in range(2):
                    if d == 1:
                        pe.wait_ge(go_evac, TT)
                    for j in range(4):
                        pe.matmul(ps[:, j, :], w2s[:, d, j // 2 * P:(j // 2 + 1) * P],
                                  small[:, j % 2 * SEQ:(j % 2 + 1) * SEQ], start=True,
                                  stop=True).then_inc(z_psum, 1)
                    for ht in range(2):
                        pe.wait_ge(gx_used, (d * 2 + ht) * 4 + 4)
                        for b in range(2):
                            r = (d * 2 + ht) * 2 + b
                            if r >= 2:
                                pe.wait_ge(ktok_ready, r - 1)
                            for i in range(4):
                                tt = b * 4 + i
                                tr = pe.transpose(ps[:, 4 + b, i * P:(i + 1) * P],
                                                  ktil[:, tt * P:(tt + 1) * P], ident[:])
                            tr.then_inc(ktil_psum, 1)
                    pe.wait_ge(ktok_ready, d * 4 + 4)
                    for c in range(NCH - 1):
                        ci = step_of(d, c)
                        n = d * (NCH - 1) + c
                        if n >= 2:
                            pe.wait_ge(state_ready, n - 1)
                        rows = slice(ci % 4 * CH, (ci % 4 + 1) * CH)
                        for s in range(NSEQ):
                            tt = s * SB + ci // 4
                            for h in range(GH):
                                half = slice(h % 2 * HD, (h % 2 + 1) * HD)
                                c0 = (s * 2 + h // 2) * HD
                                mm = pe.matmul(ps[half, 6 + n % 2, c0:c0 + HD],
                                               ktok[rows, tt, h * HD:(h + 1) * HD],
                                               gv[rows, tt, h * HD:(h + 1) * HD], start=True, stop=True)
                        mm.then_inc(kv_psum, 1)

                    def scores(tt):
                        n = d * TT + tt
                        if tt >= 2:
                            pe.wait_ge(gat_ready, n - 1)
                        tok = slice(tt * P, (tt + 1) * P)
                        for h in range(GH):
                            half = slice(h % 2 * HD, (h % 2 + 1) * HD)
                            mm = pe.matmul(ps[:, tt % 2 * 4 + h % 2, h // 2 * P:(h // 2 + 1) * P], khat[half, h // 2, tok],
                                           qhat[half, h // 2, tok], start=True, stop=True)
                        mm.then_inc(gat_psum, 1)

                    scores(0)
                    pe.wait_ge(state_ready, (d + 1) * (NCH - 1))
                    for tt in range(TT):
                        if tt + 1 < TT:
                            scores(tt + 1)
                        n = d * TT + tt
                        pe.wait_ge(gat_ready, n + 1)
                        if tt >= 2:
                            pe.wait_ge(go_evac, n - 1)
                        s = tt // SB
                        for h in range(GH):
                            half = slice(h % 2 * HD, (h % 2 + 1) * HD)
                            bank, cols = 2 + tt % 2 * 4 + h % 2, slice(h // 2 * HD, (h // 2 + 1) * HD)
                            mm = pe.matmul(ps[:, bank, cols], attT[:, tt % 2, h % 2, h // 2, :],
                                           gv[:, tt, h * HD:(h + 1) * HD],
                                           start=True, stop=False, skip_group_check=True)
                            for r in range(4):
                                c = step_of(d, tt % SB * 4 + r)
                                t0 = tt * P + r * CH
                                mm = pe.matmul(ps[r * CH:(r + 1) * CH, bank, cols],
                                               qtil[half, h // 2, t0:t0 + CH], st[half, c, s, h // 2, :],
                                               start=False, stop=True, skip_group_check=True)
                        mm.then_inc(go_psum, 1)

                pe.wait_ge(gla_done, 1)
                pe.wait_ge(ml_consts, 32)
                pe.wait_ge(rc_ready, 1)
                for i, src in enumerate((Cr, mm_rows)):
                    for tt in range(TT):
                        tr = pe.transpose(ps[:, i, tt * GROWS:(tt + 1) * GROWS],
                                          src[:, tt * P:(tt + 1) * P], ident[0:GROWS, 0:GROWS])
                    tr.then_inc(ct_psum, 1)
                pe.wait_ge(ct_ready, 2)
                for w in range(NSEQ * MH):
                    s, h = w // MH, w % MH
                    tok = slice(s * SEQ, (s + 1) * SEQ)
                    rows = slice(h % 2 * HD, (h % 2 + 1) * HD)
                    for d in range(2):
                        if w >= 1:
                            pe.wait_ge(dt_ready, 2 * SB * w)
                        pe.matmul(ps[:, 4 + d, :], sels[:, d * MH + h, :], Rr[:, tok], start=True,
                                  stop=True).then_inc(rb_psum, 1)
                    if w >= 1:
                        pe.wait_ge(wt_ready, 2 * SB * w)
                    for i in range(SB):
                        k0 = s * SEQ + i * P
                        pe.matmul(ps[:, i, :], qkM[rows, 2 + h // 2, k0:k0 + P], qkM[rows, h // 2, tok],
                                  start=True, stop=True).then_inc(qk_psum, 1)
                    if w >= 1:
                        pe.wait_ge(ml_evac, w)
                    pe.wait_ge(wt_ready, 2 * SB * (w + 1))
                    for d in range(2):
                        for j in range(SB):
                            keys = range(j + 1) if d == 0 else range(j, SB)
                            for i in keys:
                                mm = pe.matmul(ps[:, 6 + d, j * (HD + 1):(j + 1) * (HD + 1)],
                                               Dt[:, d, i, j * P:(j + 1) * P], vaug[:, s * SB + i, h, :],
                                               start=(i == keys[0]), stop=(i == keys[-1]))
                    mm.then_inc(num_psum, 1)

                pe.wait_ge(ml_done, 1)
                for tt in range(TT):
                    for b in range(2):
                        if tt >= 4:
                            pe.wait_ge(mixl_ready, 3 * (tt - 4) + 1 + 2 * b)
                        for i in range(4):
                            src = (tokA[:, tt, i * P:(i + 1) * P] if b == 0 else
                                   (gg, co)[i // 2][:, tt, i % 2 * P:(i % 2 + 1) * P])
                            tr = pe.transpose(ps[:, tt % 4 * 2 + b, i * P:(i + 1) * P], src, ident[:])
                        tr.then_inc(mix_psum, 1)
                pe.wait_ge(mixl_ready, 3 * TT)
                for o in range(KT):
                    u = N_IN + o
                    pe.wait_ge(lo_ready, u + 1)
                    if o >= 4:
                        pe.wait_ge(wo_done, o - 3)
                    for s in range(NSEQ):
                        tok = slice(s * SEQ, (s + 1) * SEQ)
                        for k in range(KT):
                            mm3 = passes3(ps[:, o % 4 * 2 + s, :], (whi[:, u % SPLIT, k, :], wlo[:, u % SPLIT, k, :]),
                                          (hh[:, k, tok], hl[:, k, tok]), k == 0, k == KT - 1)
                    mm3.then_inc(wo_psum, 1)
                    pe.wait_ge(wo_psum, o + 1)
                    pe.sem_inc(unit_used, 1)

                pe.wait_ge(wo_done, KT)
                norm_sums(1)
                pe.wait_ge(h_ready, 4 * KT)

                def up(kind, j):
                    pe.wait_ge(f_lo[kind], j + 1)
                    for s in range(NSEQ):
                        for k in range(KT):
                            mm3 = passes3(ps[:, 2 * kind + s, :], (whi[:, kind, k, :], wlo[:, kind, k, :]),
                                          (hh[:, k, s * SEQ:(s + 1) * SEQ], hl[:, k, s * SEQ:(s + 1) * SEQ]),
                                          k == 0, k == KT - 1)
                    mm3.then_inc(f_used[kind], 1)

                def down(j, first=False, last=False):
                    pe.wait_ge(f_lo[2], j + 1)
                    pe.wait_ge(actl_ready, j + 1)
                    for o in range(KT):
                        if not (first and o < 2):
                            pe.wait_ge(d_done, j * KT + o - 1)
                        for s in range(NSEQ):
                            mm3 = passes3(ps[:, 4 + o % 2 * 2 + s, :], (whi[:, 2, o, :], wlo[:, 2, o, :]),
                                          (acth[:, s, :], actl[:, s, :]), True, True)
                        mm3.then_inc(d_psum, 1)
                    pe.wait_ge(d_psum, (j + 1) * KT)
                    pe.sem_inc(f_used[2], 1)

                up(0, 0)
                up(1, 0)

                def iteration(j, first=False):
                    pe.wait_ge(g_conv, j)
                    up(0, j)
                    pe.wait_ge(v_conv, j)
                    up(1, j)
                    down(j - 1, first=first)

                iteration(1, first=True)
                with pe.Fori(2, FT) as j:
                    iteration(j)
                down(FT - 1)
                pe.sem_inc(layer_end, 1)
                pe.wait_ge(layer_go, l + 1)

        @block.scalar
        def _(act):
            act.wait_ge(x_loaded, 16 * KT)
            act.wait_ge(ones_set, 2)
            with act.Fori(0, DEPTH) as l:
                chain = [0]

                def link(ins):
                    chain[0] += 1
                    ins.then_inc(act_chain, 1)
                    act.wait_ge(act_chain, chain[0])

                def split_hi(n):
                    act.wait_ge(raw_full[n % RAW], 16 * (n // RAW + 1))
                    if n >= SPLIT:
                        act.wait_ge(unit_used, n - SPLIT + 1)
                    act.activation(whi[:, n % SPLIT, :, :], raw[:, n % RAW, :].rearrange("p (k c) -> p k c", k=KT),
                                   ACT.Copy).then_inc(hi_ready, 1)

                def norm(n):
                    for s in range(NSEQ):
                        tok = slice(s * SEQ, (s + 1) * SEQ)
                        for k in range(KT):
                            i = (n * NSEQ + s) * KT + k
                            if i >= 4:
                                act.wait_ge(sq_used, i - 3)
                            act.activation(sq[:, i % 4, :], x[:, k, tok], ACT.Square).then_inc(sq_ready, 1)
                    for s in range(NSEQ):
                        act.wait_ge(sq_used, (n * NSEQ + s + 1) * KT)
                        act.activation(rms[:, s, :], ps[:, s, :], ACT.Sqrt, bias=eps[:], scale=1.0 / D)\
                           .then_inc(rms_ready, 1)
                    for s in range(NSEQ):
                        for k in range(KT):
                            i = (n * NSEQ + s) * KT + k
                            act.wait_ge(hf_ready, i + 1)
                            act.activation(hh[:, k, s * SEQ:(s + 1) * SEQ], hf[:, i % 2, :], ACT.Copy)\
                               .then_inc(hh_ready, 1)

                split_hi(0)
                split_hi(1)
                norm(0)
                split_hi(2)
                split_hi(3)
                act.wait_ge(h_ready, NSEQ * KT)

                def evacuate(e):
                    if e == E_TOK:
                        act.wait_ge(spilled, 16)
                    act.wait_ge(proj_ready, e + 1)
                    dst, src = evac_source(e)
                    act.activation(dst, src, ACT.Copy).then_inc(act_evac, 1)

                for c in range(len(TOK_COLS)):
                    if c >= 1:
                        for u in (2 * c + 2, 2 * c + 3):
                            split_hi(u)
                    for e in range(c * TT, (c + 1) * TT, 2):
                        evacuate(e)
                for u in range(N_TOK, N_IN):
                    for v in ([u + 2, u + 3] if u == N_TOK else [u + 3]):
                        if v < N_IN:
                            split_hi(v)
                    evacuate(E_TOK + 2 * (u - N_TOK))

                act.wait_ge(qk_sums, 1)
                act.activation(rqk[:], ssq[:], ACT.Sqrt, bias=eps[:], scale=1.0 / HD).then_inc(qk_rms, 1)
                for tt in range(TT):
                    bank, tok = tt % 2 * 2, slice(tt * P, (tt + 1) * P)
                    act.wait_ge(qkT_psum, 2 * tt + 1)
                    act.activation(qT[:, :, tok], ps[:, bank, :].rearrange("p (b t) -> p b t", b=AH // 2),
                                   ACT.Copy).then_inc(qkT_ready, 1)
                    act.wait_ge(qkT_psum, 2 * tt + 2)
                    act.activation(kT[:, :, tok], ps[:, bank + 1, 0:2 * P].rearrange("p (b t) -> p b t", b=KVH),
                                   ACT.Copy).then_inc(qkT_ready, 1)
                n_att = NSEQ * AH * SB
                for v in range(n_att):
                    act.wait_ge(nmx_ready, v + 1)
                    if v >= 2:
                        act.wait_ge(pT_psum, v - 1)
                    act.activation(prob[:, v % 2, :], ps[:, 4 + v % 2, :], ACT.Exp, bias=nmx[:, v:v + 1],
                                   accum_out=rsum[:, v:v + 1]).then_inc(prob_ready, 1)

                act.wait_ge(ao_done, n_att)
                for d in range(2):
                    for j in range(4):
                        r = d * 4 + j
                        if r >= 2:
                            act.wait_ge(la_ready, r - 1)
                        act.wait_ge(z_psum, r + 1)
                        e = ee[:, j % 2, :]
                        link(act.activation(e, ps[:, j, :], ACT.Abs, bias=vec[:, V_GB + 2 * d + j // 2:V_GB + 2 * d + j // 2 + 1]))
                        link(act.activation(e, e, ACT.Exp, scale=-1.0))
                        act.activation(e, e, ACT.Ln, bias=ones[:, 0:1]).then_inc(ln_ready, 1)
                    act.wait_ge(cum_ready, 2 * d + 2)
                    for ht in range(2):
                        r = d * 2 + ht
                        for m, (src, sc) in enumerate(((dml[:], 1), (dml[:], -1), (G[:, ht, :], 1), (dml[:], 1))):
                            n = 4 * r + m
                            if m in (0, 1, 3):
                                act.wait_ge(dml_ready, 2 * r + (2 if m == 3 else 1))
                            if n >= 2:
                                act.wait_ge(gx_used, n - 1)
                            act.activation(gx[:, m % 2, :], src, ACT.Exp, scale=sc / GLA_TAU).then_inc(gx_ready, 1)
                        last = CH - 1 if d == 0 else 0
                        if d == 1 and ht == 0:
                            act.wait_ge(state_ready, NCH - 1)
                        act.activation(aL[:, ht, :], G[:, ht, :].rearrange("p (c t) -> p c t", t=CH)[:, :, last],
                                       ACT.Exp, scale=1.0 / GLA_TAU).then_inc(aL_ready, 1)
                        for b in range(2):
                            act.wait_ge(ktil_psum, 2 * r + b + 1)
                            if d == 1 and ht == 0 and b == 0:
                                act.wait_ge(kv_psum, NCH - 1)
                            act.activation(ktok[:, 4 * b:4 * b + 4, ht * P:(ht + 1) * P],
                                           ps[:, 4 + b, :].rearrange("p (i c) -> p i c", i=4), ACT.Copy)\
                               .then_inc(ktok_ready, 1)
                act.wait_ge(go_evac, 2 * TT)
                for hb in range(2):
                    act.activation(gx[:, hb, :].rearrange("p (t c) -> p t c", t=4), oacc[:, 4 * hb:4 * hb + 4, :],
                                   ACT.Square, scale=HD ** -0.5).then_inc(gsq_ready, 1)
                act.wait_ge(gss_ready, 2)
                act.activation(gss[:, 1, :], gss[:, 0, :], ACT.Sqrt, bias=eps[:], scale=1.0 / HD)\
                   .then_inc(grms_ready, 1)
                for hb in range(2):
                    act.activation(gx[:, hb, :].rearrange("p (t c) -> p t c", t=4), gg[:, 4 * hb:4 * hb + 4, :],
                                   ACT.Sigmoid).then_inc(gsig_ready, 1)

                act.activation(co[:], co[:], ACT.Sigmoid).then_inc(msig_ready, 1)
                act.wait_ge(yf_ready, 1)
                link(act.activation(fl[:], yf[:], ACT.Abs))
                link(act.activation(fl[:], fl[:], ACT.Exp, scale=-1.0))
                act.activation(fl[:], fl[:], ACT.Ln, bias=ones[0:GROWS, 0:1]).then_inc(fl_ready, 1)
                act.wait_ge(ct_psum, 1)
                act.activation(CT[:], ps[:, 0, 0:TT * GROWS].rearrange("p (t r) -> p t r", t=TT), ACT.Copy)\
                   .then_inc(ct_ready, 1)
                act.wait_ge(ct_psum, 2)
                act.activation(EM[:], ps[:, 1, 0:TT * GROWS].rearrange("p (t r) -> p t r", t=TT), ACT.Exp,
                               scale=-1.0).then_inc(ct_ready, 1)
                act.wait_ge(ct_ready, 2)
                for w in range(NSEQ * MH):
                    s, h = w // MH, w % MH
                    if w >= 1:
                        act.wait_ge(num_psum, w)
                    for d in range(2):
                        act.wait_ge(rb_psum, 2 * w + d + 1)
                        act.wait_ge(mr_ready, 2 * w + d + 1)
                        for i in range(SB):
                            lo, hi = fwd_or_bwd_range(d, i)
                            own = slice(i * P, (i + 1) * P)
                            bias = CT[:, s * SB + i, 32 * d + h:32 * d + h + 1]
                            rest = slice((i + 1) * P, SEQ) if d == 0 else slice(0, i * P)
                            if rest.stop > rest.start:
                                act.activation(Dt[:, d, i, rest], ps[:, 4 + d, rest], ACT.Exp, bias=bias)
                            act.activation(Dt[:, d, i, own], mR[:, d, own], ACT.Exp, bias=bias)\
                               .then_inc(dt_ready, 1)
                act.wait_ge(heads_gated, 1)
                for hb in range(2):
                    sq_to = Dt[:, hb, 0:2, :].rearrange("p a b -> p (a b)").rearrange("p (t c) -> p t c", t=4)
                    act.activation(sq_to, co[:, 4 * hb:4 * hb + 4, :], ACT.Square).then_inc(msq_ready, 1)
                act.wait_ge(mss_ready, 2)
                act.activation(mss[:, 1, :], mss[:, 0, :], ACT.Sqrt, bias=eps[:], scale=1.0 / HD)\
                   .then_inc(mrms_ready, 1)

                act.wait_ge(ml_done, 1)
                for u in range(N_IN, N_IN + SPLIT):
                    split_hi(u)
                for tt in range(TT):
                    tok = slice(tt * P, (tt + 1) * P)
                    bank = tt % 4 * 2
                    act.wait_ge(mix_psum, 2 * tt + 1)
                    act.activation(hh[:, 0:4, tok], ps[:, bank, :].rearrange("p (i t) -> p i t", i=4), ACT.Copy)\
                       .then_inc(mixh_ready, 1)
                    act.wait_ge(mix_psum, 2 * tt + 2)
                    for i, g in enumerate((V_GLAN, V_MLN)):
                        act.activation(hh[:, 4 + 2 * i:6 + 2 * i, tok],
                                       ps[:, bank + 1, 2 * i * P:(2 * i + 2) * P].rearrange("p (i t) -> p i t", i=2),
                                       ACT.Copy, scale=vec[:, g:g + 1]).then_inc(mixh_ready, 1)
                for u in range(N_IN + SPLIT, N_UNITS):
                    split_hi(u)

                act.wait_ge(wo_done, KT)

                def ffn_hi(kind, j):
                    act.wait_ge(f_full[kind], 16 * (j + 1))
                    act.activation(whi[:, kind, :, :], raw[:, kind, :].rearrange("p (k c) -> p k c", k=KT),
                                   ACT.Copy).then_inc(f_hi[kind], 1)

                act.wait_ge(unit_used, N_UNITS)
                for kind in (0, 1):
                    ffn_hi(kind, 0)
                norm(1)
                act.wait_ge(h_ready, 2 * NSEQ * KT)
                act.wait_ge(conv_loaded, 16)

                def iteration(j, first=False, last=False):
                    if not first:
                        act.wait_ge(v_conv, j)
                    act.activation(cw[:], convs[:, j, :], ACT.Copy).then_inc(cw_ready, 1)
                    act.wait_ge(cw_ready, j + 1)
                    act.wait_ge(f_used[0], j + 1)
                    act.activation(accg[:], ps[:, 0:2, :], ACT.Identity, bias=cw[:, 3:4], scale=cw[:, 1:2])\
                       .then_inc(g_init, 1)
                    if not last:
                        ffn_hi(0, j + 1)
                    if not first:
                        act.wait_ge(act_ready, j)
                    act.wait_ge(g_conv, j + 1)
                    act.activation(sil[:], accg[:], ACT.Silu).then_inc(sil_ready, 1)
                    act.wait_ge(f_used[1], j + 1)
                    if not first:
                        act.wait_ge(actl_ready, j)
                    act.activation(accv[:], ps[:, 2:4, :], ACT.Identity, bias=cw[:, 7:8], scale=cw[:, 5:6])\
                       .then_inc(v_init, 1)
                    if not last:
                        ffn_hi(1, j + 1)
                    if not first:
                        act.wait_ge(f_used[2], j)
                    ffn_hi(2, j)
                    act.wait_ge(act_ready, j + 1)
                    act.activation(acth[:], accv[:], ACT.Copy).then_inc(acth_ready, 1)
                    act.wait_ge(sil_ready, j + 1)

                iteration(0, first=True)
                with act.Fori(1, FT - 1) as j:
                    iteration(j)
                iteration(FT - 1, last=True)
                act.sem_inc(layer_end, 1)
                act.wait_ge(layer_go, l + 1)

        @block.vector
        def _(dve):
            dve.memset(ones[:], 1.0).then_inc(ones_set, 1)
            dve.memset(eps[:], EPS).then_inc(ones_set, 1)
            dve.wait_ge(ones_set, 2)
            dve.wait_ge(x_loaded, 16 * KT)
            with dve.Fori(0, DEPTH) as l:
                chain = [0]

                def link(ins):
                    chain[0] += 1
                    ins.then_inc(dve_chain, 1)
                    dve.wait_ge(dve_chain, chain[0])

                def split_lo(n):
                    dve.wait_ge(hi_ready, n + 1)
                    dve.tensor_tensor(wlo[:, n % SPLIT, :, :],
                                      raw[:, n % RAW, :].rearrange("p (k c) -> p k c", k=KT),
                                      whi[:, n % SPLIT, :, :].bitcast(F32), ALU.subtract).then_inc(lo_ready, 1)

                def norm(n, gain):
                    for s in range(NSEQ):
                        dve.wait_ge(rms_ready, n * NSEQ + s + 1)
                        link(dve.reciprocal(rinv[:, s, :], rms[:, s, :]))
                        tok = slice(s * SEQ, (s + 1) * SEQ)
                        for k in range(KT + 1):
                            i = (n * NSEQ + s) * KT + k
                            if k < KT:
                                if i >= 2:
                                    dve.wait_ge(h_ready, i - 1)
                                dve.scalar_tensor_tensor(hf[:, i % 2, :], x[:, k, tok], vec[:, gain + k:gain + k + 1],
                                                         rinv[:, s, :], ALU.mult, ALU.mult).then_inc(hf_ready, 1)
                            if k >= 1:
                                dve.wait_ge(hh_ready, i)
                                dve.tensor_tensor(hl[:, k - 1, tok], hf[:, (i - 1) % 2, :],
                                                  hh[:, k - 1, tok].bitcast(F32), ALU.subtract).then_inc(h_ready, 1)

                split_lo(0)
                split_lo(1)
                dve.wait_ge(vec_loaded, 16)
                norm(0, V_MIX)
                split_lo(2)
                split_lo(3)
                dve.wait_ge(h_ready, NSEQ * KT)
                link(dve.memset(vaug[:, :, :, HD:HD + 1], 1.0))

                def evacuate(e):
                    if e == E_TOK + 1:
                        dve.wait_ge(spilled, 16)
                    dve.wait_ge(proj_ready, e + 1)
                    dst, src = evac_source(e)
                    dve.tensor_copy(dst, src).then_inc(dve_evac, 1)

                for c in range(len(TOK_COLS)):
                    if c >= 1:
                        for u in (2 * c + 2, 2 * c + 3):
                            split_lo(u)
                    for e in range(c * TT + 1, (c + 1) * TT, 2):
                        evacuate(e)
                for u in range(N_TOK, N_IN):
                    for v in ([u + 2, u + 3] if u == N_TOK else [u + 3]):
                        if v < N_IN:
                            split_lo(v)
                    evacuate(E_TOK + 2 * (u - N_TOK) + 1)

                dve.wait_ge(att_consts, 48)
                dve.wait_ge(dve_evac, E_ALL // 2)
                dve.wait_ge(act_evac, E_ALL // 2)
                for tab, base in ((tabc, ropec), (tabs, ropes)):
                    for g, (h0, nh) in enumerate(((0, AH), (AH, KVH))):
                        shape = [P, SB, nh, HD]
                        link(dve.tensor_tensor(
                            tab[:, :, h0:h0 + nh, :],
                            base[:].unsqueeze(2).to_broadcast(shape),
                            qkgain[:, g:g + 1, :].unsqueeze(1).to_broadcast(shape), ALU.mult))
                for tt in range(TT):
                    qk = tokA[:, tt, 0:NQK * HD]
                    link(dve.tensor_tensor(t1[:], qk, qk, ALU.mult))
                    link(dve.tensor_reduce(ssq[:, tt, :], t1[:].rearrange("p (h d) -> p h d", h=NQK), AX_X, ALU.add))
                dve.sem_inc(qk_sums, 1)
                dve.wait_ge(qk_rms, 1)
                link(dve.reciprocal(rqk[:], rqk[:]))
                link(dve.tensor_scalar(rqk[:, :, AH:NQK], rqk[:, :, AH:NQK], HD ** -0.5, None, ALU.mult))
                for tt in range(TT):
                    qk = tokA[:, tt, 0:NQK * HD]
                    half = HD // 4
                    link(dve.tensor_tensor(t2[:], qk, tabs[:, tt % SB, :, :].rearrange("p h d -> p (h d)"), ALU.mult))
                    link(dve.tensor_tensor(t1[:], qk, tabc[:, tt % SB, :, :].rearrange("p h d -> p (h d)"), ALU.mult))
                    link(dve.tensor_tensor(t1[:].rearrange("p (a r f) -> p a r f", r=2, f=half),
                                           t1[:].rearrange("p (a r f) -> p a r f", r=2, f=half),
                                           t2[:].rearrange("p (a r f) -> p a r f", r=2, f=half)[:, :, ::-1, :], ALU.add))
                    if tt >= 2:
                        dve.wait_ge(qkT_psum, 2 * (tt - 2) + 2)
                    r3 = t1[:].rearrange("p (h d) -> p h d", h=NQK)
                    rk = rqk[:, tt, AH:NQK].unsqueeze(2)
                    for rep in range(2):
                        link(dve.tensor_tensor(kdup[:, tt % 2, :, rep, :], r3[:, AH:NQK, :],
                                               rk.to_broadcast([P, KVH, HD]), ALU.mult))
                    dve.tensor_tensor(tokA[:, tt, 0:AH * HD].rearrange("p (h d) -> p h d", h=AH), r3[:, 0:AH, :],
                                      rqk[:, tt, 0:AH].unsqueeze(2).to_broadcast([P, AH, HD]), ALU.mult)\
                       .then_inc(rot_ready, 1)
                    dve.wait_ge(rot_ready, tt + 1)
                n_att = NSEQ * AH * SB
                for i in range(n_att + 2):
                    if i < n_att:
                        dve.wait_ge(sc_ready, i + 1)
                        dve.tensor_reduce(nmx[:, i:i + 1], ps[:, 4 + i % 2, :], AX_X, ALU.max, negate=True)\
                           .then_inc(nmx_ready, 1)
                    if 1 <= i <= n_att:
                        v = i - 1
                        dve.wait_ge(pT_psum, v + 1)
                        if v >= 2:
                            dve.wait_ge(ao_psum, v - 1)
                        dve.tensor_copy(pT[:, v % 2, :, :].rearrange("p k q -> p (k q)"), ps[:, 6 + v % 2, :])\
                           .then_inc(pT_ready, 1)
                        link(dve.reciprocal(rinvp[:, v:v + 1], rsum[:, v:v + 1]))
                    if i >= 2:
                        v = i - 2
                        s, h, qt = v // (AH * SB), v // SB % AH, v % SB
                        dve.wait_ge(ao_psum, v + 1)
                        dve.tensor_scalar(tokA[:, s * SB + qt, h * HD:(h + 1) * HD], ps[:, v % 2, 0:HD],
                                          rinvp[:, v:v + 1], None, ALU.mult).then_inc(ao_done, 1)

                dve.wait_ge(ao_done, n_att)
                dve.wait_ge(gla_consts, 48)
                link(dve.memset(attT[:], 0.0))
                for d in range(2):
                    rev = slice(None, None, -1) if d else slice(None)
                    if d == 1:
                        link(dve.memset(attT[:], 0.0))
                    for j in range(4):
                        r = d * 4 + j
                        gs = G[:, j // 2, j % 2 * SEQ:(j % 2 + 1) * SEQ]
                        b0 = V_GB + 2 * d + j // 2
                        dve.wait_ge(ln_ready, r + 1)
                        link(dve.tensor_scalar(gs, ps[:, j, :], vec[:, b0:b0 + 1], 0.0, ALU.add, ALU.min))
                        dve.tensor_tensor(gs, gs, ee[:, j % 2, :], ALU.subtract).then_inc(la_ready, 1)
                        dve.wait_ge(la_ready, r + 1)
                        if j % 2:
                            for s in range(NSEQ):
                                gq = G[:, j // 2, s * SEQ:(s + 1) * SEQ][:, rev]
                                ins = dve.tensor_tensor_scan(gq, cmask[:], gq, 0.0,
                                                             ALU.mult, ALU.add)
                                if s == 0:
                                    link(ins)
                                else:
                                    ins.then_inc(cum_ready, 1)
                                    dve.wait_ge(cum_ready, 2 * d + j // 2 + 1)
                    mid, last = (CH // 2 - 1, CH - 1) if d == 0 else (CH // 2, 0)
                    for ht in range(2):
                        r = d * 2 + ht
                        gc = G[:, ht, :].rearrange("p (c t) -> p c t", t=CH)
                        shape = [P, NSEQ * NCH, CH]
                        q, k = qkG[:, ht, :], qkG[:, 2 + ht, :]
                        dv = dml[:].rearrange("p (c t) -> p c t", t=CH)
                        dve.tensor_tensor(dv, gc, gc[:, :, mid:mid + 1].to_broadcast(shape), ALU.subtract)\
                           .then_inc(dml_ready, 1)
                        for m, (dst, src) in enumerate(((qhat[:, ht, :], q), (khat[:, ht, :], k),
                                                        (qtil[:, ht, :], q), (ktil[:], k))):
                            n = 4 * r + m
                            dve.wait_ge(gx_ready, n + 1)
                            if m == 3 and r >= 1:
                                dve.wait_ge(ktil_psum, 2 * r)
                            if m == 0 and r == 2:
                                dve.wait_ge(go_psum, TT)
                            dve.tensor_tensor(dst, src, gx[:, m % 2, :], ALU.mult).then_inc(gx_used, 1)
                            dve.wait_ge(gx_used, n + 1)
                            if m == 1:
                                dve.tensor_tensor(dv, gc[:, :, last:last + 1].to_broadcast(shape), gc, ALU.subtract)\
                                   .then_inc(dml_ready, 1)
                    dve.wait_ge(aL_ready, 2 * d + 2)
                    link(dve.memset(st[:, 0, :, :, :], 0.0))
                    for c in range(NCH - 1):
                        ci = step_of(d, c)
                        n = d * (NCH - 1) + c
                        decay = aL[:].rearrange("p h (s c) -> p s h c", s=NSEQ)[:, :, :, ci:ci + 1]
                        link(dve.tensor_tensor(gtmp[:].rearrange("p (s h e) -> p s h e", s=2, h=2), st[:, c, :, :, :],
                                               decay.to_broadcast([P, NSEQ, 2, HD]), ALU.mult))
                        dve.wait_ge(kv_psum, n + 1)
                        dve.tensor_tensor(st[:, c + 1, :, :, :].rearrange("p s h e -> p (s h e)"), gtmp[:],
                                          ps[:, 6 + n % 2, 0:256], ALU.add).then_inc(state_ready, 1)
                        dve.wait_ge(state_ready, n + 1)
                    for i in range(TT + 1):
                        if i < TT:
                            n = d * TT + i
                            dve.wait_ge(gat_psum, n + 1)
                            if i >= 2:
                                dve.wait_ge(go_psum, n - 1)
                            dve.copy_predicated(attT[:, i % 2, :, :, :],
                                                gam[:, d:d + 1, :].unsqueeze(1).to_broadcast([P, 2, 2, P]),
                                                ps[:, i % 2 * 4:i % 2 * 4 + 2, 0:2 * P].rearrange(
                                                    "p r (q t) -> p r q t", q=2))\
                               .then_inc(gat_ready, 1)
                        if i >= 1:
                            tt = i - 1
                            n = d * TT + tt
                            dve.wait_ge(go_psum, n + 1)
                            b = 2 + tt % 2 * 4
                            got = ps[:, b:b + 2, 0:2 * HD].rearrange("p r (q d) -> p r q d", q=2)
                            acc = oacc[:, tt, :].rearrange("p (q r d) -> p r q d", q=2, r=2)
                            if d == 0:
                                dve.tensor_copy(acc, got).then_inc(go_evac, 1)
                            else:
                                dve.tensor_tensor(acc, acc, got, ALU.add)\
                                   .then_inc(go_evac, 1)
                    dve.wait_ge(go_evac, (d + 1) * TT)
                for hb in range(2):
                    dve.wait_ge(gsq_ready, hb + 1)
                    dve.tensor_reduce(gss[:, 0, hb * 16:(hb + 1) * 16],
                                      gx[:, hb, :].rearrange("p (a d) -> p a d", d=HD), AX_X, ALU.add)\
                       .then_inc(gss_ready, 1)
                dve.wait_ge(grms_ready, 1)
                link(dve.reciprocal(gss[:, 0, :], gss[:, 1, :]))
                link(dve.tensor_scalar(gss[:, 0, :], gss[:, 0, :], HD ** -0.5, None, ALU.mult))
                oa = oacc[:].rearrange("p t (h d) -> p (t h) d", d=HD)
                link(dve.tensor_tensor(oa, oa, gss[:, 0, :].unsqueeze(2).to_broadcast([P, TT * GH, HD]), ALU.mult))
                dve.wait_ge(gsig_ready, 2)
                flat = "p t c -> p (t c)"
                link(dve.tensor_tensor(oacc[:].rearrange(flat), oacc[:].rearrange(flat), gg[:].rearrange(flat), ALU.mult))
                dve.tensor_tensor(gg[:].rearrange(flat), oacc[:].rearrange(flat), gx[:].rearrange("p a b -> p (a b)"),
                                  ALU.mult).then_inc(gla_done, 1)
                dve.wait_ge(gla_done, 1)

                dve.wait_ge(ml_consts, 32)
                dve.tensor_scalar(yf[:], small[64:64 + GROWS, :], vec[64:64 + GROWS, V_GBF:V_GBF + 1], None, ALU.add)\
                   .then_inc(yf_ready, 1)
                link(dve.tensor_scalar(ri[:], small[0:GROWS, :], vec[0:GROWS, V_GBI:V_GBI + 1], None, ALU.add))
                link(dve.memset(zr[:], 0.0))
                link(dve.memset(Fc[:], 0.0))
                link(dve.memset(mm_rows[:], 0.0))
                dve.wait_ge(yf_ready, 1)
                dve.wait_ge(fl_ready, 1)
                link(dve.scalar_tensor_tensor(fl[:], yf[:], 0.0, fl[:], ALU.min, ALU.subtract))
                for d in range(2):
                    rows = slice(32 * d, 32 * d + MH)
                    rev = slice(None, None, -1) if d else slice(None)
                    for s in range(NSEQ):
                        tok = slice(s * SEQ, (s + 1) * SEQ)
                        lf, ig = fl[rows, tok][:, rev], ri[rows, tok][:, rev]
                        link(dve.tensor_tensor_scan(Fc[rows, tok][:, rev], lf, zr[rows, :], 0.0, ALU.add, ALU.add))
                        link(dve.tensor_tensor_scan(mm_rows[rows, tok][:, rev], lf, ig, 0.0, ALU.add, ALU.max))
                link(dve.tensor_tensor(Rr[:], Fc[:], mm_rows[:], ALU.subtract))
                dve.tensor_tensor(Cr[:], ri[:], Fc[:], ALU.subtract).then_inc(rc_ready, 1)
                for w in range(NSEQ * MH):
                    s, h = w // MH, w % MH
                    for d in range(2):
                        dve.wait_ge(rb_psum, 2 * w + d + 1)
                        if w >= 1:
                            dve.wait_ge(dt_ready, 2 * SB * w)
                        dve.tensor_tensor(mR[:, d, :].rearrange("p (j t) -> p j t", j=SB),
                                          ps[:, 4 + d, :].rearrange("p (j t) -> p j t", j=SB),
                                          mmask[:, d:d + 1, :].to_broadcast([P, SB, P]), ALU.add).then_inc(mr_ready, 1)
                    for d in range(2):
                        for i in range(SB):
                            lo, hi = fwd_or_bwd_range(d, i)
                            dve.wait_ge(dt_ready, 2 * SB * w + d * SB + i + 1)
                            dve.wait_ge(qk_psum, SB * w + i + 1)
                            dve.scalar_tensor_tensor(Dt[:, d, i, lo:hi], ps[:, i, lo:hi], HD ** -0.5,
                                                     Dt[:, d, i, lo:hi], ALU.mult, ALU.mult).then_inc(wt_ready, 1)
                    num = ps[:, 6:8, 0:SB * (HD + 1)].rearrange("p d (j e) -> p d j e", j=SB)
                    dve.wait_ge(num_psum, w + 1)
                    link(dve.tensor_copy(dn[:].unsqueeze(3), num[:, :, :, HD:HD + 1]))
                    link(dve.scalar_tensor_tensor(rc[:], dn[:], -1.0, dn[:], ALU.mult, ALU.max))
                    link(dve.tensor_tensor(
                        rc[:], rc[:], EM[:, s * SB:(s + 1) * SB, h:h + 33:32].rearrange("p t d -> p d t"), ALU.max))
                    link(dve.reciprocal(rc[:], rc[:]))
                    dve.tensor_tensor(t12[:], num[:, :, :, 0:HD], rc[:].unsqueeze(3).to_broadcast([P, 2, SB, HD]),
                                      ALU.mult).then_inc(ml_evac, 1)
                    dve.wait_ge(ml_evac, w + 1)
                    link(dve.tensor_tensor(hs[:], t12[:, 0, :, :], t12[:, 1, :, :], ALU.add))
                    cs = co[:, s * SB:(s + 1) * SB, h * HD:(h + 1) * HD]
                    dve.wait_ge(msig_ready, 1)
                    link(dve.tensor_tensor(cs, cs, hs[:], ALU.mult))
                dve.sem_inc(heads_gated, 1)
                for hb in range(2):
                    dve.wait_ge(msq_ready, hb + 1)
                    dve.tensor_reduce(mss[:, 0, hb * 16:(hb + 1) * 16],
                                      Dt[:, hb, 0:2, :].rearrange("p a b -> p (a b)").rearrange("p (a d) -> p a d", d=HD),
                                      AX_X, ALU.add).then_inc(mss_ready, 1)
                dve.wait_ge(mrms_ready, 1)
                link(dve.reciprocal(mss[:, 0, :], mss[:, 1, :]))
                ca = co[:].rearrange("p t (h d) -> p (t h) d", d=HD)
                dve.tensor_tensor(ca, ca, mss[:, 0, :].unsqueeze(2).to_broadcast([P, TT * MH, HD]), ALU.mult)\
                   .then_inc(ml_done, 1)
                dve.wait_ge(ml_done, 1)

                for u in range(N_IN, N_IN + SPLIT):
                    split_lo(u)
                for tt in range(TT):
                    tok = slice(tt * P, (tt + 1) * P)
                    bank = tt % 4 * 2
                    dve.wait_ge(mixh_ready, 3 * tt + 1)
                    dve.tensor_tensor(hl[:, 0:4, tok], ps[:, bank, :].rearrange("p (i t) -> p i t", i=4),
                                      hh[:, 0:4, tok].bitcast(F32), ALU.subtract).then_inc(mixl_ready, 1)
                    dve.wait_ge(mixh_ready, 3 * tt + 3)
                    for i, g in enumerate((V_GLAN, V_MLN)):
                        dve.scalar_tensor_tensor(
                            hl[:, 4 + 2 * i:6 + 2 * i, tok],
                            ps[:, bank + 1, 2 * i * P:(2 * i + 2) * P].rearrange("p (i t) -> p i t", i=2),
                            vec[:, g:g + 1], hh[:, 4 + 2 * i:6 + 2 * i, tok].bitcast(F32), ALU.mult,
                            ALU.subtract).then_inc(mixl_ready, 1)
                dve.wait_ge(reloaded, 16)
                for o in range(KT):
                    dve.wait_ge(wo_psum, o + 1)
                    dve.tensor_tensor(x[:, o, :], x[:, o, :], ps[:, o % 4 * 2:o % 4 * 2 + 2, :].rearrange("p s t -> p (s t)"),
                                      ALU.add).then_inc(wo_done, 1)
                    if o + SPLIT < KT:
                        split_lo(N_IN + SPLIT + o)

                def ffn_lo(kind, j):
                    dve.wait_ge(f_hi[kind], j + 1)
                    dve.tensor_tensor(wlo[:, kind, :, :], raw[:, kind, :].rearrange("p (k c) -> p k c", k=KT),
                                      whi[:, kind, :, :].bitcast(F32), ALU.subtract).then_inc(f_lo[kind], 1)

                for kind in (0, 1):
                    ffn_lo(kind, 0)
                norm(1, V_FFN)

                def conv(acc, pair, taps, init, half, done, j):
                    dve.wait_ge(init, j + 1)
                    dve.scalar_tensor_tensor(acc[:, :, 1:SEQ], ps[:, pair:pair + 2, 0:SEQ - 1], cw[:, taps:taps + 1],
                                             acc[:, :, 1:SEQ], ALU.mult, ALU.add).then_inc(half, 1)
                    dve.wait_ge(half, j + 1)
                    dve.scalar_tensor_tensor(acc[:, :, 0:SEQ - 1], ps[:, pair:pair + 2, 1:SEQ], cw[:, taps + 2:taps + 3],
                                             acc[:, :, 0:SEQ - 1], ALU.mult, ALU.add).then_inc(done, 1)

                def add_down(j):
                    for o in range(KT):
                        dve.wait_ge(d_psum, j * KT + o + 1)
                        b = 4 + o % 2 * 2
                        dve.tensor_tensor(x[:, o, :], x[:, o, :], ps[:, b:b + 2, :].rearrange("p s t -> p (s t)"),
                                          ALU.add).then_inc(d_done, 1)

                def iteration(j, first=False, last=False):
                    conv(accg, 0, 0, g_init, g_half, g_conv, j)
                    if not last:
                        ffn_lo(0, j + 1)
                    if not first:
                        add_down(j - 1)
                    conv(accv, 2, 4, v_init, v_half, v_conv, j)
                    if not last:
                        ffn_lo(1, j + 1)
                    dve.wait_ge(sil_ready, j + 1)
                    dve.wait_ge(v_conv, j + 1)
                    dve.tensor_tensor(accv[:], accv[:], sil[:], ALU.mult).then_inc(act_ready, 1)
                    ffn_lo(2, j)
                    dve.wait_ge(acth_ready, j + 1)
                    dve.tensor_tensor(actl[:], accv[:], acth[:].bitcast(F32), ALU.subtract).then_inc(actl_ready, 1)

                iteration(0, first=True)
                with dve.Fori(1, FT - 1) as j:
                    iteration(j)
                iteration(FT - 1, last=True)
                add_down(FT - 1)
                dve.sem_inc(layer_end, 1)
                dve.wait_ge(layer_go, l + 1)


def axial_tables():
    pos = np.arange(SEQ)
    row = (pos // GRID_W).astype(np.float32)
    col = (pos % GRID_W).astype(np.float32)
    n = HD // 4
    inv = np.power(np.float32(ROPE_THETA), -np.arange(n, dtype=np.float32) / np.float32(n)).astype(np.float32)
    ang = np.stack([row[:, None] * inv, col[:, None] * inv], axis=1)
    c, s = np.cos(ang), np.sin(ang)
    cos = np.stack([c, c], axis=2).reshape(SEQ, HD)
    sin = np.stack([s, -s], axis=2).reshape(SEQ, HD)
    lay = lambda t: t.reshape(SB, P, HD).transpose(1, 0, 2)
    return np.ascontiguousarray(np.stack([lay(cos), lay(sin)])).astype(np.float32)


def masks():
    s, t = np.arange(P)[:, None], np.arange(P)[None, :]
    same = (s // CH) == (t // CH)
    gla = np.stack([same & (s <= t), same & (s >= t)], axis=1).astype(np.uint32)
    chunk = np.broadcast_to((np.arange(SEQ) % CH != 0).astype(np.float32), (P, SEQ))
    ml = np.stack([np.where(s <= t, 0.0, -1e30), np.where(s >= t, 0.0, -1e30)], axis=1).astype(np.float32)
    sel = np.zeros((GROWS, 2 * MH, P), np.float32)
    for d in range(2):
        for h in range(MH):
            sel[32 * d + h, d * MH + h, :] = 1.0
    return gla, np.ascontiguousarray(chunk), ml, sel


def layouts(i):
    f = lambda a: np.asarray(a, np.float32) if np.asarray(a).dtype != np.float32 else np.asarray(a)
    x = np.concatenate([f(i["x_prompt"])[0], f(i["x_sample"])[0]], axis=0)
    x_in = np.ascontiguousarray(x.T.reshape(KT, P, T).transpose(1, 0, 2))
    w_in = f(i["w_in"])
    small = np.zeros((DEPTH, D, P), np.float32)
    for d in range(2):
        small[:, :, 32 * d:32 * d + MH] = w_in[:, :, CG + d * MH:CG + (d + 1) * MH]
        small[:, :, BA_ROW[d]:BA_ROW[d] + 16] = w_in[:, :, BA + 16 * d:BA + 16 * (d + 1)]
        small[:, :, 64 + 32 * d:64 + 32 * d + MH] = w_in[:, :, CG + (2 + d) * MH:CG + (3 + d) * MH]
    cols = [c + o for c in TOK_COLS for o in (0, P)] + FEAT_COLS
    unit = lambda w: w.reshape(DEPTH, KT, P, P).transpose(0, 2, 1, 3).reshape(DEPTH, P, UNIT)
    units = [unit(w_in[:, :, c:c + P]) for c in cols] + [unit(small)]
    w_out = f(i["w_out"])
    units += [unit(w_out[:, :, o * P:(o + 1) * P]) for o in range(KT)]
    w_units = np.ascontiguousarray(np.stack(units, axis=1))
    up = f(i["w_up"]).reshape(DEPTH, KT, P, 2, FT, P).transpose(0, 4, 3, 2, 1, 5).reshape(DEPTH, FT, 2, P, UNIT)
    down = f(i["w_down"]).reshape(DEPTH, FT, 1, P, UNIT)
    w_ffn = np.ascontiguousarray(np.concatenate([up, down], axis=2))
    vecs = np.zeros((DEPTH, P, NVEC), np.float32)
    vecs[:, :, V_MIX:V_MIX + KT] = f(i["norm_mix_g"]).reshape(DEPTH, KT, P).transpose(0, 2, 1)
    vecs[:, :, V_FFN:V_FFN + KT] = f(i["norm_ffn_g"]).reshape(DEPTH, KT, P).transpose(0, 2, 1)
    vecs[:, :, V_GLAN] = np.tile(f(i["gla_norm_g"]), (1, 2))
    vecs[:, :, V_MLN] = np.tile(f(i["mlstm_norm_g"]), (1, 2))
    vecs[:, :, V_GB:V_GB + 4] = f(i["gla_gate_b"]).reshape(DEPTH, 4, P).transpose(0, 2, 1)
    gb = f(i["mlstm_gate_b"])
    for d in range(2):
        vecs[:, 32 * d:32 * d + MH, V_GBI] = gb[:, d]
        vecs[:, 64 + 32 * d:64 + 32 * d + MH, V_GBF] = gb[:, 2 + d]
    w2p = np.zeros((DEPTH, P, 2, 256), np.float32)
    for d in range(2):
        w2p[:, BA_ROW[d]:BA_ROW[d] + 16, d, :] = f(i["gla_gate_w2"])[:, d]
    qkg = np.stack([f(i["attn_qn_g"]), f(i["attn_kn_g"])], axis=1)
    qkg = np.ascontiguousarray(np.broadcast_to(qkg[:, None], (DEPTH, P, 2, HD)))
    taps = np.concatenate([f(i["conv_w"]), f(i["conv_b"])[:, None]], axis=1)
    convp = np.ascontiguousarray(taps.reshape(DEPTH, 4, 2, FT, P).transpose(0, 4, 3, 2, 1).reshape(DEPTH, P, FT, 8))
    gla, chunk, ml, sel = masks()
    return {"x_in": x_in, "w_units": w_units, "w_ffn": w_ffn, "vecs": vecs, "w2p": w2p, "qkg": qkg,
            "convp": convp, "rope": axial_tables(), "gmask": gla, "chunkmask": chunk, "lmask": ml,
            "sel": sel, "ident_in": np.eye(P, dtype=np.float32)}


def kernel(**inputs):
    import concourse.bacc as bacc
    from concourse.bass_utils import run_bass_kernel_spmd as run

    arrays = layouts(inputs)
    nc = bacc.Bacc("TRN2", target_bir_lowering=False, num_devices=1)
    args = [nc.dram_tensor(f"d_{n}", a.shape, mybir.dt.from_np(a.dtype), kind="ExternalInput").ap()
            for n, a in arrays.items()]
    out = nc.dram_tensor("d_x_out", (P, KT, T), F32, kind="ExternalOutput").ap()
    build(nc, *args, out)
    r = run(nc, [{f"d_{n}": a for n, a in arrays.items()}], core_ids=[0])
    y = r.results[0]["d_x_out"].transpose(1, 0, 2).reshape(D, T)
    return (np.ascontiguousarray(y[:, 0:SEQ].T)[None], np.ascontiguousarray(y[:, SEQ:T].T)[None])
```

```python
from contextlib import ExitStack

import numpy as np

import concourse.bass as bass
from concourse import mybir
from concourse.alu_op_type import AluOpType as ALU

F32 = mybir.dt.float32
F32R = mybir.dt.float32r
U32 = mybir.dt.uint32
ACT = mybir.ActivationFunctionType
AX_X = mybir.AxisListType.X

P = 128
DEPTH = 2
D = 1024
SEQ = 512
NSEQ = 2
T = NSEQ * SEQ
KT = D // P
TT = T // P
SB = SEQ // P
HD = 64
EPS = 1e-6
GRID_W = 64
ROPE_THETA = 10000.0
AH, KVH = 8, 2
NQK = AH + KVH
N_ATT = NSEQ * AH * SB
GH = MH = 4
GLA_TAU = 16.0
DFF = 2816
FT = DFF // P
CH = 32
NCH = SEQ // CH
UNIT = KT * P

AQ, AK, AV = 0, 512, 640
BQ, BK, BV, BG, BA = 768, 1024, 1280, 1536, 1792
CQ, CK, CV, CO, CG = 1824, 2080, 2336, 2592, 2848

TOK_COLS = [AQ, AQ + 256, AK, BV, BG, CV, CO]
FEAT_COLS = [CQ, CQ + 128, CK, CK + 128, BQ, BQ + 128, BK, BK + 128]
N_TOK = 2 * len(TOK_COLS)
N_IN = N_TOK + len(FEAT_COLS) + 1
N_OUT = KT
N_UNITS = N_IN + N_OUT
RAW, SPLIT = 3, 4
E_TOK = len(TOK_COLS) * TT
C_ROT = 4
E_ALL = E_TOK + 2 * (N_IN - N_TOK)

BA_ROW = (4, 36)
GROWS = 36

V_MIX, V_FFN, V_GLAN, V_MLN, V_GB, V_GBI, V_GBF = 0, 8, 16, 17, 18, 22, 23
NVEC = 24


def build(nc, x_in, w_units, w_ffn, vecs, w2p, qkg, convp, rope, gmask, chunkmask, lmask, sel,
          ident_in, x_out):
    ctx = ExitStack()
    with ctx:
        def fixed(name, shape, dt=F32):
            return ctx.enter_context(nc.sbuf_tensor(name, shape, dt))

        def region(size, specs):
            assert sum(int(np.prod(shape[1:])) * 4 + 31 & ~31 for _, shape, _ in specs) <= size, specs[0][0]
            with ExitStack() as phase:
                return [phase.enter_context(nc.sbuf_tensor(n, s, d)) for n, s, d in specs]

        W_BYTES = 2 * SPLIT * UNIT * 4
        H_BYTES = 2 * KT * T * 4
        Q_BYTES = 4 * (2 * 4 * T + TT * (768 + 3 * 256 + MH * (HD + 1)) + T)
        ident = fixed("ident", [P, P])
        ones = fixed("ones", [P, P])
        eps = fixed("eps", [P, 1])
        vec = fixed("vec", [P, NVEC])
        raw = fixed("raw", [P, RAW, UNIT])

        with ExitStack() as w_region:
            whi = w_region.enter_context(nc.sbuf_tensor("whi", [P, SPLIT, KT, P], F32R))
            wlo = w_region.enter_context(nc.sbuf_tensor("wlo", [P, SPLIT, KT, P], F32R))
        st, oacc, ktok = region(W_BYTES, [
            ("states", [P, NCH, NSEQ, 2, HD], F32), ("oacc", [P, TT, 256], F32), ("ktok", [P, TT, 256], F32)])
        qd, kd = region(W_BYTES, [
            ("qd", [P, 2, AH, 2, HD], F32R), ("kd", [P, 2, 2, KVH, 2, HD], F32R)])
        Dt1, qh2, ql2, ks2 = region(W_BYTES, [
            ("Dt1", [P, 2, SB, SEQ], F32), ("qh2", [P, 2, SEQ], F32R), ("ql2", [P, 2, SEQ], F32R),
            ("ks2", [P, 2, SEQ], F32R)])
        w_hold = ctx.enter_context(nc.sbuf_tensor("w_region", [P, W_BYTES // 4], F32))

        hh, hl = region(H_BYTES, [("hh", [P, KT, T], F32R), ("hl", [P, KT, T], F32R)])
        (qs, ks, prob, pT, nmx, rsum, rinvp) = region(H_BYTES, [
            ("qs", [P, AH, T], F32R), ("ks", [P, 2, KVH, T], F32R),
            ("prob", [P, 3, SEQ], F32), ("pT", [P, 2, SB, P], F32),
            ("nmx", [P, 64], F32), ("rsum", [P, 64], F32), ("rinvp", [P, 64], F32)])
        (G, gx, dml, qhat, khat, qtil, ktil, attT, gam, cmask, aL, w2s, gss,
         gtmp) = region(H_BYTES, [
            ("G", [P, 2, T], F32), ("gx", [P, 2, T], F32), ("dml", [P, T], F32),
            ("qhat", [P, 2, T], F32), ("khat", [P, 2, T], F32), ("qtil", [P, 2, T], F32),
            ("ktil", [P, T], F32), ("attT", [P, 2, 2, 2, P], F32),
            ("gam", [P, 2, P], U32), ("cmask", [P, SEQ], F32), ("aL", [P, 2, NSEQ * NCH], F32),
            ("w2s", [P, 2, 256], F32), ("gss", [P, 2, TT * GH], F32), ("gtmp", [P, 256], F32)])
        ee = ktil[:].rearrange("p (a t) -> p a t", a=2)
        (yf, ri, fl, Fc, mm_rows, Rh, Rl, zr, selr, mmask, CT, EM, mR, Dt0, rc, dn, t12, hs,
         mss) = region(H_BYTES, [
            ("yf", [GROWS, T], F32), ("ri", [GROWS, T], F32),
            ("fl", [GROWS, T], F32), ("Fc", [GROWS, T], F32), ("mm_rows", [GROWS, T], F32),
            ("Rh", [GROWS, T], F32R), ("Rl", [GROWS, T], F32R), ("zr", [GROWS, SEQ], F32),
            ("selr", [GROWS, 2 * MH, P], F32R), ("mmask", [P, 2, P], F32),
            ("CT", [P, TT, GROWS], F32), ("EM", [P, TT, GROWS], F32),
            ("mR", [P, 2, SEQ], F32), ("Dt0", [P, 2, SB, SEQ], F32),
            ("rc", [P, 2, SB], F32), ("dn", [P, 2, SB], F32), ("t12", [P, 2, SB, HD], F32),
            ("hs", [P, SB, HD], F32), ("mss", [P, 2, TT * MH], F32)])
        Rr, Cr = yf, ri
        sels = mR[0:GROWS, :, :].rearrange("p a (b c) -> p (a b) c", c=P)
        h_hold = ctx.enter_context(nc.sbuf_tensor("h_region", [P, H_BYTES // 4], F32))

        (qkM, qkG, tokA, gv, gg, vaug, co, small) = region(Q_BYTES, [
            ("qkM", [P, 4, T], F32), ("qkG", [P, 4, T], F32), ("tokA", [P, TT, 768], F32),
            ("gv", [P, TT, 256], F32), ("gg", [P, TT, 256], F32),
            ("vaug", [P, TT, MH, HD + 1], F32), ("co", [P, TT, 256], F32),
            ("small", [P, T], F32)])
        (ropec, ropes, tabc, tabs, t1, t2, qkgain, ssq, rqk) = region(4 * KT * T, [
            ("ropec", [P, SB, HD], F32), ("ropes", [P, SB, HD], F32),
            ("tabc", [P, SB, NQK, HD], F32), ("tabs", [P, SB, NQK, HD], F32),
            ("t1", [P, NQK * HD], F32), ("t2", [P, NQK * HD], F32), ("qkgain", [P, 2, HD], F32),
            ("ssq", [P, TT, NQK], F32), ("rqk", [P, TT, NQK], F32)])
        (x, sq, hf, rms, rinv, accg, accv, sil, acth, actl, convs, cw) = region(Q_BYTES, [
            ("x", [P, KT, T], F32), ("sq", [P, 4, SEQ], F32), ("hf", [P, 2, SEQ], F32),
            ("rms", [P, NSEQ, SEQ], F32), ("rinv", [P, NSEQ, SEQ], F32),
            ("accg", [P, NSEQ, SEQ], F32), ("accv", [P, NSEQ, SEQ], F32),
            ("sil", [P, NSEQ, SEQ], F32), ("acth", [P, NSEQ, SEQ], F32R),
            ("actl", [P, NSEQ, SEQ], F32R), ("convs", [P, FT, 8], F32), ("cw", [P, 8], F32)])
        q_hold = ctx.enter_context(nc.sbuf_tensor("q_region", [P, Q_BYTES // 4], F32))

        ps = ctx.enter_context(nc.psum_tensor("ps", [P, 8, 512], F32))
        x_spill = nc.dram_tensor("x_spill", [P, KT * T], F32, kind="Internal").ap()

        def sem(name):
            return ctx.enter_context(nc.semaphore(name))

        per_layer = []

        def lsem(name):
            s = sem(name)
            per_layer.append(s)
            return s

        x_loaded, consts_loaded, ones_set = sem("x_loaded"), sem("consts_loaded"), sem("ones_set")
        layer_end, layer_go, out_done = lsem("layer_end"), sem("layer_go"), sem("out_done")
        vec_loaded, spilled, reloaded = lsem("vec_loaded"), lsem("spilled"), lsem("reloaded")
        act_chain, dve_chain = lsem("act_chain"), lsem("dve_chain")
        sq_ready, sq_used = lsem("sq_ready"), lsem("sq_used")
        rms_ready, hf_ready = lsem("rms_ready"), lsem("hf_ready")
        hh_ready, h_ready = lsem("hh_ready"), lsem("h_ready")
        raw_full = [lsem(f"raw_full{i}") for i in range(RAW)]
        hi_ready, lo_ready, unit_used = lsem("hi_ready"), lsem("lo_ready"), lsem("unit_used")
        proj_ready, act_evac, dve_evac = lsem("proj_ready"), lsem("act_evac"), lsem("dve_evac")
        att_consts = lsem("att_consts")
        qk_sums, qk_rms, rot_ready = lsem("qk_sums"), lsem("qk_rms"), lsem("rot_ready")
        qk_hi, qk_lo, qkT_psum = lsem("qk_hi"), lsem("qk_lo"), lsem("qkT_psum")
        qkT_act, qkT_dve = lsem("qkT_act"), lsem("qkT_dve")
        sc_ready, nmx_ready, prob_ready = lsem("sc_ready"), lsem("nmx_ready"), lsem("prob_ready")
        pT_psum, pT_even, pT_odd = lsem("pT_psum"), lsem("pT_even"), lsem("pT_odd")
        ao_psum, ao_done = lsem("ao_psum"), lsem("ao_done")
        gla_consts, z_psum, ln_ready = lsem("gla_consts"), lsem("z_psum"), lsem("ln_ready")
        la_ready, cum_ready, dml_ready = lsem("la_ready"), lsem("cum_ready"), lsem("dml_ready")
        gx_ready, gx_used = lsem("gx_ready"), lsem("gx_used")
        ktil_psum, ktok_ready, aL_ready = lsem("ktil_psum"), lsem("ktok_ready"), lsem("aL_ready")
        kv_psum, state_ready = lsem("kv_psum"), lsem("state_ready")
        gat_psum, gat_ready = lsem("gat_psum"), lsem("gat_ready")
        go_psum, go_evac = lsem("go_psum"), lsem("go_evac")
        gsq_ready, gss_ready, grms_ready = lsem("gsq_ready"), lsem("gss_ready"), lsem("grms_ready")
        gsig_ready, gla_done = lsem("gsig_ready"), lsem("gla_done")
        ml_consts, yf_ready, fl_ready = lsem("ml_consts"), lsem("yf_ready"), lsem("fl_ready")
        rc_ready, ct_psum, ct_ready = lsem("rc_ready"), lsem("ct_psum"), lsem("ct_ready")
        qk_psum, rb_psum, mr_ready = lsem("qk_psum"), lsem("rb_psum"), lsem("mr_ready")
        dt_ready, wt_ready, num_psum = lsem("dt_ready"), lsem("wt_ready"), lsem("num_psum")
        sel_ready, R_split = lsem("sel_ready"), lsem("R_split")
        R_hi = lsem("R_hi")
        stk_hi, stk_lo = lsem("stk_hi"), lsem("stk_lo")
        heads_gated, ml_evac = lsem("heads_gated"), lsem("ml_evac")
        msq_ready, mss_ready, mrms_ready = lsem("msq_ready"), lsem("mss_ready"), lsem("mrms_ready")
        msig_ready, ml_done = lsem("msig_ready"), lsem("ml_done")
        mix_psum, mixh_ready, mixl_ready = lsem("mix_psum"), lsem("mixh_ready"), lsem("mixl_ready")
        wo_psum, wo_done = lsem("wo_psum"), lsem("wo_done")
        f_full = [lsem(f"f_full_{k}") for k in "gvd"]
        f_hi = [lsem(f"f_hi_{k}") for k in "gvd"]
        f_lo = [lsem(f"f_lo_{k}") for k in "gvd"]
        f_used = [lsem(f"f_used_{k}") for k in "gvd"]
        conv_loaded, cw_ready = lsem("conv_loaded"), lsem("cw_ready")
        g_init, v_init = lsem("g_init"), lsem("v_init")
        g_half, v_half = lsem("g_half"), lsem("v_half")
        g_conv, v_conv = lsem("g_conv"), lsem("v_conv")
        sil_ready, act_ready = lsem("sil_ready"), lsem("act_ready")
        acth_ready, actl_ready = lsem("acth_ready"), lsem("actl_ready")
        d_psum, d_done = lsem("d_psum"), lsem("d_done")

        def evac_target(e):
            if e < E_TOK:
                c, tt = divmod(e, TT)
                col = TOK_COLS[c]
                if col < BQ:
                    return tokA[:, tt, col:col + 256], 256
                if col == CV:
                    return vaug[:, tt, :, 0:HD], 256
                return {BV: gv, BG: gg, CO: co}[col][:, tt, :], 256
            f, s = divmod(e - E_TOK, NSEQ)
            cols = slice(s * SEQ, (s + 1) * SEQ)
            if f < 4:
                return qkM[:, f, cols], SEQ
            if f < 8:
                return qkG[:, f - 4, cols], SEQ
            return small[:, cols], SEQ

        def evac_source(e):
            dst, n = evac_target(e)
            src = ps[:, e % 8, 0:n]
            if e < E_TOK and TOK_COLS[e // TT] == CV:
                src = src.rearrange("p (h d) -> p h d", h=MH)
            return dst, src

        N_ML = NSEQ * MH
        Dts = (Dt0, Dt1)

        def head_rows(w):
            s, h = w // MH, w % MH
            return s, h, slice(s * SEQ, (s + 1) * SEQ), slice(h % 2 * HD, (h % 2 + 1) * HD),\
                slice((1 - h % 2) * HD, (2 - h % 2) * HD)

        def fwd_or_bwd_range(d, i):
            return (i * P, SEQ) if d == 0 else (0, (i + 1) * P)

        def step_of(d, ci):
            return ci if d == 0 else NCH - 1 - ci

        block = ctx.enter_context(nc.Block())

        @block.sync
        def _(sp):
            for k in range(KT):
                sp.dma_start(x[:, k, :], x_in[:, k, :]).then_inc(x_loaded, 16)
            sp.dma_start(ident[:], ident_in).then_inc(consts_loaded, 16)
            sp.wait_ge(x_loaded, 16 * KT)
            with sp.Fori(0, DEPTH) as l:
                sp.dma_start(vec[:], vecs[l]).then_inc(vec_loaded, 16)

                def load_unit(n):
                    if n >= RAW:
                        sp.wait_ge(lo_ready, n - RAW + 1)
                    sp.dma_start(raw[:, n % RAW, :], w_units[l, n]).then_inc(raw_full[n % RAW], 16)

                load_unit(0)
                load_unit(1)
                sp.dma_start(x_spill, x[:].rearrange("p k t -> p (k t)")).then_inc(spilled, 16)
                for n in range(2, 6):
                    load_unit(n)
                sp.wait_ge(spilled, 16)
                sp.wait_ge(h_ready, NSEQ * KT)
                sp.dma_start(ropec[:], rope[0]).then_inc(att_consts, 16)
                sp.dma_start(ropes[:], rope[1]).then_inc(att_consts, 16)
                sp.dma_start(qkgain[:], qkg[l]).then_inc(att_consts, 16)
                for n in range(6, N_IN + RAW):
                    load_unit(n)
                sp.wait_ge(ao_done, N_ATT)
                sp.dma_start(gam[:], gmask).then_inc(gla_consts, 16)
                sp.dma_start(cmask[:], chunkmask).then_inc(gla_consts, 16)
                sp.dma_start(w2s[:], w2p[l]).then_inc(gla_consts, 16)
                sp.wait_ge(gla_done, 1)
                sp.dma_start(sels[:], sel).then_inc(ml_consts, 16)
                sp.dma_start(mmask[:], lmask).then_inc(ml_consts, 16)
                sp.wait_ge(ml_done, 1)
                sp.wait_ge(spilled, 16)
                sp.dma_start(x[:].rearrange("p k t -> p (k t)"), x_spill).then_inc(reloaded, 16)
                for n in range(N_IN + RAW, N_UNITS):
                    load_unit(n)

                sp.wait_ge(mix_psum, 2 * TT)
                sp.dma_start(convs[:], convp[l]).then_inc(conv_loaded, 16)

                def load_ffn(j):
                    for kind in range(3):
                        if isinstance(j, int) and j == 0:
                            sp.wait_ge(lo_ready, N_UNITS)
                        else:
                            sp.wait_ge(f_lo[kind], j)
                        sp.dma_start(raw[:, kind, :], w_ffn[l, j, kind]).then_inc(f_full[kind], 16)

                load_ffn(0)
                with sp.Fori(1, FT) as j:
                    load_ffn(j)
                sp.wait_ge(d_done, FT * KT)
                sp.wait_ge(layer_end, 3)
                for s in per_layer:
                    sp.sem_clear(s)
                sp.sem_inc(layer_go, 1)
            sp.dma_start(x_out, x[:]).then_inc(out_done, 16)
            sp.wait_ge(out_done, 16)

        @block.tensor
        def _(pe):
            pe.wait_ge(consts_loaded, 16)
            pe.wait_ge(ones_set, 2)
            with pe.Fori(0, DEPTH) as l:
                def norm_sums(n):
                    for s in range(NSEQ):
                        for k in range(KT):
                            i = (n * NSEQ + s) * KT + k
                            pe.wait_ge(sq_ready, i + 1)
                            pe.matmul(ps[:, s, :], ones[:], sq[:, i % 4, :], start=(k == 0),
                                      stop=(k == KT - 1)).then_inc(sq_used, 1)

                def passes3(out, stat, mov, first, last):
                    pe.matmul(out, stat[1], mov[0], start=first, stop=False)
                    pe.matmul(out, stat[0], mov[1], start=False, stop=False)
                    return pe.matmul(out, stat[0], mov[0], start=False, stop=last)

                norm_sums(0)

                def bank_free(e):
                    if e >= 8:
                        pe.wait_ge((act_evac, dve_evac)[e % 2], e // 2 - 3)

                for c in range(len(TOK_COLS)):
                    pe.wait_ge(lo_ready, 2 * c + 2)
                    slot = 2 * c % SPLIT
                    for tt in range(TT):
                        e = c * TT + tt
                        bank_free(e)
                        if c == 0 and tt == 0:
                            pe.wait_ge(rms_ready, 2)
                        for k in range(KT):
                            if c == 0 and tt % SB == 0:
                                pe.wait_ge(h_ready, tt // SB * KT + k + 1)
                            tok = slice(tt * P, (tt + 1) * P)
                            mm3 = passes3(ps[:, e % 8, 0:256], (hh[:, k, tok], hl[:, k, tok]),
                                          (whi[:, slot:slot + 2, k, :], wlo[:, slot:slot + 2, k, :]),
                                          k == 0, k == KT - 1)
                        mm3.then_inc(proj_ready, 1)
                        if tt == TT - 1:
                            pe.wait_ge(proj_ready, e + 1)
                            pe.sem_inc(unit_used, 2)

                for u in range(N_TOK, N_IN):
                    pe.wait_ge(lo_ready, u + 1)
                    for s in range(NSEQ):
                        e = E_TOK + 2 * (u - N_TOK) + s
                        bank_free(e)
                        tok = slice(s * SEQ, (s + 1) * SEQ)
                        for k in range(KT):
                            mm3 = passes3(ps[:, e % 8, :], (whi[:, u % SPLIT, k, :], wlo[:, u % SPLIT, k, :]),
                                          (hh[:, k, tok], hl[:, k, tok]), k == 0, k == KT - 1)
                        mm3.then_inc(proj_ready, 1)
                    pe.wait_ge(proj_ready, e + 1)
                    pe.sem_inc(unit_used, 1)

                pe.wait_ge(act_evac, E_ALL // 2)
                pe.wait_ge(dve_evac, E_ALL // 2)
                for tt in range(TT):
                    pe.wait_ge(qk_lo, 2 * tt + 2)
                    if tt >= 2:
                        pe.wait_ge(qkT_act, 2 * (tt - 1))
                        pe.wait_ge(qkT_dve, tt - 1)
                    for b in range(3):
                        for i in range(4):
                            src = (qd[:, tt % 2, 4 * b + i, :, :] if b < 2 else kd[:, tt % 2, i // 2, i % 2, :, :])
                            tr = pe.transpose(ps[:, tt % 2 * 3 + b, i * P:(i + 1) * P],
                                              src.rearrange("p r d -> p (r d)").bitcast(F32), ident[:])
                        tr.then_inc(qkT_psum, 1)
                for i in range(N_ATT + 3):
                    if i < N_ATT:
                        s, h, qt = i // (AH * SB), i // SB % AH, i % SB
                        if i == 0:
                            pe.wait_ge(qkT_act, 2 * TT)
                            pe.wait_ge(qkT_dve, TT)
                        if i >= 3:
                            pe.wait_ge(prob_ready, i - 2)
                        q = qs[:, h, s * SEQ + qt * P:s * SEQ + (qt + 1) * P]
                        keys = slice(s * SEQ, (s + 1) * SEQ)
                        pe.matmul(ps[:, 3 + i % 3, :], q, ks[:, 1, h // 4, keys], start=True, stop=False)
                        pe.matmul(ps[:, 3 + i % 3, :], q, ks[:, 0, h // 4, keys], start=False,
                                  stop=True).then_inc(sc_ready, 1)
                    if 2 <= i < N_ATT + 2:
                        v = i - 2
                        pe.wait_ge(prob_ready, v + 1)
                        if v >= 2:
                            pe.wait_ge((pT_even, pT_odd)[v % 2], v // 2)
                        for kt in range(SB):
                            tr = pe.transpose(ps[:, 6 + v % 2, kt * P:(kt + 1) * P],
                                              prob[:, v % 3, kt * P:(kt + 1) * P], ident[:])
                        tr.then_inc(pT_psum, 1)
                    if i >= 3:
                        v = i - 3
                        s, h = v // (AH * SB), v // SB % AH
                        pe.wait_ge((pT_even, pT_odd)[v % 2], v // 2 + 1)
                        if v >= 3:
                            pe.wait_ge(ao_done, v - 2)
                        c0 = AV + h // 4 * HD
                        for kt in range(SB):
                            mm = pe.matmul(ps[:, v % 3, 0:HD], pT[:, v % 2, kt, :],
                                           tokA[:, s * SB + kt, c0:c0 + HD], start=(kt == 0), stop=(kt == SB - 1))
                        mm.then_inc(ao_psum, 1)

                pe.wait_ge(ao_done, N_ATT)
                pe.wait_ge(gla_consts, 48)
                for d in range(2):
                    if d == 1:
                        pe.wait_ge(go_evac, TT)
                    for j in range(4):
                        pe.matmul(ps[:, j, :], w2s[:, d, j // 2 * P:(j // 2 + 1) * P],
                                  small[:, j % 2 * SEQ:(j % 2 + 1) * SEQ], start=True,
                                  stop=True).then_inc(z_psum, 1)
                    for ht in range(2):
                        pe.wait_ge(gx_used, (d * 2 + ht) * 4 + 4)
                        for b in range(2):
                            r = (d * 2 + ht) * 2 + b
                            if r >= 2:
                                pe.wait_ge(ktok_ready, r - 1)
                            for i in range(4):
                                tt = b * 4 + i
                                tr = pe.transpose(ps[:, 4 + b, i * P:(i + 1) * P],
                                                  ktil[:, tt * P:(tt + 1) * P], ident[:])
                            tr.then_inc(ktil_psum, 1)
                    pe.wait_ge(ktok_ready, d * 4 + 4)
                    for c in range(NCH - 1):
                        ci = step_of(d, c)
                        n = d * (NCH - 1) + c
                        if n >= 2:
                            pe.wait_ge(state_ready, n - 1)
                        rows = slice(ci % 4 * CH, (ci % 4 + 1) * CH)
                        for s in range(NSEQ):
                            tt = s * SB + ci // 4
                            for h in range(GH):
                                half = slice(h % 2 * HD, (h % 2 + 1) * HD)
                                c0 = (s * 2 + h // 2) * HD
                                mm = pe.matmul(ps[half, 6 + n % 2, c0:c0 + HD],
                                               ktok[rows, tt, h * HD:(h + 1) * HD],
                                               gv[rows, tt, h * HD:(h + 1) * HD], start=True, stop=True)
                        mm.then_inc(kv_psum, 1)

                    def scores(tt):
                        n = d * TT + tt
                        if tt >= 2:
                            pe.wait_ge(gat_ready, n - 1)
                        tok = slice(tt * P, (tt + 1) * P)
                        for h in range(GH):
                            half = slice(h % 2 * HD, (h % 2 + 1) * HD)
                            mm = pe.matmul(ps[:, tt % 2 * 4 + h % 2, h // 2 * P:(h // 2 + 1) * P], khat[half, h // 2, tok],
                                           qhat[half, h // 2, tok], start=True, stop=True)
                        mm.then_inc(gat_psum, 1)

                    scores(0)
                    pe.wait_ge(state_ready, (d + 1) * (NCH - 1))
                    for tt in range(TT):
                        if tt + 1 < TT:
                            scores(tt + 1)
                        n = d * TT + tt
                        pe.wait_ge(gat_ready, n + 1)
                        if tt >= 2:
                            pe.wait_ge(go_evac, n - 1)
                        s = tt // SB
                        for h in range(GH):
                            half = slice(h % 2 * HD, (h % 2 + 1) * HD)
                            bank, cols = 2 + tt % 2 * 4 + h % 2, slice(h // 2 * HD, (h // 2 + 1) * HD)
                            mm = pe.matmul(ps[:, bank, cols], attT[:, tt % 2, h % 2, h // 2, :],
                                           gv[:, tt, h * HD:(h + 1) * HD],
                                           start=True, stop=False, skip_group_check=True)
                            for r in range(4):
                                c = step_of(d, tt % SB * 4 + r)
                                t0 = tt * P + r * CH
                                mm = pe.matmul(ps[r * CH:(r + 1) * CH, bank, cols],
                                               qtil[half, h // 2, t0:t0 + CH], st[half, c, s, h // 2, :],
                                               start=False, stop=True, skip_group_check=True)
                        mm.then_inc(go_psum, 1)

                pe.wait_ge(gla_done, 1)
                pe.wait_ge(ml_consts, 32)
                pe.wait_ge(rc_ready, 1)
                for i, src in enumerate((Cr, mm_rows)):
                    for tt in range(TT):
                        tr = pe.transpose(ps[:, i, tt * GROWS:(tt + 1) * GROWS],
                                          src[:, tt * P:(tt + 1) * P], ident[0:GROWS, 0:GROWS])
                    tr.then_inc(ct_psum, 1)
                pe.wait_ge(ct_ready, 2)
                pe.wait_ge(sel_ready, 1)
                pe.wait_ge(R_split, 1)

                def row_terms(w):
                    s, h, tok, _, _ = head_rows(w)
                    for d in range(2):
                        if w >= 1:
                            pe.wait_ge(dt_ready, 2 * SB * w)
                        pe.matmul(ps[:, 4 + d, :], selr[:, d * MH + h, :], Rl[:, tok], start=True, stop=False)
                        pe.matmul(ps[:, 4 + d, :], selr[:, d * MH + h, :], Rh[:, tok], start=False,
                                  stop=True).then_inc(rb_psum, 1)

                def key_query(w):
                    pe.wait_ge(stk_lo, 3 * (w + 1))
                    for i in range(SB):
                        if w >= 1:
                            pe.wait_ge(wt_ready, 2 * SB * (w - 1) + 2 * i + 2)
                        k = ks2[:, w % 2, i * P:(i + 1) * P]
                        pe.matmul(ps[:, i, :], k, ql2[:, w % 2, :], start=True, stop=False)
                        pe.matmul(ps[:, i, :], k, qh2[:, w % 2, :], start=False, stop=True).then_inc(qk_psum, 1)

                row_terms(0)
                key_query(0)
                for w in range(N_ML):
                    s, h = w // MH, w % MH
                    if w + 1 < N_ML:
                        row_terms(w + 1)
                        key_query(w + 1)
                    if w >= 1:
                        pe.wait_ge(ml_evac, w)
                    pe.wait_ge(wt_ready, 2 * SB * (w + 1))
                    for d in range(2):
                        for j in range(SB):
                            keys = range(j + 1) if d == 0 else range(j, SB)
                            for i in keys:
                                mm = pe.matmul(ps[:, 6 + d, j * (HD + 1):(j + 1) * (HD + 1)],
                                               Dts[w % 2][:, d, i, j * P:(j + 1) * P], vaug[:, s * SB + i, h, :],
                                               start=(i == keys[0]), stop=(i == keys[-1]))
                    mm.then_inc(num_psum, 1)

                pe.wait_ge(ml_done, 1)
                for tt in range(TT):
                    for b in range(2):
                        if tt >= 4:
                            pe.wait_ge(mixl_ready, 3 * (tt - 4) + 1 + 2 * b)
                        for i in range(4):
                            src = (tokA[:, tt, i * P:(i + 1) * P] if b == 0 else
                                   (gg, co)[i // 2][:, tt, i % 2 * P:(i % 2 + 1) * P])
                            tr = pe.transpose(ps[:, tt % 4 * 2 + b, i * P:(i + 1) * P], src, ident[:])
                        tr.then_inc(mix_psum, 1)
                pe.wait_ge(mixl_ready, 3 * TT)
                for o in range(KT):
                    u = N_IN + o
                    pe.wait_ge(lo_ready, u + 1)
                    if o >= 4:
                        pe.wait_ge(wo_done, o - 3)
                    for s in range(NSEQ):
                        tok = slice(s * SEQ, (s + 1) * SEQ)
                        for k in range(KT):
                            mm3 = passes3(ps[:, o % 4 * 2 + s, :], (whi[:, u % SPLIT, k, :], wlo[:, u % SPLIT, k, :]),
                                          (hh[:, k, tok], hl[:, k, tok]), k == 0, k == KT - 1)
                    mm3.then_inc(wo_psum, 1)
                    pe.wait_ge(wo_psum, o + 1)
                    pe.sem_inc(unit_used, 1)

                pe.wait_ge(wo_done, KT)
                norm_sums(1)
                pe.wait_ge(h_ready, 4 * KT)

                def up(kind, j):
                    pe.wait_ge(f_lo[kind], j + 1)
                    for s in range(NSEQ):
                        for k in range(KT):
                            mm3 = passes3(ps[:, 2 * kind + s, :], (whi[:, kind, k, :], wlo[:, kind, k, :]),
                                          (hh[:, k, s * SEQ:(s + 1) * SEQ], hl[:, k, s * SEQ:(s + 1) * SEQ]),
                                          k == 0, k == KT - 1)
                    mm3.then_inc(f_used[kind], 1)

                def down(j, first=False, last=False):
                    pe.wait_ge(f_lo[2], j + 1)
                    pe.wait_ge(actl_ready, j + 1)
                    for o in range(KT):
                        if not (first and o < 2):
                            pe.wait_ge(d_done, j * KT + o - 1)
                        for s in range(NSEQ):
                            mm3 = passes3(ps[:, 4 + o % 2 * 2 + s, :], (whi[:, 2, o, :], wlo[:, 2, o, :]),
                                          (acth[:, s, :], actl[:, s, :]), True, True)
                        mm3.then_inc(d_psum, 1)
                    pe.wait_ge(d_psum, (j + 1) * KT)
                    pe.sem_inc(f_used[2], 1)

                up(0, 0)
                up(1, 0)

                def iteration(j, first=False):
                    pe.wait_ge(g_conv, j)
                    up(0, j)
                    pe.wait_ge(v_conv, j)
                    up(1, j)
                    down(j - 1, first=first)

                iteration(1, first=True)
                with pe.Fori(2, FT) as j:
                    iteration(j)
                down(FT - 1)
                pe.sem_inc(layer_end, 1)
                pe.wait_ge(layer_go, l + 1)

        @block.scalar
        def _(act):
            act.wait_ge(x_loaded, 16 * KT)
            act.wait_ge(ones_set, 2)
            with act.Fori(0, DEPTH) as l:
                chain = [0]

                def link(ins):
                    chain[0] += 1
                    ins.then_inc(act_chain, 1)
                    act.wait_ge(act_chain, chain[0])

                def split_hi(n):
                    act.wait_ge(raw_full[n % RAW], 16 * (n // RAW + 1))
                    if n >= SPLIT:
                        act.wait_ge(unit_used, n - SPLIT + 1)
                    act.activation(whi[:, n % SPLIT, :, :], raw[:, n % RAW, :].rearrange("p (k c) -> p k c", k=KT),
                                   ACT.Copy).then_inc(hi_ready, 1)

                def norm(n):
                    for s in range(NSEQ):
                        tok = slice(s * SEQ, (s + 1) * SEQ)
                        for k in range(KT):
                            i = (n * NSEQ + s) * KT + k
                            if i >= 4:
                                act.wait_ge(sq_used, i - 3)
                            act.activation(sq[:, i % 4, :], x[:, k, tok], ACT.Square).then_inc(sq_ready, 1)
                    for s in range(NSEQ):
                        act.wait_ge(sq_used, (n * NSEQ + s + 1) * KT)
                        act.activation(rms[:, s, :], ps[:, s, :], ACT.Sqrt, bias=eps[:], scale=1.0 / D)\
                           .then_inc(rms_ready, 1)
                    for s in range(NSEQ):
                        for k in range(KT):
                            i = (n * NSEQ + s) * KT + k
                            act.wait_ge(hf_ready, i + 1)
                            act.activation(hh[:, k, s * SEQ:(s + 1) * SEQ], hf[:, i % 2, :], ACT.Copy)\
                               .then_inc(hh_ready, 1)

                split_hi(0)
                split_hi(1)
                norm(0)
                split_hi(2)
                split_hi(3)
                act.wait_ge(h_ready, NSEQ * KT)

                def evacuate(e):
                    if e == E_TOK:
                        act.wait_ge(rot_ready, TT)
                    act.wait_ge(proj_ready, e + 1)
                    dst, src = evac_source(e)
                    act.activation(dst, src, ACT.Copy).then_inc(act_evac, 1)

                for c in range(len(TOK_COLS)):
                    if c >= 1:
                        for u in (2 * c + 2, 2 * c + 3):
                            split_hi(u)
                    for e in range(c * TT, (c + 1) * TT, 2):
                        evacuate(e)
                        if e == C_ROT * TT:
                            act.wait_ge(qk_sums, 1)
                            act.activation(rqk[:], ssq[:], ACT.Sqrt, bias=eps[:], scale=1.0 / HD)\
                               .then_inc(qk_rms, 1)
                for u in range(N_TOK, N_IN):
                    for v in ([u + 2, u + 3] if u == N_TOK else [u + 3]):
                        if v < N_IN:
                            split_hi(v)
                    evacuate(E_TOK + 2 * (u - N_TOK))

                act.wait_ge(act_evac, E_ALL // 2)
                act.wait_ge(dve_evac, E_ALL // 2)
                for tt in range(TT + 1):
                    if tt < TT:
                        if tt >= 2:
                            act.wait_ge(qkT_psum, 3 * (tt - 1))
                        act.activation(qd[:, tt % 2, :, 0, :], tokA[:, tt, 0:AH * HD].rearrange("p (h d) -> p h d", h=AH),
                                       ACT.Copy).then_inc(qk_hi, 1)
                        act.activation(kd[:, tt % 2, 0, :, :, :],
                                       tokA[:, tt, AK:AV].rearrange("p (g d) -> p g d", g=KVH).unsqueeze(2)
                                       .to_broadcast([P, KVH, 2, HD]), ACT.Copy).then_inc(qk_hi, 1)
                    if tt >= 1:
                        u = tt - 1
                        tok = slice(u * P, (u + 1) * P)
                        for b, dst in ((0, qs[:, 0:4, tok]), (2, ks[:, :, :, tok].rearrange("p r g t -> p (r g) t"))):
                            act.wait_ge(qkT_psum, 3 * u + b + 1)
                            act.activation(dst, ps[:, u % 2 * 3 + b, :].rearrange("p (h t) -> p h t", h=4),
                                           ACT.Copy).then_inc(qkT_act, 1)
                for i in range(N_ATT + 2):
                    if i < N_ATT:
                        act.wait_ge(nmx_ready, i + 1)
                        if i >= 3:
                            act.wait_ge(pT_psum, i - 2)
                        act.activation(prob[:, i % 3, :], ps[:, 3 + i % 3, :], ACT.Exp, bias=nmx[:, i:i + 1],
                                       accum_out=rsum[:, i:i + 1]).then_inc(prob_ready, 1)
                    v = i - 2
                    if v >= 0 and v % 2 == 1:
                        act.wait_ge(pT_psum, v + 1)
                        if v >= 2:
                            act.wait_ge(ao_psum, v - 1)
                        act.activation(pT[:, 1, :, :].rearrange("p k q -> p (k q)"), ps[:, 7, :], ACT.Copy)\
                           .then_inc(pT_odd, 1)

                act.wait_ge(ao_done, N_ATT)
                for d in range(2):
                    for j in range(4):
                        r = d * 4 + j
                        if r >= 2:
                            act.wait_ge(la_ready, r - 1)
                        act.wait_ge(z_psum, r + 1)
                        e = ee[:, j % 2, :]
                        link(act.activation(e, ps[:, j, :], ACT.Abs, bias=vec[:, V_GB + 2 * d + j // 2:V_GB + 2 * d + j // 2 + 1]))
                        link(act.activation(e, e, ACT.Exp, scale=-1.0))
                        act.activation(e, e, ACT.Ln, bias=ones[:, 0:1]).then_inc(ln_ready, 1)
                    act.wait_ge(cum_ready, 2 * d + 2)
                    for ht in range(2):
                        r = d * 2 + ht
                        for m, (src, sc) in enumerate(((dml[:], 1), (dml[:], -1), (G[:, ht, :], 1), (dml[:], 1))):
                            n = 4 * r + m
                            if m in (0, 1, 3):
                                act.wait_ge(dml_ready, 2 * r + (2 if m == 3 else 1))
                            if n >= 2:
                                act.wait_ge(gx_used, n - 1)
                            act.activation(gx[:, m % 2, :], src, ACT.Exp, scale=sc / GLA_TAU).then_inc(gx_ready, 1)
                        last = CH - 1 if d == 0 else 0
                        if d == 1 and ht == 0:
                            act.wait_ge(state_ready, NCH - 1)
                        act.activation(aL[:, ht, :], G[:, ht, :].rearrange("p (c t) -> p c t", t=CH)[:, :, last],
                                       ACT.Exp, scale=1.0 / GLA_TAU).then_inc(aL_ready, 1)
                        for b in range(2):
                            act.wait_ge(ktil_psum, 2 * r + b + 1)
                            if d == 1 and ht == 0 and b == 0:
                                act.wait_ge(kv_psum, NCH - 1)
                            act.activation(ktok[:, 4 * b:4 * b + 4, ht * P:(ht + 1) * P],
                                           ps[:, 4 + b, :].rearrange("p (i c) -> p i c", i=4), ACT.Copy)\
                               .then_inc(ktok_ready, 1)
                act.wait_ge(go_evac, 2 * TT)
                for hb in range(2):
                    act.activation(gx[:, hb, :].rearrange("p (t c) -> p t c", t=4), oacc[:, 4 * hb:4 * hb + 4, :],
                                   ACT.Square, scale=HD ** -0.5).then_inc(gsq_ready, 1)
                act.wait_ge(gss_ready, 2)
                act.activation(gss[:, 1, :], gss[:, 0, :], ACT.Sqrt, bias=eps[:], scale=1.0 / HD)\
                   .then_inc(grms_ready, 1)
                for hb in range(2):
                    act.activation(gx[:, hb, :].rearrange("p (t c) -> p t c", t=4), gg[:, 4 * hb:4 * hb + 4, :],
                                   ACT.Sigmoid).then_inc(gsig_ready, 1)

                act.activation(co[:], co[:], ACT.Sigmoid).then_inc(msig_ready, 1)
                act.wait_ge(yf_ready, 1)
                link(act.activation(fl[:], yf[:], ACT.Abs))
                link(act.activation(fl[:], fl[:], ACT.Exp, scale=-1.0))
                act.activation(fl[:], fl[:], ACT.Ln, bias=ones[0:GROWS, 0:1]).then_inc(fl_ready, 1)
                act.wait_ge(ml_consts, 32)
                act.activation(selr[:], sels, ACT.Copy).then_inc(sel_ready, 1)
                act.wait_ge(rc_ready, 1)
                act.activation(Rh[:], Rr[:], ACT.Copy).then_inc(R_hi, 1)

                def stack_hi(w):
                    s, h, tok, rows, other = head_rows(w)
                    if w >= 2:
                        act.wait_ge(qk_psum, SB * (w - 1))
                    q, k = qkM[rows, h // 2, tok], qkM[rows, 2 + h // 2, tok]
                    act.activation(qh2[rows, w % 2, :], q, ACT.Copy).then_inc(stk_hi, 1)
                    act.activation(ks2[rows, w % 2, :], k, ACT.Copy).then_inc(stk_hi, 1)
                    act.activation(qh2[other, w % 2, :], q, ACT.Copy).then_inc(stk_hi, 1)

                act.wait_ge(gla_done, 1)
                stack_hi(0)
                act.wait_ge(ct_psum, 1)
                act.activation(CT[:], ps[:, 0, 0:TT * GROWS].rearrange("p (t r) -> p t r", t=TT), ACT.Copy)\
                   .then_inc(ct_ready, 1)
                act.wait_ge(ct_psum, 2)
                act.activation(EM[:], ps[:, 1, 0:TT * GROWS].rearrange("p (t r) -> p t r", t=TT), ACT.Exp,
                               scale=-1.0).then_inc(ct_ready, 1)
                act.wait_ge(ct_ready, 2)
                for w in range(N_ML):
                    s, h = w // MH, w % MH
                    if w + 1 < N_ML:
                        stack_hi(w + 1)
                    if w >= 2:
                        act.wait_ge(num_psum, w - 1)
                    Dt = Dts[w % 2]
                    bias = lambda d, i: CT[:, s * SB + i, 32 * d + h:32 * d + h + 1]
                    for d in range(2):
                        act.wait_ge(mr_ready, 2 * w + d + 1)
                        for i in range(SB):
                            rest = slice((i + 1) * P, SEQ) if d == 0 else slice(0, i * P)
                            if rest.stop > rest.start:
                                act.activation(Dt[:, d, i, rest], ps[:, 4 + d, rest], ACT.Exp, bias=bias(d, i))
                    for i in range(SB):
                        for d in range(2):
                            own = slice(i * P, (i + 1) * P)
                            act.activation(Dt[:, d, i, own], mR[:, d, own], ACT.Exp, bias=bias(d, i))\
                               .then_inc(dt_ready, 1)
                act.wait_ge(heads_gated, 1)
                for hb in range(2):
                    sq_to = Dt0[:, hb, 0:2, :].rearrange("p a b -> p (a b)").rearrange("p (t c) -> p t c", t=4)
                    act.activation(sq_to, co[:, 4 * hb:4 * hb + 4, :], ACT.Square).then_inc(msq_ready, 1)
                act.wait_ge(mss_ready, 2)
                act.activation(mss[:, 1, :], mss[:, 0, :], ACT.Sqrt, bias=eps[:], scale=1.0 / HD)\
                   .then_inc(mrms_ready, 1)

                act.wait_ge(ml_done, 1)
                for u in range(N_IN, N_IN + SPLIT):
                    split_hi(u)
                for tt in range(TT):
                    tok = slice(tt * P, (tt + 1) * P)
                    bank = tt % 4 * 2
                    act.wait_ge(mix_psum, 2 * tt + 1)
                    act.activation(hh[:, 0:4, tok], ps[:, bank, :].rearrange("p (i t) -> p i t", i=4), ACT.Copy)\
                       .then_inc(mixh_ready, 1)
                    act.wait_ge(mix_psum, 2 * tt + 2)
                    for i, g in enumerate((V_GLAN, V_MLN)):
                        act.activation(hh[:, 4 + 2 * i:6 + 2 * i, tok],
                                       ps[:, bank + 1, 2 * i * P:(2 * i + 2) * P].rearrange("p (i t) -> p i t", i=2),
                                       ACT.Copy, scale=vec[:, g:g + 1]).then_inc(mixh_ready, 1)
                for u in range(N_IN + SPLIT, N_UNITS):
                    split_hi(u)

                act.wait_ge(wo_done, KT)

                def ffn_hi(kind, j):
                    act.wait_ge(f_full[kind], 16 * (j + 1))
                    act.activation(whi[:, kind, :, :], raw[:, kind, :].rearrange("p (k c) -> p k c", k=KT),
                                   ACT.Copy).then_inc(f_hi[kind], 1)

                act.wait_ge(unit_used, N_UNITS)
                for kind in (0, 1):
                    ffn_hi(kind, 0)
                norm(1)
                act.wait_ge(h_ready, 2 * NSEQ * KT)
                act.wait_ge(conv_loaded, 16)

                def iteration(j, first=False, last=False):
                    if not first:
                        act.wait_ge(v_conv, j)
                    act.activation(cw[:], convs[:, j, :], ACT.Copy).then_inc(cw_ready, 1)
                    act.wait_ge(cw_ready, j + 1)
                    act.wait_ge(f_used[0], j + 1)
                    act.activation(accg[:], ps[:, 0:2, :], ACT.Identity, bias=cw[:, 3:4], scale=cw[:, 1:2])\
                       .then_inc(g_init, 1)
                    if not last:
                        ffn_hi(0, j + 1)
                    if not first:
                        act.wait_ge(act_ready, j)
                    act.wait_ge(g_conv, j + 1)
                    act.activation(sil[:], accg[:], ACT.Silu).then_inc(sil_ready, 1)
                    act.wait_ge(f_used[1], j + 1)
                    if not first:
                        act.wait_ge(actl_ready, j)
                    act.activation(accv[:], ps[:, 2:4, :], ACT.Identity, bias=cw[:, 7:8], scale=cw[:, 5:6])\
                       .then_inc(v_init, 1)
                    if not last:
                        ffn_hi(1, j + 1)
                    if not first:
                        act.wait_ge(f_used[2], j)
                    ffn_hi(2, j)
                    act.wait_ge(act_ready, j + 1)
                    act.activation(acth[:], accv[:], ACT.Copy).then_inc(acth_ready, 1)
                    act.wait_ge(sil_ready, j + 1)

                iteration(0, first=True)
                with act.Fori(1, FT - 1) as j:
                    iteration(j)
                iteration(FT - 1, last=True)
                act.sem_inc(layer_end, 1)
                act.wait_ge(layer_go, l + 1)

        @block.vector
        def _(dve):
            dve.memset(ones[:], 1.0).then_inc(ones_set, 1)
            dve.memset(eps[:], EPS).then_inc(ones_set, 1)
            dve.wait_ge(ones_set, 2)
            dve.wait_ge(x_loaded, 16 * KT)
            with dve.Fori(0, DEPTH) as l:
                chain = [0]

                def link(ins):
                    chain[0] += 1
                    ins.then_inc(dve_chain, 1)
                    dve.wait_ge(dve_chain, chain[0])

                def split_lo(n):
                    dve.wait_ge(hi_ready, n + 1)
                    dve.tensor_tensor(wlo[:, n % SPLIT, :, :],
                                      raw[:, n % RAW, :].rearrange("p (k c) -> p k c", k=KT),
                                      whi[:, n % SPLIT, :, :].bitcast(F32), ALU.subtract).then_inc(lo_ready, 1)

                def norm(n, gain):
                    for s in range(NSEQ):
                        dve.wait_ge(rms_ready, n * NSEQ + s + 1)
                        link(dve.reciprocal(rinv[:, s, :], rms[:, s, :]))
                        tok = slice(s * SEQ, (s + 1) * SEQ)
                        for k in range(KT + 1):
                            i = (n * NSEQ + s) * KT + k
                            if k < KT:
                                if i >= 2:
                                    dve.wait_ge(h_ready, i - 1)
                                dve.scalar_tensor_tensor(hf[:, i % 2, :], x[:, k, tok], vec[:, gain + k:gain + k + 1],
                                                         rinv[:, s, :], ALU.mult, ALU.mult).then_inc(hf_ready, 1)
                            if k >= 1:
                                dve.wait_ge(hh_ready, i)
                                dve.tensor_tensor(hl[:, k - 1, tok], hf[:, (i - 1) % 2, :],
                                                  hh[:, k - 1, tok].bitcast(F32), ALU.subtract).then_inc(h_ready, 1)

                split_lo(0)
                split_lo(1)
                dve.wait_ge(vec_loaded, 16)
                norm(0, V_MIX)
                split_lo(2)
                split_lo(3)
                dve.wait_ge(h_ready, NSEQ * KT)
                link(dve.memset(vaug[:, :, :, HD:HD + 1], 1.0))

                def evacuate(e):
                    if e == E_TOK + 1:
                        dve.wait_ge(rot_ready, TT)
                    dve.wait_ge(proj_ready, e + 1)
                    dst, src = evac_source(e)
                    dve.tensor_copy(dst, src).then_inc(dve_evac, 1)

                def rotary_tables():
                    dve.wait_ge(att_consts, 48)
                    for tab, base in ((tabc, ropec), (tabs, ropes)):
                        for g, (h0, nh) in enumerate(((0, AH), (AH, KVH))):
                            shape = [P, SB, nh, HD]
                            link(dve.tensor_tensor(
                                tab[:, :, h0:h0 + nh, :],
                                base[:].unsqueeze(2).to_broadcast(shape),
                                qkgain[:, g:g + 1, :].unsqueeze(1).to_broadcast(shape), ALU.mult))

                def head_squares(tt):
                    qk = tokA[:, tt, 0:NQK * HD]
                    link(dve.tensor_tensor(t1[:], qk, qk, ALU.mult))
                    link(dve.tensor_reduce(ssq[:, tt, :], t1[:].rearrange("p (h d) -> p h d", h=NQK), AX_X, ALU.add))

                def head_rms():
                    dve.wait_ge(qk_rms, 1)
                    link(dve.reciprocal(rqk[:], rqk[:]))
                    link(dve.tensor_scalar(rqk[:, :, AH:NQK], rqk[:, :, AH:NQK], HD ** -0.5, None, ALU.mult))

                def rotate(tt):
                    qk = tokA[:, tt, 0:NQK * HD]
                    pairs = lambda t: t[:].rearrange("p (a r f) -> p a r f", r=2, f=HD // 4)
                    heads = "p (h d) -> p h d"
                    link(dve.tensor_tensor(t2[:], qk, tabs[:, tt % SB, :, :].rearrange("p h d -> p (h d)"), ALU.mult))
                    link(dve.tensor_tensor(t1[:], qk, tabc[:, tt % SB, :, :].rearrange("p h d -> p (h d)"), ALU.mult))
                    link(dve.tensor_tensor(pairs(t1), pairs(t1), pairs(t2)[:, :, ::-1, :], ALU.add))
                    dve.tensor_tensor(qk.rearrange(heads, h=NQK), t1[:].rearrange(heads, h=NQK),
                                      rqk[:, tt, :].unsqueeze(2).to_broadcast([P, NQK, HD]), ALU.mult)\
                       .then_inc(rot_ready, 1)
                    dve.wait_ge(rot_ready, tt + 1)

                for c in range(len(TOK_COLS)):
                    if c >= 1:
                        for u in (2 * c + 2, 2 * c + 3):
                            split_lo(u)
                    for i, e in enumerate(range(c * TT + 1, (c + 1) * TT, 2)):
                        evacuate(e)
                        if c == C_ROT - 2 and i == 1:
                            rotary_tables()
                        if c == C_ROT - 1:
                            if i == 0:
                                dve.wait_ge(act_evac, (C_ROT - 1) * TT // 2)
                                dve.wait_ge(dve_evac, (C_ROT - 1) * TT // 2)
                            for tt in (2 * i, 2 * i + 1):
                                head_squares(tt)
                            if i == 3:
                                dve.sem_inc(qk_sums, 1)
                        if c >= C_ROT:
                            n = (c - C_ROT) * 4 + i
                            if n == 0:
                                head_rms()
                            elif n <= TT:
                                rotate(n - 1)
                for u in range(N_TOK, N_IN):
                    for v in ([u + 2, u + 3] if u == N_TOK else [u + 3]):
                        if v < N_IN:
                            split_lo(v)
                    evacuate(E_TOK + 2 * (u - N_TOK) + 1)

                dve.wait_ge(act_evac, E_ALL // 2)
                dve.wait_ge(dve_evac, E_ALL // 2)
                for tt in range(TT + 1):
                    if tt < TT:
                        dve.wait_ge(qk_hi, 2 * tt + 1)
                        dve.tensor_tensor(qd[:, tt % 2, :, 1, :], tokA[:, tt, 0:AH * HD].rearrange("p (h d) -> p h d", h=AH),
                                          qd[:, tt % 2, :, 0, :].bitcast(F32), ALU.subtract).then_inc(qk_lo, 1)
                        dve.wait_ge(qk_hi, 2 * tt + 2)
                        dve.tensor_tensor(kd[:, tt % 2, 1, :, :, :],
                                          tokA[:, tt, AK:AV].rearrange("p (g d) -> p g d", g=KVH).unsqueeze(2)
                                          .to_broadcast([P, KVH, 2, HD]),
                                          kd[:, tt % 2, 0, :, :, :].bitcast(F32), ALU.subtract).then_inc(qk_lo, 1)
                    if tt >= 1:
                        u = tt - 1
                        dve.wait_ge(qkT_psum, 3 * u + 2)
                        dve.tensor_copy(qs[:, 4:8, u * P:(u + 1) * P],
                                        ps[:, u % 2 * 3 + 1, :].rearrange("p (h t) -> p h t", h=4)).then_inc(qkT_dve, 1)
                for i in range(N_ATT + 3):
                    if i < N_ATT:
                        dve.wait_ge(sc_ready, i + 1)
                        dve.tensor_reduce(nmx[:, i:i + 1], ps[:, 3 + i % 3, :], AX_X, ALU.max, negate=True)\
                           .then_inc(nmx_ready, 1)
                    if 2 <= i < N_ATT + 2:
                        v = i - 2
                        if v % 2 == 0:
                            dve.wait_ge(pT_psum, v + 1)
                            if v >= 2:
                                dve.wait_ge(ao_psum, v - 1)
                            dve.tensor_copy(pT[:, 0, :, :].rearrange("p k q -> p (k q)"), ps[:, 6, :])\
                               .then_inc(pT_even, 1)
                        dve.wait_ge(prob_ready, v + 1)
                        link(dve.reciprocal(rinvp[:, v:v + 1], rsum[:, v:v + 1]))
                    if i >= 3:
                        v = i - 3
                        s, h, qt = v // (AH * SB), v // SB % AH, v % SB
                        dve.wait_ge(ao_psum, v + 1)
                        dve.tensor_scalar(tokA[:, s * SB + qt, h * HD:(h + 1) * HD], ps[:, v % 3, 0:HD],
                                          rinvp[:, v:v + 1], None, ALU.mult).then_inc(ao_done, 1)

                dve.wait_ge(ao_done, N_ATT)
                dve.wait_ge(gla_consts, 48)
                link(dve.memset(attT[:], 0.0))
                for d in range(2):
                    rev = slice(None, None, -1) if d else slice(None)
                    if d == 1:
                        link(dve.memset(attT[:], 0.0))
                    for j in range(4):
                        r = d * 4 + j
                        gs = G[:, j // 2, j % 2 * SEQ:(j % 2 + 1) * SEQ]
                        b0 = V_GB + 2 * d + j // 2
                        dve.wait_ge(ln_ready, r + 1)
                        link(dve.tensor_scalar(gs, ps[:, j, :], vec[:, b0:b0 + 1], 0.0, ALU.add, ALU.min))
                        dve.tensor_tensor(gs, gs, ee[:, j % 2, :], ALU.subtract).then_inc(la_ready, 1)
                        dve.wait_ge(la_ready, r + 1)
                        if j % 2:
                            for s in range(NSEQ):
                                gq = G[:, j // 2, s * SEQ:(s + 1) * SEQ][:, rev]
                                ins = dve.tensor_tensor_scan(gq, cmask[:], gq, 0.0,
                                                             ALU.mult, ALU.add)
                                if s == 0:
                                    link(ins)
                                else:
                                    ins.then_inc(cum_ready, 1)
                                    dve.wait_ge(cum_ready, 2 * d + j // 2 + 1)
                    mid, last = (CH // 2 - 1, CH - 1) if d == 0 else (CH // 2, 0)
                    for ht in range(2):
                        r = d * 2 + ht
                        gc = G[:, ht, :].rearrange("p (c t) -> p c t", t=CH)
                        shape = [P, NSEQ * NCH, CH]
                        q, k = qkG[:, ht, :], qkG[:, 2 + ht, :]
                        dv = dml[:].rearrange("p (c t) -> p c t", t=CH)
                        dve.tensor_tensor(dv, gc, gc[:, :, mid:mid + 1].to_broadcast(shape), ALU.subtract)\
                           .then_inc(dml_ready, 1)
                        for m, (dst, src) in enumerate(((qhat[:, ht, :], q), (khat[:, ht, :], k),
                                                        (qtil[:, ht, :], q), (ktil[:], k))):
                            n = 4 * r + m
                            dve.wait_ge(gx_ready, n + 1)
                            if m == 3 and r >= 1:
                                dve.wait_ge(ktil_psum, 2 * r)
                            if m == 0 and r == 2:
                                dve.wait_ge(go_psum, TT)
                            dve.tensor_tensor(dst, src, gx[:, m % 2, :], ALU.mult).then_inc(gx_used, 1)
                            dve.wait_ge(gx_used, n + 1)
                            if m == 1:
                                dve.tensor_tensor(dv, gc[:, :, last:last + 1].to_broadcast(shape), gc, ALU.subtract)\
                                   .then_inc(dml_ready, 1)
                    dve.wait_ge(aL_ready, 2 * d + 2)
                    link(dve.memset(st[:, 0, :, :, :], 0.0))
                    for c in range(NCH - 1):
                        ci = step_of(d, c)
                        n = d * (NCH - 1) + c
                        decay = aL[:].rearrange("p h (s c) -> p s h c", s=NSEQ)[:, :, :, ci:ci + 1]
                        link(dve.tensor_tensor(gtmp[:].rearrange("p (s h e) -> p s h e", s=2, h=2), st[:, c, :, :, :],
                                               decay.to_broadcast([P, NSEQ, 2, HD]), ALU.mult))
                        dve.wait_ge(kv_psum, n + 1)
                        dve.tensor_tensor(st[:, c + 1, :, :, :].rearrange("p s h e -> p (s h e)"), gtmp[:],
                                          ps[:, 6 + n % 2, 0:256], ALU.add).then_inc(state_ready, 1)
                        dve.wait_ge(state_ready, n + 1)
                    for i in range(TT + 1):
                        if i < TT:
                            n = d * TT + i
                            dve.wait_ge(gat_psum, n + 1)
                            if i >= 2:
                                dve.wait_ge(go_psum, n - 1)
                            dve.copy_predicated(attT[:, i % 2, :, :, :],
                                                gam[:, d:d + 1, :].unsqueeze(1).to_broadcast([P, 2, 2, P]),
                                                ps[:, i % 2 * 4:i % 2 * 4 + 2, 0:2 * P].rearrange(
                                                    "p r (q t) -> p r q t", q=2))\
                               .then_inc(gat_ready, 1)
                        if i >= 1:
                            tt = i - 1
                            n = d * TT + tt
                            dve.wait_ge(go_psum, n + 1)
                            b = 2 + tt % 2 * 4
                            got = ps[:, b:b + 2, 0:2 * HD].rearrange("p r (q d) -> p r q d", q=2)
                            acc = oacc[:, tt, :].rearrange("p (q r d) -> p r q d", q=2, r=2)
                            if d == 0:
                                dve.tensor_copy(acc, got).then_inc(go_evac, 1)
                            else:
                                dve.tensor_tensor(acc, acc, got, ALU.add)\
                                   .then_inc(go_evac, 1)
                    dve.wait_ge(go_evac, (d + 1) * TT)
                for hb in range(2):
                    dve.wait_ge(gsq_ready, hb + 1)
                    dve.tensor_reduce(gss[:, 0, hb * 16:(hb + 1) * 16],
                                      gx[:, hb, :].rearrange("p (a d) -> p a d", d=HD), AX_X, ALU.add)\
                       .then_inc(gss_ready, 1)
                dve.wait_ge(grms_ready, 1)
                link(dve.reciprocal(gss[:, 0, :], gss[:, 1, :]))
                link(dve.tensor_scalar(gss[:, 0, :], gss[:, 0, :], HD ** -0.5, None, ALU.mult))
                oa = oacc[:].rearrange("p t (h d) -> p (t h) d", d=HD)
                link(dve.tensor_tensor(oa, oa, gss[:, 0, :].unsqueeze(2).to_broadcast([P, TT * GH, HD]), ALU.mult))
                dve.wait_ge(gsig_ready, 2)
                flat = "p t c -> p (t c)"
                link(dve.tensor_tensor(oacc[:].rearrange(flat), oacc[:].rearrange(flat), gg[:].rearrange(flat), ALU.mult))
                dve.tensor_tensor(gg[:].rearrange(flat), oacc[:].rearrange(flat), gx[:].rearrange("p a b -> p (a b)"),
                                  ALU.mult).then_inc(gla_done, 1)
                dve.wait_ge(gla_done, 1)

                dve.wait_ge(ml_consts, 32)
                dve.tensor_scalar(yf[:], small[64:64 + GROWS, :], vec[64:64 + GROWS, V_GBF:V_GBF + 1], None, ALU.add)\
                   .then_inc(yf_ready, 1)
                link(dve.tensor_scalar(ri[:], small[0:GROWS, :], vec[0:GROWS, V_GBI:V_GBI + 1], None, ALU.add))
                link(dve.memset(zr[:], 0.0))
                link(dve.memset(Fc[:], 0.0))
                link(dve.memset(mm_rows[:], 0.0))
                dve.wait_ge(yf_ready, 1)
                dve.wait_ge(fl_ready, 1)
                link(dve.scalar_tensor_tensor(fl[:], yf[:], 0.0, fl[:], ALU.min, ALU.subtract))
                for d in range(2):
                    rows = slice(32 * d, 32 * d + MH)
                    rev = slice(None, None, -1) if d else slice(None)
                    for s in range(NSEQ):
                        tok = slice(s * SEQ, (s + 1) * SEQ)
                        lf, ig = fl[rows, tok][:, rev], ri[rows, tok][:, rev]
                        link(dve.tensor_tensor_scan(Fc[rows, tok][:, rev], lf, zr[rows, :], 0.0, ALU.add, ALU.add))
                        link(dve.tensor_tensor_scan(mm_rows[rows, tok][:, rev], lf, ig, 0.0, ALU.add, ALU.max))
                link(dve.tensor_tensor(Rr[:], Fc[:], mm_rows[:], ALU.subtract))
                dve.tensor_tensor(Cr[:], ri[:], Fc[:], ALU.subtract).then_inc(rc_ready, 1)
                dve.wait_ge(R_hi, 1)
                dve.tensor_tensor(Rl[:], Rr[:], Rh[:].bitcast(F32), ALU.subtract).then_inc(R_split, 1)

                def stack_lo(w):
                    s, h, tok, rows, other = head_rows(w)
                    q, k = qkM[rows, h // 2, tok], qkM[rows, 2 + h // 2, tok]
                    qh, kh = qh2[rows, w % 2, :].bitcast(F32), ks2[rows, w % 2, :].bitcast(F32)
                    dve.wait_ge(stk_hi, 3 * (w + 1))
                    dve.tensor_tensor(ql2[rows, w % 2, :], q, qh, ALU.subtract).then_inc(stk_lo, 1)
                    dve.tensor_tensor(ql2[other, w % 2, :], q, qh, ALU.subtract).then_inc(stk_lo, 1)
                    dve.tensor_tensor(ks2[other, w % 2, :], k, kh, ALU.subtract).then_inc(stk_lo, 1)

                stack_lo(0)

                def normalise(w):
                    s, h = w // MH, w % MH
                    num = ps[:, 6:8, 0:SB * (HD + 1)].rearrange("p d (j e) -> p d j e", j=SB)
                    dve.wait_ge(num_psum, w + 1)
                    link(dve.tensor_copy(dn[:].unsqueeze(3), num[:, :, :, HD:HD + 1]))
                    link(dve.scalar_tensor_tensor(rc[:], dn[:], -1.0, dn[:], ALU.mult, ALU.max))
                    link(dve.tensor_tensor(
                        rc[:], rc[:], EM[:, s * SB:(s + 1) * SB, h:h + 33:32].rearrange("p t d -> p d t"), ALU.max))
                    link(dve.reciprocal(rc[:], rc[:]))
                    dve.tensor_tensor(t12[:], num[:, :, :, 0:HD], rc[:].unsqueeze(3).to_broadcast([P, 2, SB, HD]),
                                      ALU.mult).then_inc(ml_evac, 1)
                    dve.wait_ge(ml_evac, w + 1)
                    link(dve.tensor_tensor(hs[:], t12[:, 0, :, :], t12[:, 1, :, :], ALU.add))
                    cs = co[:, s * SB:(s + 1) * SB, h * HD:(h + 1) * HD]
                    dve.wait_ge(msig_ready, 1)
                    link(dve.tensor_tensor(cs, cs, hs[:], ALU.mult))

                for w in range(N_ML):
                    for d in range(2):
                        dve.wait_ge(rb_psum, 2 * w + d + 1)
                        if w >= 1:
                            dve.wait_ge(dt_ready, 2 * SB * w)
                        dve.tensor_tensor(mR[:, d, :].rearrange("p (j t) -> p j t", j=SB),
                                          ps[:, 4 + d, :].rearrange("p (j t) -> p j t", j=SB),
                                          mmask[:, d:d + 1, :].to_broadcast([P, SB, P]), ALU.add).then_inc(mr_ready, 1)
                    if w + 1 < N_ML:
                        stack_lo(w + 1)
                    if w >= 1:
                        normalise(w - 1)
                    for i in range(SB):
                        dve.wait_ge(qk_psum, SB * w + i + 1)
                        for d in range(2):
                            lo, hi = fwd_or_bwd_range(d, i)
                            dve.wait_ge(dt_ready, 2 * SB * w + 2 * i + d + 1)
                            D_t = Dts[w % 2][:, d, i, lo:hi]
                            dve.scalar_tensor_tensor(D_t, ps[:, i, lo:hi], HD ** -0.5, D_t, ALU.mult,
                                                     ALU.mult).then_inc(wt_ready, 1)
                normalise(N_ML - 1)
                dve.sem_inc(heads_gated, 1)
                for hb in range(2):
                    dve.wait_ge(msq_ready, hb + 1)
                    dve.tensor_reduce(mss[:, 0, hb * 16:(hb + 1) * 16],
                                      Dt0[:, hb, 0:2, :].rearrange("p a b -> p (a b)").rearrange("p (a d) -> p a d", d=HD),
                                      AX_X, ALU.add).then_inc(mss_ready, 1)
                dve.wait_ge(mrms_ready, 1)
                link(dve.reciprocal(mss[:, 0, :], mss[:, 1, :]))
                ca = co[:].rearrange("p t (h d) -> p (t h) d", d=HD)
                dve.tensor_tensor(ca, ca, mss[:, 0, :].unsqueeze(2).to_broadcast([P, TT * MH, HD]), ALU.mult)\
                   .then_inc(ml_done, 1)
                dve.wait_ge(ml_done, 1)

                for u in range(N_IN, N_IN + SPLIT):
                    split_lo(u)
                for tt in range(TT):
                    tok = slice(tt * P, (tt + 1) * P)
                    bank = tt % 4 * 2
                    dve.wait_ge(mixh_ready, 3 * tt + 1)
                    dve.tensor_tensor(hl[:, 0:4, tok], ps[:, bank, :].rearrange("p (i t) -> p i t", i=4),
                                      hh[:, 0:4, tok].bitcast(F32), ALU.subtract).then_inc(mixl_ready, 1)
                    dve.wait_ge(mixh_ready, 3 * tt + 3)
                    for i, g in enumerate((V_GLAN, V_MLN)):
                        dve.scalar_tensor_tensor(
                            hl[:, 4 + 2 * i:6 + 2 * i, tok],
                            ps[:, bank + 1, 2 * i * P:(2 * i + 2) * P].rearrange("p (i t) -> p i t", i=2),
                            vec[:, g:g + 1], hh[:, 4 + 2 * i:6 + 2 * i, tok].bitcast(F32), ALU.mult,
                            ALU.subtract).then_inc(mixl_ready, 1)
                dve.wait_ge(reloaded, 16)
                for o in range(KT):
                    dve.wait_ge(wo_psum, o + 1)
                    dve.tensor_tensor(x[:, o, :], x[:, o, :], ps[:, o % 4 * 2:o % 4 * 2 + 2, :].rearrange("p s t -> p (s t)"),
                                      ALU.add).then_inc(wo_done, 1)
                    if o + SPLIT < KT:
                        split_lo(N_IN + SPLIT + o)

                def ffn_lo(kind, j):
                    dve.wait_ge(f_hi[kind], j + 1)
                    dve.tensor_tensor(wlo[:, kind, :, :], raw[:, kind, :].rearrange("p (k c) -> p k c", k=KT),
                                      whi[:, kind, :, :].bitcast(F32), ALU.subtract).then_inc(f_lo[kind], 1)

                for kind in (0, 1):
                    ffn_lo(kind, 0)
                norm(1, V_FFN)

                def conv(acc, pair, taps, init, half, done, j):
                    dve.wait_ge(init, j + 1)
                    dve.scalar_tensor_tensor(acc[:, :, 1:SEQ], ps[:, pair:pair + 2, 0:SEQ - 1], cw[:, taps:taps + 1],
                                             acc[:, :, 1:SEQ], ALU.mult, ALU.add).then_inc(half, 1)
                    dve.wait_ge(half, j + 1)
                    dve.scalar_tensor_tensor(acc[:, :, 0:SEQ - 1], ps[:, pair:pair + 2, 1:SEQ], cw[:, taps + 2:taps + 3],
                                             acc[:, :, 0:SEQ - 1], ALU.mult, ALU.add).then_inc(done, 1)

                def add_down(j):
                    for o in range(KT):
                        dve.wait_ge(d_psum, j * KT + o + 1)
                        b = 4 + o % 2 * 2
                        dve.tensor_tensor(x[:, o, :], x[:, o, :], ps[:, b:b + 2, :].rearrange("p s t -> p (s t)"),
                                          ALU.add).then_inc(d_done, 1)

                def iteration(j, first=False, last=False):
                    conv(accg, 0, 0, g_init, g_half, g_conv, j)
                    if not last:
                        ffn_lo(0, j + 1)
                    if not first:
                        add_down(j - 1)
                    conv(accv, 2, 4, v_init, v_half, v_conv, j)
                    if not last:
                        ffn_lo(1, j + 1)
                    dve.wait_ge(sil_ready, j + 1)
                    dve.wait_ge(v_conv, j + 1)
                    dve.tensor_tensor(accv[:], accv[:], sil[:], ALU.mult).then_inc(act_ready, 1)
                    ffn_lo(2, j)
                    dve.wait_ge(acth_ready, j + 1)
                    dve.tensor_tensor(actl[:], accv[:], acth[:].bitcast(F32), ALU.subtract).then_inc(actl_ready, 1)

                iteration(0, first=True)
                with dve.Fori(1, FT - 1) as j:
                    iteration(j)
                iteration(FT - 1, last=True)
                add_down(FT - 1)
                dve.sem_inc(layer_end, 1)
                dve.wait_ge(layer_go, l + 1)


def axial_tables():
    pos = np.arange(SEQ)
    row = (pos // GRID_W).astype(np.float32)
    col = (pos % GRID_W).astype(np.float32)
    n = HD // 4
    inv = np.power(np.float32(ROPE_THETA), -np.arange(n, dtype=np.float32) / np.float32(n)).astype(np.float32)
    ang = np.stack([row[:, None] * inv, col[:, None] * inv], axis=1)
    c, s = np.cos(ang), np.sin(ang)
    cos = np.stack([c, c], axis=2).reshape(SEQ, HD)
    sin = np.stack([s, -s], axis=2).reshape(SEQ, HD)
    lay = lambda t: t.reshape(SB, P, HD).transpose(1, 0, 2)
    return np.ascontiguousarray(np.stack([lay(cos), lay(sin)])).astype(np.float32)


def masks():
    s, t = np.arange(P)[:, None], np.arange(P)[None, :]
    same = (s // CH) == (t // CH)
    gla = np.stack([same & (s <= t), same & (s >= t)], axis=1).astype(np.uint32)
    chunk = np.broadcast_to((np.arange(SEQ) % CH != 0).astype(np.float32), (P, SEQ))
    ml = np.stack([np.where(s <= t, 0.0, -1e30), np.where(s >= t, 0.0, -1e30)], axis=1).astype(np.float32)
    sel = np.zeros((GROWS, 2 * MH, P), np.float32)
    for d in range(2):
        for h in range(MH):
            sel[32 * d + h, d * MH + h, :] = 1.0
    return gla, np.ascontiguousarray(chunk), ml, sel


def layouts(i):
    f = lambda a: np.asarray(a, np.float32) if np.asarray(a).dtype != np.float32 else np.asarray(a)
    x = np.concatenate([f(i["x_prompt"])[0], f(i["x_sample"])[0]], axis=0)
    x_in = np.ascontiguousarray(x.T.reshape(KT, P, T).transpose(1, 0, 2))
    w_in = f(i["w_in"])
    small = np.zeros((DEPTH, D, P), np.float32)
    for d in range(2):
        small[:, :, 32 * d:32 * d + MH] = w_in[:, :, CG + d * MH:CG + (d + 1) * MH]
        small[:, :, BA_ROW[d]:BA_ROW[d] + 16] = w_in[:, :, BA + 16 * d:BA + 16 * (d + 1)]
        small[:, :, 64 + 32 * d:64 + 32 * d + MH] = w_in[:, :, CG + (2 + d) * MH:CG + (3 + d) * MH]
    cols = [c + o for c in TOK_COLS for o in (0, P)] + FEAT_COLS
    unit = lambda w: w.reshape(DEPTH, KT, P, P).transpose(0, 2, 1, 3).reshape(DEPTH, P, UNIT)
    units = [unit(w_in[:, :, c:c + P]) for c in cols] + [unit(small)]
    w_out = f(i["w_out"])
    units += [unit(w_out[:, :, o * P:(o + 1) * P]) for o in range(KT)]
    w_units = np.ascontiguousarray(np.stack(units, axis=1))
    up = f(i["w_up"]).reshape(DEPTH, KT, P, 2, FT, P).transpose(0, 4, 3, 2, 1, 5).reshape(DEPTH, FT, 2, P, UNIT)
    down = f(i["w_down"]).reshape(DEPTH, FT, 1, P, UNIT)
    w_ffn = np.ascontiguousarray(np.concatenate([up, down], axis=2))
    vecs = np.zeros((DEPTH, P, NVEC), np.float32)
    vecs[:, :, V_MIX:V_MIX + KT] = f(i["norm_mix_g"]).reshape(DEPTH, KT, P).transpose(0, 2, 1)
    vecs[:, :, V_FFN:V_FFN + KT] = f(i["norm_ffn_g"]).reshape(DEPTH, KT, P).transpose(0, 2, 1)
    vecs[:, :, V_GLAN] = np.tile(f(i["gla_norm_g"]), (1, 2))
    vecs[:, :, V_MLN] = np.tile(f(i["mlstm_norm_g"]), (1, 2))
    vecs[:, :, V_GB:V_GB + 4] = f(i["gla_gate_b"]).reshape(DEPTH, 4, P).transpose(0, 2, 1)
    gb = f(i["mlstm_gate_b"])
    for d in range(2):
        vecs[:, 32 * d:32 * d + MH, V_GBI] = gb[:, d]
        vecs[:, 64 + 32 * d:64 + 32 * d + MH, V_GBF] = gb[:, 2 + d]
    w2p = np.zeros((DEPTH, P, 2, 256), np.float32)
    for d in range(2):
        w2p[:, BA_ROW[d]:BA_ROW[d] + 16, d, :] = f(i["gla_gate_w2"])[:, d]
    qkg = np.stack([f(i["attn_qn_g"]), f(i["attn_kn_g"])], axis=1)
    qkg = np.ascontiguousarray(np.broadcast_to(qkg[:, None], (DEPTH, P, 2, HD)))
    taps = np.concatenate([f(i["conv_w"]), f(i["conv_b"])[:, None]], axis=1)
    convp = np.ascontiguousarray(taps.reshape(DEPTH, 4, 2, FT, P).transpose(0, 4, 3, 2, 1).reshape(DEPTH, P, FT, 8))
    gla, chunk, ml, sel = masks()
    return {"x_in": x_in, "w_units": w_units, "w_ffn": w_ffn, "vecs": vecs, "w2p": w2p, "qkg": qkg,
            "convp": convp, "rope": axial_tables(), "gmask": gla, "chunkmask": chunk, "lmask": ml,
            "sel": sel, "ident_in": np.eye(P, dtype=np.float32)}


def kernel(**inputs):
    import concourse.bacc as bacc
    from concourse.bass_utils import run_bass_kernel_spmd as run

    arrays = layouts(inputs)
    nc = bacc.Bacc("TRN2", target_bir_lowering=False, num_devices=1)
    args = [nc.dram_tensor(f"d_{n}", a.shape, mybir.dt.from_np(a.dtype), kind="ExternalInput").ap()
            for n, a in arrays.items()]
    out = nc.dram_tensor("d_x_out", (P, KT, T), F32, kind="ExternalOutput").ap()
    build(nc, *args, out)
    r = run(nc, [{f"d_{n}": a for n, a in arrays.items()}], core_ids=[0])
    y = r.results[0]["d_x_out"].transpose(1, 0, 2).reshape(D, T)
    return (np.ascontiguousarray(y[:, 0:SEQ].T)[None], np.ascontiguousarray(y[:, SEQ:T].T)[None])
```

```python
from contextlib import ExitStack

import numpy as np

import concourse.bass as bass
from concourse import mybir
from concourse.alu_op_type import AluOpType as ALU

F32 = mybir.dt.float32
F32R = mybir.dt.float32r
U32 = mybir.dt.uint32
ACT = mybir.ActivationFunctionType
AX_X = mybir.AxisListType.X

P = 128
DEPTH = 2
D = 1024
SEQ = 512
NSEQ = 2
T = NSEQ * SEQ
KT = D // P
TT = T // P
SB = SEQ // P
HD = 64
EPS = 1e-6
GRID_W = 64
ROPE_THETA = 10000.0
AH, KVH = 8, 2
NQK = AH + KVH
N_ATT = NSEQ * AH * SB
GH = MH = 4
GLA_TAU = 16.0
DFF = 2816
FT = DFF // P
TILES_AFTER = (2, 3, 6, 7, 10, 11, 14, 14)
Z_AFTER = (0, 2, 4, 6)
KEYS_AT = 4
KEY_TILES = sum(c <= KEYS_AT for c in TILES_AFTER)
CH = 32
NCH = SEQ // CH
UNIT = KT * P

AQ, AK, AV = 0, 512, 640
BQ, BK, BV, BG, BA = 768, 1024, 1280, 1536, 1792
CQ, CK, CV, CO, CG = 1824, 2080, 2336, 2592, 2848

TOK_COLS = [AQ, AQ + 256, AK, BV, BG, CV, CO]
FEAT_COLS = [CQ, CQ + 128, CK, CK + 128, BQ, BQ + 128, BK, BK + 128]
N_TOK = 2 * len(TOK_COLS)
N_IN = N_TOK + len(FEAT_COLS) + 1
N_OUT = KT
N_UNITS = N_IN + N_OUT
RAW, SPLIT = 3, 4
E_TOK = len(TOK_COLS) * TT
C_ROT = 4
E_ALL = E_TOK + 2 * (N_IN - N_TOK)

BA_ROW = (4, 36)
GROWS = 36
RROWS = 64 + GROWS

V_MIX, V_FFN, V_GLAN, V_MLN, V_GB, V_GBI, V_GBF = 0, 8, 16, 17, 18, 22, 23
NVEC = 24


def build(nc, x_in, w_units, w_ffn, vecs, w2p, qkg, convp, rope, gmask, chunkmask, lmask, sel,
          ident_in, x_out):
    ctx = ExitStack()
    with ctx:
        def fixed(name, shape, dt=F32):
            return ctx.enter_context(nc.sbuf_tensor(name, shape, dt))

        def region(size, specs):
            assert sum(int(np.prod(shape[1:])) * 4 + 31 & ~31 for _, shape, _ in specs) <= size, specs[0][0]
            with ExitStack() as phase:
                return [phase.enter_context(nc.sbuf_tensor(n, s, d)) for n, s, d in specs]

        W_BYTES = 2 * SPLIT * UNIT * 4
        H_BYTES = 2 * KT * T * 4
        Q_BYTES = 4 * (2 * 4 * T + TT * (768 + 3 * 256 + MH * (HD + 1)) + T)
        ident = fixed("ident", [P, P])
        ones = fixed("ones", [P, P])
        eps = fixed("eps", [P, 1])
        vec = fixed("vec", [P, NVEC])
        gam = fixed("gam", [P, 2, P], U32)
        cmask = fixed("cmask", [P, SEQ])
        raw = fixed("raw", [P, RAW, UNIT])

        with ExitStack() as w_region:
            whi = w_region.enter_context(nc.sbuf_tensor("whi", [P, SPLIT, KT, P], F32R))
            wlo = w_region.enter_context(nc.sbuf_tensor("wlo", [P, SPLIT, KT, P], F32R))
        st, ktok0, oacc = region(W_BYTES, [
            ("states", [P, NCH, NSEQ, 2, HD], F32), ("ktok0", [P, TT, 256], F32), ("oacc", [P, TT, 256], F32)])
        qd, kd, G1, G0, w2s = region(W_BYTES, [
            ("qd", [P, 2, AH, 2, HD], F32R), ("kd", [P, 2, 2, KVH, 2, HD], F32R),
            ("G1", [P, 2, T], F32), ("G0", [P, 2, T], F32), ("w2s", [P, 2, 256], F32)])
        e0, = region(W_BYTES, [("e0", [P, 2, T], F32)])
        Dt1, qh2, ql2 = region(W_BYTES, [
            ("Dt1", [P, 2, SB, SEQ], F32), ("qh2", [P, 2, SEQ], F32R), ("ql2", [P, 2, SEQ], F32R)])
        w_hold = ctx.enter_context(nc.sbuf_tensor("w_region", [P, W_BYTES // 4], F32))

        hh, hl = region(H_BYTES, [("hh", [P, KT, T], F32R), ("hl", [P, KT, T], F32R)])
        (qs, ks, prob, pT, nmx, rsum, rinvp) = region(H_BYTES, [
            ("qs", [P, AH, T], F32R), ("ks", [P, 2, KVH, T], F32R),
            ("prob", [P, 3, SEQ], F32), ("pT", [P, 2, SB, P], F32),
            ("nmx", [P, 64], F32), ("rsum", [P, 64], F32), ("rinvp", [P, 64], F32)])
        (G, gx, dml, ktil, qhat0, khat0, qtil0, qtil1, attT, aL,
         gtmp, gss) = region(H_BYTES, [
            ("G", [P, 2, T], F32), ("gx", [P, 2, T], F32), ("dml", [P, T], F32), ("ktil", [P, T], F32),
            ("qhat0", [P, 2, T], F32), ("khat0", [P, 2, T], F32),
            ("qtil0", [P, 2, T], F32), ("qtil1", [P, 2, T], F32), ("attT", [P, 2, 2, 2, P], F32),
            ("aL", [P, 2, 2, NSEQ * NCH], F32),
            ("gtmp", [P, 256], F32), ("gss", [P, 2, TT * GH], F32)])
        Gs = (G0, G)
        (yf, ri, fl, Fc, mm_rows, Rs, selr, mmask, CT, EM, mR, Dt0, rc, dn, t12, hs,
         mss, ks2) = region(H_BYTES, [
            ("yf", [GROWS, T], F32), ("ri", [GROWS, T], F32),
            ("fl", [GROWS, T], F32), ("Fc", [GROWS, T], F32), ("mm_rows", [GROWS, T], F32),
            ("Rs", [RROWS, T], F32R),
            ("selr", [RROWS, 2 * MH, P], F32R), ("mmask", [P, 2, P], F32),
            ("CT", [P, TT, GROWS], F32), ("EM", [P, TT, GROWS], F32),
            ("mR", [P, 2, SEQ], F32), ("Dt0", [P, 2, SB, SEQ], F32),
            ("rc", [P, 2, SB], F32), ("dn", [P, 2, SB], F32), ("t12", [P, 2, SB, HD], F32),
            ("hs", [P, SB, HD], F32), ("mss", [P, 2, TT * MH], F32),
            ("ks2", [P, 2, SEQ], F32R)])
        Rr, Cr = yf, ri
        sels = mR[0:RROWS, :, :].rearrange("p a (b c) -> p (a b) c", c=P)
        h_hold = ctx.enter_context(nc.sbuf_tensor("h_region", [P, H_BYTES // 4], F32))

        (qkM, qkG, tokA, gv, gg, vaug, co, small) = region(Q_BYTES, [
            ("qkM", [P, 4, T], F32), ("qkG", [P, 4, T], F32), ("tokA", [P, TT, 768], F32),
            ("gv", [P, TT, 256], F32), ("gg", [P, TT, 256], F32),
            ("vaug", [P, TT, MH, HD + 1], F32), ("co", [P, TT, 256], F32),
            ("small", [P, T], F32)])
        (ropec, ropes, tabc, tabs, t1, t2, qkgain, ssq, rqk) = region(4 * KT * T, [
            ("ropec", [P, SB, HD], F32), ("ropes", [P, SB, HD], F32),
            ("tabc", [P, SB, NQK, HD], F32), ("tabs", [P, SB, NQK, HD], F32),
            ("t1", [P, NQK * HD], F32), ("t2", [P, NQK * HD], F32), ("qkgain", [P, 2, HD], F32),
            ("ssq", [P, TT, NQK], F32), ("rqk", [P, TT, NQK], F32)])
        (x, sq, sqsum, rms, rinv, diag, accg, accv, sil, acth, actl, convs, cw, hf) = region(Q_BYTES, [
            ("x", [P, KT, T], F32), ("sq", [P, 2, T], F32), ("sqsum", [P, T], F32),
            ("rms", [P, TT], F32), ("rinv", [P, TT], F32), ("diag", [P, TT, P], F32),
            ("accg", [P, NSEQ, SEQ], F32), ("accv", [P, NSEQ, SEQ], F32),
            ("sil", [P, NSEQ, SEQ], F32), ("acth", [P, NSEQ, SEQ], F32R),
            ("actl", [P, NSEQ, SEQ], F32R), ("convs", [P, FT, 8], F32), ("cw", [P, 8], F32),
            ("hf", [P, 2, SEQ], F32)])
        q_hold = ctx.enter_context(nc.sbuf_tensor("q_region", [P, Q_BYTES // 4], F32))

        ps = ctx.enter_context(nc.psum_tensor("ps", [P, 8, 512], F32))

        def sem(name):
            return ctx.enter_context(nc.semaphore(name))

        per_layer, mixers_only = [], []

        def lsem(name):
            s = sem(name)
            per_layer.append(s)
            return s

        def msem(name):
            s = sem(name)
            mixers_only.append(s)
            return s

        x_loaded = [sem(f"x_loaded{k}") for k in range(KT)]
        consts_loaded, ones_set = sem("consts_loaded"), sem("ones_set")
        layer_end, layer_go, x_stored = lsem("layer_end"), sem("layer_go"), sem("x_stored")
        vec_loaded, reloaded = lsem("vec_loaded"), lsem("reloaded")
        act_chain, dve_chain = lsem("act_chain"), lsem("dve_chain")
        first_sq_ready, first_sq_used = sem("first_sq_ready"), sem("first_sq_used")
        first_rms_ready, first_diag_ready = sem("first_rms_ready"), sem("first_diag_ready")
        first_ss_psum = sem("first_ss_psum")
        first_rinv_ready, first_rinv_spread = sem("first_rinv_ready"), sem("first_rinv_spread")
        sq_ready, sq_used = lsem("sq_ready"), lsem("sq_used")
        rms_ready, diag_ready, rinv_spread = lsem("rms_ready"), lsem("diag_ready"), lsem("rinv_spread")
        ss_psum = lsem("ss_psum")
        rinv_ready, hf_ready = lsem("rinv_ready"), lsem("hf_ready")
        hh_ready, h_ready = lsem("hh_ready"), lsem("h_ready")
        raw_full = [msem(f"raw_full{i}") for i in range(RAW)]
        hi_ready, lo_ready, unit_used = msem("hi_ready"), msem("lo_ready"), msem("unit_used")
        proj_ready, act_evac, dve_evac = msem("proj_ready"), msem("act_evac"), msem("dve_evac")
        att_consts = msem("att_consts")
        qk_sums, qk_rms, rot_ready = msem("qk_sums"), msem("qk_rms"), msem("rot_ready")
        qk_hi, qk_lo, qkT_psum = msem("qk_hi"), msem("qk_lo"), msem("qkT_psum")
        qkT_act, qkT_dve = msem("qkT_act"), msem("qkT_dve")
        sc_ready, nmx_ready, prob_ready = msem("sc_ready"), msem("nmx_ready"), msem("prob_ready")
        pT_psum, pT_even, pT_odd = msem("pT_psum"), msem("pT_even"), msem("pT_odd")
        ao_psum, ao_done = msem("ao_psum"), msem("ao_done")
        z_taken, z_abs = msem("z_taken"), msem("z_abs")
        gla_consts, z_psum, ln_ready = msem("gla_consts"), msem("z_psum"), msem("ln_ready")
        la_ready, cum_ready, dml_ready = msem("la_ready"), msem("cum_ready"), msem("dml_ready")
        gx_ready, gx_used = msem("gx_ready"), msem("gx_used")
        ktil_psum, ktok_ready, aL_ready = msem("ktil_psum"), msem("ktok_ready"), msem("aL_ready")
        kv_psum, state_ready = msem("kv_psum"), msem("state_ready")
        gat_psum, gat_ready = msem("gat_psum"), msem("gat_ready")
        go_psum, go_evac = msem("go_psum"), msem("go_evac")
        gsq_ready, gss_ready, grms_ready = msem("gsq_ready"), msem("gss_ready"), msem("grms_ready")
        gsig_ready, gla_done = msem("gsig_ready"), msem("gla_done")
        ml_consts, yf_ready, fl_ready = msem("ml_consts"), msem("yf_ready"), msem("fl_ready")
        rc_ready, ct_psum, ct_ready = msem("rc_ready"), msem("ct_psum"), msem("ct_ready")
        qk_psum, rb_psum, mr_ready = msem("qk_psum"), msem("rb_psum"), msem("mr_ready")
        dt_ready, wt_ready, num_psum = msem("dt_ready"), msem("wt_ready"), msem("num_psum")
        sel_ready, R_split = msem("sel_ready"), msem("R_split")
        R_hi = msem("R_hi")
        stk_hi, stk_lo = msem("stk_hi"), msem("stk_lo")
        heads_gated, ml_evac = msem("heads_gated"), msem("ml_evac")
        msq_ready, mss_ready, mrms_ready = msem("msq_ready"), msem("mss_ready"), msem("mrms_ready")
        msig_ready, ml_done = msem("msig_ready"), msem("ml_done")
        mix_psum, mixh_ready, mixl_ready = msem("mix_psum"), msem("mixh_ready"), msem("mixl_ready")
        wo_psum, wo_done = msem("wo_psum"), msem("wo_done")
        f_full = [lsem(f"f_full_{k}") for k in "gvd"]
        f_hi = [lsem(f"f_hi_{k}") for k in "gvd"]
        f_lo = [lsem(f"f_lo_{k}") for k in "gvd"]
        f_used = [lsem(f"f_used_{k}") for k in "gvd"]
        conv_loaded, cw_ready = lsem("conv_loaded"), lsem("cw_ready")
        g_init, v_init = lsem("g_init"), lsem("v_init")
        g_half, v_half = lsem("g_half"), lsem("v_half")
        g_conv, v_conv = lsem("g_conv"), lsem("v_conv")
        sil_ready, act_ready = lsem("sil_ready"), lsem("act_ready")
        acth_ready, actl_ready = lsem("acth_ready"), lsem("actl_ready")
        d_psum, d_done = lsem("d_psum"), lsem("d_done")

        def evac_target(e):
            if e < E_TOK:
                c, tt = divmod(e, TT)
                col = TOK_COLS[c]
                if col < BQ:
                    return tokA[:, tt, col:col + 256], 256
                if col == CV:
                    return vaug[:, tt, :, 0:HD], 256
                return {BV: gv, BG: gg, CO: co}[col][:, tt, :], 256
            f, s = divmod(e - E_TOK, NSEQ)
            cols = slice(s * SEQ, (s + 1) * SEQ)
            if f < 4:
                return qkM[:, f, cols], SEQ
            if f < 8:
                return qkG[:, f - 4, cols], SEQ
            return small[:, cols], SEQ

        def evac_bank(e):
            return e - 6 if e in (6, 7) else e % 8

        def evac_source(e):
            dst, n = evac_target(e)
            src = ps[:, evac_bank(e), 0:n]
            if e < E_TOK and TOK_COLS[e // TT] == CV:
                src = src.rearrange("p (h d) -> p h d", h=MH)
            return dst, src

        qhat, khat, qtil = (qhat0, qkG[:, 0:2, :]), (khat0, qkG[:, 2:4, :]), (qtil0, qtil1)
        ktok = (ktok0, tokA[:, :, AK:AK + 256])

        N_ML = NSEQ * MH
        Dts = (Dt0, Dt1)

        def head_rows(w):
            s, h = w // MH, w % MH
            return s, h, slice(s * SEQ, (s + 1) * SEQ), slice(h % 2 * HD, (h % 2 + 1) * HD),\
                slice((1 - h % 2) * HD, (2 - h % 2) * HD)

        def fwd_or_bwd_range(d, i):
            return (i * P, SEQ) if d == 0 else (0, (i + 1) * P)

        def step_of(d, ci):
            return ci if d == 0 else NCH - 1 - ci

        def tile_of(d, i):
            return (i // 2 if d == 0 else SB - 1 - i // 2) + i % 2 * SB

        block = ctx.enter_context(nc.Block())

        @block.sync
        def _(sp):
            for dst, src in ((ident, ident_in), (gam, gmask), (cmask, chunkmask)):
                sp.dma_start(dst[:], src).then_inc(consts_loaded, 16)
            for k in range(KT):
                sp.dma_start(x[:, k, :], x_in[:, k, :]).then_inc(x_loaded[k], 16)
            for k in range(KT):
                sp.wait_ge(x_loaded[k], 16)
                sp.dma_start(x_out[:, k, :], x[:, k, :]).then_inc(x_stored, 16)
            with sp.Fori(0, DEPTH) as l:
                sp.dma_start(vec[:], vecs[l]).then_inc(vec_loaded, 16)

                def load_unit(n):
                    if n >= RAW:
                        sp.wait_ge(lo_ready, n - RAW + 1)
                    sp.dma_start(raw[:, n % RAW, :], w_units[l, n]).then_inc(raw_full[n % RAW], 16)

                load_unit(0)
                load_unit(1)
                for n in range(2, 6):
                    load_unit(n)
                sp.wait_ge(x_stored, l * (16 * KT) + 16 * KT)
                sp.wait_ge(h_ready, NSEQ * KT)
                sp.dma_start(ropec[:], rope[0]).then_inc(att_consts, 16)
                sp.dma_start(ropes[:], rope[1]).then_inc(att_consts, 16)
                sp.dma_start(qkgain[:], qkg[l]).then_inc(att_consts, 16)
                for n in range(6, N_IN + RAW):
                    load_unit(n)
                sp.wait_ge(proj_ready, E_ALL)
                sp.dma_start(w2s[:], w2p[l]).then_inc(gla_consts, 16)
                sp.wait_ge(go_evac, 2 * TT)
                sp.dma_start(sels[:], sel).then_inc(ml_consts, 16)
                sp.dma_start(mmask[:], lmask).then_inc(ml_consts, 16)
                sp.wait_ge(ml_done, 1)
                load_unit(N_IN + RAW)
                load_unit(N_IN + RAW + 1)
                sp.dma_start(x[:], x_out).then_inc(reloaded, 16)
                for n in range(N_IN + RAW + 2, N_UNITS):
                    load_unit(n)

                sp.wait_ge(mix_psum, 2 * TT)
                sp.dma_start(convs[:], convp[l]).then_inc(conv_loaded, 16)

                def load_ffn(j):
                    for kind in range(3):
                        if isinstance(j, int) and j == 0:
                            sp.wait_ge(lo_ready, N_UNITS)
                        else:
                            sp.wait_ge(f_lo[kind], j)
                        sp.dma_start(raw[:, kind, :], w_ffn[l, j, kind]).then_inc(f_full[kind], 16)

                load_ffn(0)
                sp.wait_ge(f_used[0], 1)
                sp.wait_ge(f_hi[0], 1)
                sp.wait_ge(f_lo[0], 1)
                for s in mixers_only:
                    sp.sem_clear(s)
                with sp.Fori(1, FT) as j:
                    load_ffn(j)
                for k in range(KT):
                    sp.wait_ge(d_done, ((FT - 1) * KT + k + 1) * NSEQ)
                    sp.dma_start(x_out[:, k, :], x[:, k, :]).then_inc(x_stored, 16)
                sp.wait_ge(layer_end, 3)
                for s in per_layer:
                    sp.sem_clear(s)
                sp.sem_inc(layer_go, 1)
            sp.wait_ge(x_stored, 16 * KT * (DEPTH + 1))

        @block.tensor
        def _(pe):
            pe.wait_ge(consts_loaded, 48)
            pe.wait_ge(ones_set, 2)

            def sum_squares(bank, used, total, done):
                pe.wait_ge(used, total)
                for tt in range(TT):
                    mm = pe.matmul(ps[:, bank, tt:tt + 1], sqsum[:, tt * P:(tt + 1) * P], ones[:, 0:1],
                                   start=(tt == 0), stop=True, skip_group_check=True)
                mm.then_inc(done, 1)

            def spread(ready, done, count=0):
                for s in range(NSEQ):
                    pe.wait_ge(ready, count + s + 1)
                    pe.matmul(ps[:, 6 + s, :], ones[:], diag[:, s * SB:(s + 1) * SB, :].rearrange("p b t -> p (b t)"),
                              start=True, stop=True).then_inc(done, 1)

            sum_squares(0, first_sq_used, KT, first_ss_psum)
            spread(first_diag_ready, first_rinv_spread)
            with pe.Fori(0, DEPTH) as l:
                def passes3(out, stat, mov, first, last):
                    pe.matmul(out, stat[1], mov[0], start=first, stop=False)
                    pe.matmul(out, stat[0], mov[1], start=False, stop=False)
                    return pe.matmul(out, stat[0], mov[0], start=False, stop=last)

                def bank_free(e):
                    if e in (6, 7, 8, 9):
                        pe.wait_ge((act_evac, dve_evac)[e % 2], 1 if e < 8 else 4)
                    elif e >= 10:
                        pe.wait_ge((act_evac, dve_evac)[e % 2], e // 2 - 3)

                pe.wait_ge(lo_ready, 2)
                for s in range(NSEQ):
                    tiles = range(s * SB, (s + 1) * SB)
                    for k in range(KT):
                        pe.wait_ge(h_ready, s * KT + k + 1)
                        for tt in tiles:
                            if k == 0:
                                bank_free(tt)
                            tok = slice(tt * P, (tt + 1) * P)
                            mm3 = passes3(ps[:, evac_bank(tt), 0:256], (hh[:, k, tok], hl[:, k, tok]),
                                          (whi[:, 0:2, k, :], wlo[:, 0:2, k, :]), k == 0, k == KT - 1)
                            if k == KT - 1:
                                mm3.then_inc(proj_ready, 1)
                pe.wait_ge(proj_ready, TT)
                pe.sem_inc(unit_used, 2)

                for c in range(1, len(TOK_COLS)):
                    pe.wait_ge(lo_ready, 2 * c + 2)
                    slot = 2 * c % SPLIT
                    for tt in range(TT):
                        e = c * TT + tt
                        bank_free(e)
                        for k in range(KT):
                            tok = slice(tt * P, (tt + 1) * P)
                            mm3 = passes3(ps[:, evac_bank(e), 0:256], (hh[:, k, tok], hl[:, k, tok]),
                                          (whi[:, slot:slot + 2, k, :], wlo[:, slot:slot + 2, k, :]),
                                          k == 0, k == KT - 1)
                        mm3.then_inc(proj_ready, 1)
                        if tt == TT - 1:
                            pe.wait_ge(proj_ready, e + 1)
                            pe.sem_inc(unit_used, 2)

                for u in range(N_TOK, N_IN):
                    pe.wait_ge(lo_ready, u + 1)
                    for s in range(NSEQ):
                        e = E_TOK + 2 * (u - N_TOK) + s
                        bank_free(e)
                        tok = slice(s * SEQ, (s + 1) * SEQ)
                        for k in range(KT):
                            mm3 = passes3(ps[:, e % 8, :], (whi[:, u % SPLIT, k, :], wlo[:, u % SPLIT, k, :]),
                                          (hh[:, k, tok], hl[:, k, tok]), k == 0, k == KT - 1)
                        mm3.then_inc(proj_ready, 1)
                    pe.wait_ge(proj_ready, e + 1)
                    pe.sem_inc(unit_used, 1)

                pe.wait_ge(act_evac, E_ALL // 2)
                pe.wait_ge(dve_evac, E_ALL // 2)
                def gate_inputs(d, j, bank):
                    pe.matmul(ps[:, bank, :], w2s[:, d, j // 2 * P:(j // 2 + 1) * P],
                              small[:, j % 2 * SEQ:(j % 2 + 1) * SEQ], start=True, stop=True).then_inc(z_psum, 1)

                for tt in range(TT):
                    pe.wait_ge(qk_lo, 2 * tt + 2)
                    if tt >= 2:
                        pe.wait_ge(qkT_act, 2 * (tt - 1))
                        pe.wait_ge(qkT_dve, tt - 1)
                    for b in range(3):
                        for i in range(4):
                            src = (qd[:, tt % 2, 4 * b + i, :, :] if b < 2 else kd[:, tt % 2, i // 2, i % 2, :, :])
                            tr = pe.transpose(ps[:, tt % 2 * 3 + b, i * P:(i + 1) * P],
                                              src.rearrange("p r d -> p (r d)").bitcast(F32), ident[:])
                        tr.then_inc(qkT_psum, 1)
                    if tt in Z_AFTER:
                        pe.wait_ge(gla_consts, 16)
                        n = Z_AFTER.index(tt)
                        if n:
                            pe.wait_ge(z_taken, 2 * n)
                        gate_inputs(n // 2, n % 2 * 2, 6)
                        gate_inputs(n // 2, n % 2 * 2 + 1, 7)
                for i in range(N_ATT + 3):
                    if i < N_ATT:
                        s, h, qt = i // (AH * SB), i // SB % AH, i % SB
                        if i == 0:
                            pe.wait_ge(qkT_act, 2 * TT)
                            pe.wait_ge(qkT_dve, TT)
                        if i >= 3:
                            pe.wait_ge(prob_ready, i - 2)
                        q = qs[:, h, s * SEQ + qt * P:s * SEQ + (qt + 1) * P]
                        keys = slice(s * SEQ, (s + 1) * SEQ)
                        pe.matmul(ps[:, 3 + i % 3, :], q, ks[:, 1, h // 4, keys], start=True, stop=False)
                        pe.matmul(ps[:, 3 + i % 3, :], q, ks[:, 0, h // 4, keys], start=False,
                                  stop=True).then_inc(sc_ready, 1)
                    if 2 <= i < N_ATT + 2:
                        v = i - 2
                        pe.wait_ge(prob_ready, v + 1)
                        if v == 0:
                            pe.wait_ge(z_taken, 8)
                        if v >= 2:
                            pe.wait_ge((pT_even, pT_odd)[v % 2], v // 2)
                        for kt in range(SB):
                            tr = pe.transpose(ps[:, 6 + v % 2, kt * P:(kt + 1) * P],
                                              prob[:, v % 3, kt * P:(kt + 1) * P], ident[:])
                        tr.then_inc(pT_psum, 1)
                    if i >= 3:
                        v = i - 3
                        s, h = v // (AH * SB), v // SB % AH
                        pe.wait_ge((pT_even, pT_odd)[v % 2], v // 2 + 1)
                        if v >= 3:
                            pe.wait_ge(ao_done, v - 2)
                        c0 = AV + h // 4 * HD
                        for kt in range(SB):
                            mm = pe.matmul(ps[:, v % 3, 0:HD], pT[:, v % 2, kt, :],
                                           tokA[:, s * SB + kt, c0:c0 + HD], start=(kt == 0), stop=(kt == SB - 1))
                        mm.then_inc(ao_psum, 1)

                pe.wait_ge(ao_done, N_ATT)

                def state_keys(d, ht):
                    r = d * 2 + ht
                    pe.wait_ge(gx_used, 4 * r + 2)
                    for b in range(2):
                        if 2 * r + b >= 2:
                            pe.wait_ge(ktok_ready, 2 * r + b - 1)
                        for i in range(4):
                            tt = b * 4 + i
                            tr = pe.transpose(ps[:, 4 + b, i * P:(i + 1) * P], ktil[:, tt * P:(tt + 1) * P], ident[:])
                        tr.then_inc(ktil_psum, 1)

                def chunk_states(d, c):
                    ci = step_of(d, c)
                    n = d * (NCH - 1) + c
                    if n >= 2:
                        pe.wait_ge(state_ready, n - 1)
                    rows = slice(ci % 4 * CH, (ci % 4 + 1) * CH)
                    for s in range(NSEQ):
                        tt = s * SB + ci // 4
                        for h in range(GH):
                            half = slice(h % 2 * HD, (h % 2 + 1) * HD)
                            c0 = (s * 2 + h // 2) * HD
                            mm = pe.matmul(ps[half, 6 + n % 2, c0:c0 + HD],
                                           ktok[d][rows, tt, h * HD:(h + 1) * HD],
                                           gv[rows, tt, h * HD:(h + 1) * HD], start=True, stop=True)
                    mm.then_inc(kv_psum, 1)

                def scores(d, i):
                    n = d * TT + i
                    if i >= 2:
                        pe.wait_ge(gat_ready, n - 1)
                    tt = tile_of(d, i)
                    tok = slice(tt * P, (tt + 1) * P)
                    for h in range(GH):
                        half = slice(h % 2 * HD, (h % 2 + 1) * HD)
                        mm = pe.matmul(ps[:, i % 2 * 2 + h % 2, h // 2 * P:(h // 2 + 1) * P],
                                       khat[d][half, h // 2, tok], qhat[d][half, h // 2, tok], start=True, stop=True)
                    mm.then_inc(gat_psum, 1)

                def output_tile(d, i):
                    if i + 1 < TT:
                        scores(d, i + 1)
                    n = d * TT + i
                    tt = tile_of(d, i)
                    s = tt // SB
                    pe.wait_ge(state_ready, d * (NCH - 1) + min(NCH - 1, 4 * (i // 2) + 3))
                    pe.wait_ge(gat_ready, n + 1)
                    if n >= 1:
                        pe.wait_ge(go_evac, n)
                    for h in range(GH):
                        half = slice(h % 2 * HD, (h % 2 + 1) * HD)
                        bank, cols = 4 + h % 2, slice(h // 2 * HD, (h // 2 + 1) * HD)
                        mm = pe.matmul(ps[:, bank, cols], attT[:, i % 2, h % 2, h // 2, :],
                                       gv[:, tt, h * HD:(h + 1) * HD],
                                       start=True, stop=False, skip_group_check=True)
                        for r in range(4):
                            c = step_of(d, tt % SB * 4 + r)
                            t0 = tt * P + r * CH
                            mm = pe.matmul(ps[r * CH:(r + 1) * CH, bank, cols],
                                           qtil[d][half, h // 2, t0:t0 + CH], st[half, c, s, h // 2, :],
                                           start=False, stop=True, skip_group_check=True)
                    mm.then_inc(go_psum, 1)

                state_keys(0, 0)
                state_keys(0, 1)
                pe.wait_ge(ktok_ready, 4)
                for d in range(2):
                    if d == 1:
                        pe.wait_ge(go_evac, TT)
                        pe.wait_ge(gx_used, 16)
                        pe.wait_ge(ktok_ready, 8)
                    for c in range(NCH - 1):
                        chunk_states(d, c)
                        if c == 0:
                            pe.wait_ge(gx_used, 8)
                            scores(d, 0)
                        for i in range(TT):
                            if TILES_AFTER[i] == c:
                                if d == 0 and i == KEY_TILES:
                                    pe.wait_ge(ktok_ready, 6)
                                output_tile(d, i)
                        if d == 0 and c == KEYS_AT:
                            pe.wait_ge(go_evac, KEY_TILES)
                            state_keys(1, 0)
                    if d == 0:
                        pe.wait_ge(go_evac, TT)
                        state_keys(1, 1)

                pe.wait_ge(go_evac, 2 * TT)
                pe.wait_ge(ml_consts, 32)
                pe.wait_ge(rc_ready, 1)
                for i, src in enumerate((Cr, mm_rows)):
                    for tt in range(TT):
                        tr = pe.transpose(ps[:, i, tt * GROWS:(tt + 1) * GROWS],
                                          src[:, tt * P:(tt + 1) * P], ident[0:GROWS, 0:GROWS])
                    tr.then_inc(ct_psum, 1)
                pe.wait_ge(ct_ready, 2)
                pe.wait_ge(sel_ready, 1)
                pe.wait_ge(R_split, 1)

                def row_terms(w):
                    _, h, tok, _, _ = head_rows(w)
                    for d in range(2):
                        if w >= 1:
                            pe.wait_ge(dt_ready, 2 * SB * w)
                        pe.matmul(ps[:, 4 + d, :], selr[:, d * MH + h, :], Rs[:, tok], start=True,
                                  stop=True).then_inc(rb_psum, 1)

                def key_query(w):
                    pe.wait_ge(stk_lo, 3 * (w + 1))
                    for i in range(SB):
                        if w >= 1:
                            pe.wait_ge(wt_ready, 2 * SB * (w - 1) + 2 * i + 2)
                        k = ks2[:, w % 2, i * P:(i + 1) * P]
                        pe.matmul(ps[:, i, :], k, ql2[:, w % 2, :], start=True, stop=False)
                        pe.matmul(ps[:, i, :], k, qh2[:, w % 2, :], start=False, stop=True).then_inc(qk_psum, 1)

                row_terms(0)
                key_query(0)
                for w in range(N_ML):
                    s, h = w // MH, w % MH
                    if w + 1 < N_ML:
                        row_terms(w + 1)
                        key_query(w + 1)
                    if w >= 1:
                        pe.wait_ge(ml_evac, w)
                    pe.wait_ge(wt_ready, 2 * SB * (w + 1))
                    for d in range(2):
                        for j in range(SB):
                            keys = range(j + 1) if d == 0 else range(j, SB)
                            for i in keys:
                                mm = pe.matmul(ps[:, 6 + d, j * (HD + 1):(j + 1) * (HD + 1)],
                                               Dts[w % 2][:, d, i, j * P:(j + 1) * P], vaug[:, s * SB + i, h, :],
                                               start=(i == keys[0]), stop=(i == keys[-1]))
                    mm.then_inc(num_psum, 1)

                pe.wait_ge(ml_done, 1)
                for tt in range(TT):
                    for b in range(2):
                        if tt >= 2:
                            pe.wait_ge(mixl_ready, 3 * (tt - 2) + 1 + 2 * b)
                        for i in range(4):
                            src = (tokA[:, tt, i * P:(i + 1) * P] if b == 0 else
                                   (gg, co)[i // 2][:, tt, i % 2 * P:(i % 2 + 1) * P])
                            tr = pe.transpose(ps[:, 4 + tt % 2 * 2 + b, i * P:(i + 1) * P], src, ident[:])
                        tr.then_inc(mix_psum, 1)
                for o in range(KT):
                    u = N_IN + o
                    pe.wait_ge(lo_ready, u + 1)
                    if o >= 3:
                        pe.wait_ge(wo_done, o - 2)
                    for s in range(NSEQ):
                        if o == 0:
                            pe.wait_ge(mixl_ready, 3 * SB * (s + 1))
                        tok = slice(s * SEQ, (s + 1) * SEQ)
                        for k in range(KT):
                            mm3 = passes3(ps[:, o % 3 * 2 + s, :], (whi[:, u % SPLIT, k, :], wlo[:, u % SPLIT, k, :]),
                                          (hh[:, k, tok], hl[:, k, tok]), k == 0, k == KT - 1)
                    mm3.then_inc(wo_psum, 1)
                    pe.wait_ge(wo_psum, o + 1)
                    pe.sem_inc(unit_used, 1)

                sum_squares(6, sq_used, KT, ss_psum)
                spread(diag_ready, rinv_spread)
                pe.wait_ge(wo_done, KT)

                def up(kind, j):
                    pe.wait_ge(f_lo[kind], j + 1)
                    for s in range(NSEQ):
                        for k in range(KT):
                            mm3 = passes3(ps[:, 2 * kind + s, :], (whi[:, kind, k, :], wlo[:, kind, k, :]),
                                          (hh[:, k, s * SEQ:(s + 1) * SEQ], hl[:, k, s * SEQ:(s + 1) * SEQ]),
                                          k == 0, k == KT - 1)
                    mm3.then_inc(f_used[kind], 1)

                def down(j, first=False, last=False):
                    if last:
                        pe.wait_ge(g_conv, FT)
                    pe.wait_ge(f_lo[2], j + 1)
                    pe.wait_ge(actl_ready, j + 1)
                    for o in range(KT):
                        for s in range(NSEQ):
                            if not (first and o < 2):
                                pe.wait_ge(d_done, j * (NSEQ * KT) + (o * NSEQ + s - 3))
                            mm3 = passes3(ps[:, 4 + o % 2 * 2 + s, :], (whi[:, 2, o, :], wlo[:, 2, o, :]),
                                          (acth[:, s, :], actl[:, s, :]), True, True)
                            mm3.then_inc(d_psum, 1)
                    pe.wait_ge(d_psum, j * (NSEQ * KT) + NSEQ * KT)
                    pe.sem_inc(f_used[2], 1)

                for kind in range(2):
                    pe.wait_ge(f_lo[kind], 1)
                for s in range(NSEQ):
                    tok = slice(s * SEQ, (s + 1) * SEQ)
                    for k in range(KT):
                        pe.wait_ge(h_ready, (NSEQ + s) * KT + k + 1)
                        for kind in range(2):
                            mm3 = passes3(ps[:, 2 * kind + s, :], (whi[:, kind, k, :], wlo[:, kind, k, :]),
                                          (hh[:, k, tok], hl[:, k, tok]), k == 0, k == KT - 1)
                            if s == NSEQ - 1 and k == KT - 1:
                                mm3.then_inc(f_used[kind], 1)

                def iteration(j, first=False):
                    pe.wait_ge(g_conv, j)
                    up(0, j)
                    pe.wait_ge(v_conv, j)
                    up(1, j)
                    down(j - 1, first=first)

                iteration(1, first=True)
                with pe.Fori(2, FT) as j:
                    iteration(j)
                down(FT - 1, last=True)
                sum_squares(0, sq_used, 2 * KT, ss_psum)
                spread(diag_ready, rinv_spread, NSEQ)
                pe.wait_ge(rinv_spread, 2 * NSEQ)
                pe.sem_inc(layer_end, 1)
                pe.wait_ge(layer_go, l + 1)

        @block.scalar
        def _(act):
            act.wait_ge(ones_set, 2)

            def square(k, ready, used, count=0):
                if count + k >= 2:
                    act.wait_ge(used, count + k - 1)
                act.activation(sq[:, k % 2, :], x[:, k, :], ACT.Square).then_inc(ready, 1)

            def roots(bank, used, total, roots_ready):
                act.wait_ge(used, total)
                act.activation(rms[:], ps[:, bank, 0:TT], ACT.Sqrt, bias=eps[:], scale=1.0 / D).then_inc(roots_ready, 1)

            for k in range(KT):
                act.wait_ge(x_loaded[k], 16)
                square(k, first_sq_ready, first_sq_used)
            roots(0, first_ss_psum, 1, first_rms_ready)
            with act.Fori(0, DEPTH) as l:
                chain = [0]

                def link(ins):
                    chain[0] += 1
                    ins.then_inc(act_chain, 1)
                    act.wait_ge(act_chain, chain[0])

                def split_hi(n):
                    act.wait_ge(raw_full[n % RAW], 16 * (n // RAW + 1))
                    if n >= SPLIT:
                        act.wait_ge(unit_used, n - SPLIT + 1)
                    act.activation(whi[:, n % SPLIT, :, :], raw[:, n % RAW, :].rearrange("p (k c) -> p k c", k=KT),
                                   ACT.Copy).then_inc(hi_ready, 1)

                def evacuate(e):
                    if e == E_TOK:
                        act.wait_ge(rot_ready, TT)
                    act.wait_ge(proj_ready, e + 1)
                    dst, src = evac_source(e)
                    act.activation(dst, src, ACT.Copy).then_inc(act_evac, 1)

                def norm(n, units=None):
                    for s in range(NSEQ):
                        for k in range(KT):
                            i = (n * NSEQ + s) * KT + k
                            if units and s == 0 and k == 3:
                                units()
                            if n == 0 and s == 1 and k == 3:
                                evacuate(0)
                                evacuate(2)
                            act.wait_ge(hf_ready, i + 1)
                            act.activation(hh[:, k, s * SEQ:(s + 1) * SEQ], hf[:, i % 2, :], ACT.Copy)\
                               .then_inc(hh_ready, 1)

                def first_units():
                    split_hi(0)
                    split_hi(1)

                norm(0, first_units)
                split_hi(2)
                split_hi(3)
                act.wait_ge(h_ready, NSEQ * KT)

                for c in range(len(TOK_COLS)):
                    if c >= 1:
                        for u in (2 * c + 2, 2 * c + 3):
                            split_hi(u)
                    for e in range(c * TT, (c + 1) * TT, 2):
                        if e >= SB:
                            evacuate(e)
                        if e == C_ROT * TT:
                            act.wait_ge(qk_sums, 1)
                            act.activation(rqk[:], ssq[:], ACT.Sqrt, bias=eps[:], scale=1.0 / HD)\
                               .then_inc(qk_rms, 1)
                for u in range(N_TOK, N_IN):
                    for v in ([u + 2, u + 3] if u == N_TOK else [u + 3]):
                        if v < N_IN:
                            split_hi(v)
                    evacuate(E_TOK + 2 * (u - N_TOK))

                act.wait_ge(act_evac, E_ALL // 2)
                act.wait_ge(dve_evac, E_ALL // 2)
                for tt in range(TT + 1):
                    if tt < TT:
                        if tt >= 2:
                            act.wait_ge(qkT_psum, 3 * (tt - 1))
                        act.activation(qd[:, tt % 2, :, 0, :], tokA[:, tt, 0:AH * HD].rearrange("p (h d) -> p h d", h=AH),
                                       ACT.Copy).then_inc(qk_hi, 1)
                        act.activation(kd[:, tt % 2, 0, :, :, :],
                                       tokA[:, tt, AK:AV].rearrange("p (g d) -> p g d", g=KVH).unsqueeze(2)
                                       .to_broadcast([P, KVH, 2, HD]), ACT.Copy).then_inc(qk_hi, 1)
                    if tt >= 1:
                        u = tt - 1
                        tok = slice(u * P, (u + 1) * P)
                        for b, dst in ((0, qs[:, 0:4, tok]), (2, ks[:, :, :, tok].rearrange("p r g t -> p (r g) t"))):
                            act.wait_ge(qkT_psum, 3 * u + b + 1)
                            act.activation(dst, ps[:, u % 2 * 3 + b, :].rearrange("p (h t) -> p h t", h=4),
                                           ACT.Copy).then_inc(qkT_act, 1)
                        if u in Z_AFTER:
                            for n in (2 * Z_AFTER.index(u), 2 * Z_AFTER.index(u) + 1):
                                act.wait_ge(z_psum, n + 1)
                                d, ht = n // 4, n // 2 % 2
                                b0 = V_GB + 2 * d + ht
                                act.activation((G0, G1)[d][:, ht, n % 2 * SEQ:(n % 2 + 1) * SEQ], ps[:, 6 + n % 2, :],
                                               ACT.Identity, bias=vec[:, b0:b0 + 1]).then_inc(z_taken, 1)
                for i in range(N_ATT + 2):
                    if i < N_ATT:
                        act.wait_ge(nmx_ready, i + 1)
                        if i >= 3:
                            act.wait_ge(pT_psum, i - 2)
                        act.activation(prob[:, i % 3, :], ps[:, 3 + i % 3, :], ACT.Exp, bias=nmx[:, i:i + 1],
                                       accum_out=rsum[:, i:i + 1]).then_inc(prob_ready, 1)
                    d, z = i // 20, (G0, G1)[min(i // 20, 1)]
                    for ht in range(2):
                        if i % 20 == 6 and d < 2:
                            act.wait_ge(z_taken, 8)
                            if d == 1:
                                act.wait_ge(la_ready, 2)
                            act.activation(e0[:, ht, :], z[:, ht, :], ACT.Abs).then_inc(z_abs, 1)
                        elif i % 20 == 10 and d < 2:
                            act.wait_ge(z_abs, 4 * d + ht + 1)
                            act.activation(e0[:, ht, :], e0[:, ht, :], ACT.Exp, scale=-1.0).then_inc(z_abs, 1)
                        elif i % 20 == 14 and d < 2:
                            act.wait_ge(z_abs, 4 * d + 3 + ht)
                            act.activation(e0[:, ht, :], e0[:, ht, :], ACT.Ln, bias=ones[:, 0:1]).then_inc(ln_ready, 1)
                    v = i - 2
                    if v >= 0 and v % 2 == 1:
                        act.wait_ge(pT_psum, v + 1)
                        if v >= 2:
                            act.wait_ge(ao_psum, v - 1)
                        act.activation(pT[:, 1, :, :].rearrange("p k q -> p (k q)"), ps[:, 7, :], ACT.Copy)\
                           .then_inc(pT_odd, 1)

                act.wait_ge(ao_done, N_ATT)
                for d in range(2):
                    for ht in range(2):
                        r = d * 2 + ht
                        act.wait_ge(cum_ready, r + 1)
                        last = CH - 1 if d == 0 else 0
                        act.activation(aL[:, d, ht, :], Gs[d][:, ht, :].rearrange("p (c t) -> p c t", t=CH)[:, :, last],
                                       ACT.Exp, scale=1.0 / GLA_TAU).then_inc(aL_ready, 1)
                        for m, (src, sc) in enumerate(((Gs[d][:, ht, :], 1), (dml[:], 1), (dml[:], 1), (dml[:], -1))):
                            n = 4 * r + m
                            if m >= 1:
                                act.wait_ge(dml_ready, 2 * r + (1 if m == 1 else 2))
                            if n >= 2:
                                act.wait_ge(gx_used, n - 1)
                            act.activation(gx[:, m % 2, :], src, ACT.Exp, scale=sc / GLA_TAU).then_inc(gx_ready, 1)
                        for b in range(2):
                            act.wait_ge(ktil_psum, 2 * r + b + 1)
                            act.wait_ge(cum_ready, 4)
                            act.activation(ktok[d][:, 4 * b:4 * b + 4, ht * P:(ht + 1) * P],
                                           ps[:, 4 + b, :].rearrange("p (i c) -> p i c", i=4), ACT.Copy)\
                               .then_inc(ktok_ready, 1)
                act.wait_ge(yf_ready, 1)
                link(act.activation(fl[:], yf[:], ACT.Abs))
                link(act.activation(fl[:], fl[:], ACT.Exp, scale=-1.0))
                act.activation(fl[:], fl[:], ACT.Ln, bias=ones[0:GROWS, 0:1]).then_inc(fl_ready, 1)
                act.wait_ge(rc_ready, 1)
                act.activation(Rs[0:GROWS, :], Rr[:], ACT.Copy).then_inc(R_hi, 1)
                act.activation(gg[:], gg[:], ACT.Silu).then_inc(gsig_ready, 1)
                act.activation(co[:], co[:], ACT.Sigmoid).then_inc(msig_ready, 1)
                act.wait_ge(go_evac, 2 * TT)
                for hb in range(2):
                    act.activation(gx[:, hb, :].rearrange("p (t c) -> p t c", t=4), oacc[:, 4 * hb:4 * hb + 4, :],
                                   ACT.Square, scale=HD ** -0.5).then_inc(gsq_ready, 1)

                act.wait_ge(ml_consts, 32)
                act.activation(selr[:], sels, ACT.Copy).then_inc(sel_ready, 1)

                def stack_hi(w):
                    _, h, tok, rows, other = head_rows(w)
                    if w >= 2:
                        act.wait_ge(qk_psum, SB * (w - 1))
                    q, k = qkM[rows, h // 2, tok], qkM[rows, 2 + h // 2, tok]
                    act.activation(qh2[rows, w % 2, :], q, ACT.Copy).then_inc(stk_hi, 1)
                    act.activation(ks2[rows, w % 2, :], k, ACT.Copy).then_inc(stk_hi, 1)
                    act.activation(qh2[other, w % 2, :], q, ACT.Copy).then_inc(stk_hi, 1)

                stack_hi(0)
                act.wait_ge(gss_ready, 2)
                act.activation(gss[:, 1, :], gss[:, 0, :], ACT.Sqrt, bias=eps[:], scale=1.0 / HD)\
                   .then_inc(grms_ready, 1)
                act.wait_ge(ct_psum, 1)
                act.activation(CT[:], ps[:, 0, 0:TT * GROWS].rearrange("p (t r) -> p t r", t=TT), ACT.Copy)\
                   .then_inc(ct_ready, 1)
                act.wait_ge(ct_psum, 2)
                act.activation(EM[:], ps[:, 1, 0:TT * GROWS].rearrange("p (t r) -> p t r", t=TT), ACT.Exp,
                               scale=-1.0).then_inc(ct_ready, 1)
                act.wait_ge(ct_ready, 2)
                for w in range(N_ML):
                    s, h = w // MH, w % MH
                    if w + 1 < N_ML:
                        stack_hi(w + 1)
                    if w >= 2:
                        act.wait_ge(num_psum, w - 1)
                    Dt = Dts[w % 2]
                    bias = lambda d, i: CT[:, s * SB + i, 32 * d + h:32 * d + h + 1]
                    for d in range(2):
                        act.wait_ge(mr_ready, 2 * w + d + 1)
                        for i in range(SB):
                            rest = slice((i + 1) * P, SEQ) if d == 0 else slice(0, i * P)
                            if rest.stop > rest.start:
                                act.activation(Dt[:, d, i, rest], ps[:, 4 + d, rest], ACT.Exp, bias=bias(d, i))
                    for i in range(SB):
                        for d in range(2):
                            own = slice(i * P, (i + 1) * P)
                            act.activation(Dt[:, d, i, own], mR[:, d, own], ACT.Exp, bias=bias(d, i))\
                               .then_inc(dt_ready, 1)
                act.wait_ge(heads_gated, 1)
                for hb in range(2):
                    sq_to = Dt0[:, hb, 0:2, :].rearrange("p a b -> p (a b)").rearrange("p (t c) -> p t c", t=4)
                    act.activation(sq_to, co[:, 4 * hb:4 * hb + 4, :], ACT.Square).then_inc(msq_ready, 1)
                act.wait_ge(mss_ready, 2)
                act.activation(mss[:, 1, :], mss[:, 0, :], ACT.Sqrt, bias=eps[:], scale=1.0 / HD)\
                   .then_inc(mrms_ready, 1)

                act.wait_ge(ml_done, 1)
                split_hi(N_IN)
                for tt in range(TT):
                    tok = slice(tt * P, (tt + 1) * P)
                    bank = 4 + tt % 2 * 2
                    act.wait_ge(mix_psum, 2 * tt + 1)
                    act.activation(hh[:, 0:4, tok], ps[:, bank, :].rearrange("p (i t) -> p i t", i=4), ACT.Copy)\
                       .then_inc(mixh_ready, 1)
                    act.wait_ge(mix_psum, 2 * tt + 2)
                    for i, g in enumerate((V_GLAN, V_MLN)):
                        act.activation(hh[:, 4 + 2 * i:6 + 2 * i, tok],
                                       ps[:, bank + 1, 2 * i * P:(2 * i + 2) * P].rearrange("p (i t) -> p i t", i=2),
                                       ACT.Copy, scale=vec[:, g:g + 1]).then_inc(mixh_ready, 1)
                for u in range(N_IN + 1, N_IN + SPLIT):
                    split_hi(u)
                for o in range(KT):
                    if o + SPLIT < KT:
                        split_hi(N_IN + SPLIT + o)
                    act.wait_ge(wo_done, o + 1)
                    square(o, sq_ready, sq_used)


                def ffn_hi(kind, j):
                    act.wait_ge(f_full[kind], 16 * (j + 1))
                    act.activation(whi[:, kind, :, :], raw[:, kind, :].rearrange("p (k c) -> p k c", k=KT),
                                   ACT.Copy).then_inc(f_hi[kind], 1)

                act.wait_ge(unit_used, N_UNITS)
                for kind in (0, 1):
                    ffn_hi(kind, 0)
                roots(6, ss_psum, 1, rms_ready)
                norm(1)
                act.wait_ge(h_ready, 2 * NSEQ * KT)
                act.wait_ge(conv_loaded, 16)

                def iteration(j, first=False, last=False):
                    if not first:
                        act.wait_ge(v_conv, j)
                    act.activation(cw[:], convs[:, j, :], ACT.Copy).then_inc(cw_ready, 1)
                    act.wait_ge(cw_ready, j + 1)
                    act.wait_ge(f_used[0], j + 1)
                    act.activation(accg[:], ps[:, 0:2, :], ACT.Identity, bias=cw[:, 3:4], scale=cw[:, 1:2])\
                       .then_inc(g_init, 1)
                    if not last:
                        ffn_hi(0, j + 1)
                    if not first:
                        act.wait_ge(act_ready, j)
                    act.wait_ge(g_conv, j + 1)
                    act.activation(sil[:], accg[:], ACT.Silu).then_inc(sil_ready, 1)
                    act.wait_ge(f_used[1], j + 1)
                    if not first:
                        act.wait_ge(actl_ready, j)
                    act.activation(accv[:], ps[:, 2:4, :], ACT.Identity, bias=cw[:, 7:8], scale=cw[:, 5:6])\
                       .then_inc(v_init, 1)
                    if not last:
                        ffn_hi(1, j + 1)
                    if not first:
                        act.wait_ge(f_used[2], j)
                    ffn_hi(2, j)
                    act.wait_ge(act_ready, j + 1)
                    act.activation(acth[:], accv[:], ACT.Copy).then_inc(acth_ready, 1)
                    act.wait_ge(sil_ready, j + 1)

                iteration(0, first=True)
                with act.Fori(1, FT - 1) as j:
                    iteration(j)
                iteration(FT - 1, last=True)
                for k in range(KT):
                    act.wait_ge(d_done, ((FT - 1) * KT + k + 1) * NSEQ)
                    square(k, sq_ready, sq_used, KT)
                roots(0, ss_psum, 2, rms_ready)
                act.sem_inc(layer_end, 1)
                act.wait_ge(layer_go, l + 1)

        @block.vector
        def _(dve):
            dve.memset(ones[:], 1.0).then_inc(ones_set, 1)
            dve.memset(eps[:], EPS).then_inc(ones_set, 1)
            dve.wait_ge(ones_set, 2)
            dve.wait_ge(consts_loaded, 48)

            def add_squares(k, ready, used, count=0):
                dve.wait_ge(ready, count + k + 1)
                if k == 0:
                    ins = dve.tensor_copy(sqsum[:], sq[:, 0, :])
                else:
                    dve.wait_ge(used, count + k)
                    ins = dve.tensor_tensor(sqsum[:], sqsum[:], sq[:, k % 2, :], ALU.add)
                ins.then_inc(used, 1)

            for k in range(KT):
                add_squares(k, first_sq_ready, first_sq_used)

            def diagonals(rms_there, total, rinv_done, ready):
                dve.wait_ge(rms_there, total)
                dve.reciprocal(rinv[:], rms[:]).then_inc(rinv_done, 1)
                dve.wait_ge(rinv_done, total)
                for s in range(NSEQ):
                    tiles = slice(s * SB, (s + 1) * SB)
                    dve.tensor_tensor(diag[:, tiles, :], ident[:].unsqueeze(1).to_broadcast([P, SB, P]),
                                      rinv[:, tiles].unsqueeze(2).to_broadcast([P, SB, P]), ALU.mult).then_inc(ready, 1)

            diagonals(first_rms_ready, 1, first_rinv_ready, first_diag_ready)
            dve.wait_ge(first_rinv_spread, NSEQ)
            with dve.Fori(0, DEPTH) as l:
                chain = [0]

                def link(ins):
                    chain[0] += 1
                    ins.then_inc(dve_chain, 1)
                    dve.wait_ge(dve_chain, chain[0])

                def split_lo(n):
                    dve.wait_ge(hi_ready, n + 1)
                    dve.tensor_tensor(wlo[:, n % SPLIT, :, :],
                                      raw[:, n % RAW, :].rearrange("p (k c) -> p k c", k=KT),
                                      whi[:, n % SPLIT, :, :].bitcast(F32), ALU.subtract).then_inc(lo_ready, 1)

                def evacuate(e):
                    if e == E_TOK + 1:
                        dve.wait_ge(rot_ready, TT)
                    dve.wait_ge(proj_ready, e + 1)
                    dst, src = evac_source(e)
                    dve.tensor_copy(dst, src).then_inc(dve_evac, 1)

                def norm(n, gain, units=None):
                    if n == 1:
                        diagonals(rms_ready, 1, rinv_ready, diag_ready)
                    for s in range(NSEQ):
                        if n == 1:
                            dve.wait_ge(rinv_spread, s + 1)
                        tok = slice(s * SEQ, (s + 1) * SEQ)
                        for k in range(KT + 1):
                            i = (n * NSEQ + s) * KT + k
                            if units and s == 0 and k == 3:
                                units()
                            if n == 0 and s == 1 and k == 3:
                                evacuate(1)
                                evacuate(3)
                            if k < KT:
                                if i >= 2:
                                    dve.wait_ge(h_ready, i - 1)
                                dve.scalar_tensor_tensor(hf[:, i % 2, :], x[:, k, tok], vec[:, gain + k:gain + k + 1],
                                                         ps[:, 6 + s, :], ALU.mult, ALU.mult).then_inc(hf_ready, 1)
                            if k >= 1:
                                dve.wait_ge(hh_ready, i)
                                dve.tensor_tensor(hl[:, k - 1, tok], hf[:, (i - 1) % 2, :],
                                                  hh[:, k - 1, tok].bitcast(F32), ALU.subtract).then_inc(h_ready, 1)

                def first_units():
                    split_lo(0)
                    split_lo(1)

                dve.wait_ge(vec_loaded, 16)
                norm(0, V_MIX, first_units)
                split_lo(2)
                split_lo(3)
                dve.wait_ge(h_ready, NSEQ * KT)
                link(dve.memset(vaug[:, :, :, HD:HD + 1], 1.0))

                def rotary_tables():
                    dve.wait_ge(att_consts, 48)
                    for tab, base in ((tabc, ropec), (tabs, ropes)):
                        for g, (h0, nh) in enumerate(((0, AH), (AH, KVH))):
                            shape = [P, SB, nh, HD]
                            link(dve.tensor_tensor(
                                tab[:, :, h0:h0 + nh, :],
                                base[:].unsqueeze(2).to_broadcast(shape),
                                qkgain[:, g:g + 1, :].unsqueeze(1).to_broadcast(shape), ALU.mult))

                def head_squares(tt):
                    qk = tokA[:, tt, 0:NQK * HD]
                    link(dve.tensor_tensor(t1[:], qk, qk, ALU.mult))
                    link(dve.tensor_reduce(ssq[:, tt, :], t1[:].rearrange("p (h d) -> p h d", h=NQK), AX_X, ALU.add))

                def head_rms():
                    dve.wait_ge(qk_rms, 1)
                    link(dve.reciprocal(rqk[:], rqk[:]))
                    link(dve.tensor_scalar(rqk[:, :, AH:NQK], rqk[:, :, AH:NQK], HD ** -0.5, None, ALU.mult))

                def rotate(tt):
                    qk = tokA[:, tt, 0:NQK * HD]
                    pairs = lambda t: t[:].rearrange("p (a r f) -> p a r f", r=2, f=HD // 4)
                    heads = "p (h d) -> p h d"
                    link(dve.tensor_tensor(t2[:], qk, tabs[:, tt % SB, :, :].rearrange("p h d -> p (h d)"), ALU.mult))
                    link(dve.tensor_tensor(t1[:], qk, tabc[:, tt % SB, :, :].rearrange("p h d -> p (h d)"), ALU.mult))
                    link(dve.tensor_tensor(pairs(t1), pairs(t1), pairs(t2)[:, :, ::-1, :], ALU.add))
                    dve.tensor_tensor(qk.rearrange(heads, h=NQK), t1[:].rearrange(heads, h=NQK),
                                      rqk[:, tt, :].unsqueeze(2).to_broadcast([P, NQK, HD]), ALU.mult)\
                       .then_inc(rot_ready, 1)
                    dve.wait_ge(rot_ready, tt + 1)

                for c in range(len(TOK_COLS)):
                    if c >= 1:
                        for u in (2 * c + 2, 2 * c + 3):
                            split_lo(u)
                    for i, e in enumerate(range(c * TT + 1, (c + 1) * TT, 2)):
                        if e >= SB:
                            evacuate(e)
                        if c == C_ROT - 2 and i == 1:
                            rotary_tables()
                        if c == C_ROT - 1:
                            if i == 0:
                                dve.wait_ge(act_evac, (C_ROT - 1) * TT // 2)
                                dve.wait_ge(dve_evac, (C_ROT - 1) * TT // 2)
                            for tt in (2 * i, 2 * i + 1):
                                head_squares(tt)
                            if i == 3:
                                dve.sem_inc(qk_sums, 1)
                        if c >= C_ROT:
                            n = (c - C_ROT) * 4 + i
                            if n == 0:
                                head_rms()
                            elif n <= TT:
                                rotate(n - 1)
                for u in range(N_TOK, N_IN):
                    for v in ([u + 2, u + 3] if u == N_TOK else [u + 3]):
                        if v < N_IN:
                            split_lo(v)
                    evacuate(E_TOK + 2 * (u - N_TOK) + 1)

                dve.wait_ge(act_evac, E_ALL // 2)
                dve.wait_ge(dve_evac, E_ALL // 2)
                for tt in range(TT + 1):
                    if tt < TT:
                        dve.wait_ge(qk_hi, 2 * tt + 1)
                        dve.tensor_tensor(qd[:, tt % 2, :, 1, :], tokA[:, tt, 0:AH * HD].rearrange("p (h d) -> p h d", h=AH),
                                          qd[:, tt % 2, :, 0, :].bitcast(F32), ALU.subtract).then_inc(qk_lo, 1)
                        dve.wait_ge(qk_hi, 2 * tt + 2)
                        dve.tensor_tensor(kd[:, tt % 2, 1, :, :, :],
                                          tokA[:, tt, AK:AV].rearrange("p (g d) -> p g d", g=KVH).unsqueeze(2)
                                          .to_broadcast([P, KVH, 2, HD]),
                                          kd[:, tt % 2, 0, :, :, :].bitcast(F32), ALU.subtract).then_inc(qk_lo, 1)
                    if tt >= 1:
                        u = tt - 1
                        dve.wait_ge(qkT_psum, 3 * u + 2)
                        dve.tensor_copy(qs[:, 4:8, u * P:(u + 1) * P],
                                        ps[:, u % 2 * 3 + 1, :].rearrange("p (h t) -> p h t", h=4)).then_inc(qkT_dve, 1)
                for i in range(N_ATT + 3):
                    if i < N_ATT:
                        dve.wait_ge(sc_ready, i + 1)
                        dve.tensor_reduce(nmx[:, i:i + 1], ps[:, 3 + i % 3, :], AX_X, ALU.max, negate=True)\
                           .then_inc(nmx_ready, 1)
                    if 2 <= i < N_ATT + 2:
                        v = i - 2
                        if v % 2 == 0:
                            dve.wait_ge(pT_psum, v + 1)
                            if v >= 2:
                                dve.wait_ge(ao_psum, v - 1)
                            dve.tensor_copy(pT[:, 0, :, :].rearrange("p k q -> p (k q)"), ps[:, 6, :])\
                               .then_inc(pT_even, 1)
                        dve.wait_ge(prob_ready, v + 1)
                        link(dve.reciprocal(rinvp[:, v:v + 1], rsum[:, v:v + 1]))
                    if i in (10, 11, 30, 31):
                        d, ht, z = i // 20, i % 2, (G0, G1)[i // 20]
                        dve.wait_ge(z_abs, 4 * d + ht + 1)
                        link(dve.tensor_scalar(z[:, ht, :], z[:, ht, :], 0.0, None, ALU.min))
                    elif i in (18, 19, 38, 39):
                        d, ht, z = i // 20, i % 2, (G0, G1)[i // 20]
                        dve.wait_ge(ln_ready, 2 * d + ht + 1)
                        dve.tensor_tensor(z[:, ht, :], z[:, ht, :], e0[:, ht, :], ALU.subtract).then_inc(la_ready, 1)
                        dve.wait_ge(la_ready, 2 * d + ht + 1)
                    elif 20 <= i < 24:
                        gq = G0[:, (i - 20) // 2, i % 2 * SEQ:(i % 2 + 1) * SEQ]
                        ins = dve.tensor_tensor_scan(gq, cmask[:], gq, 0.0, ALU.mult, ALU.add)
                        if i % 2:
                            ins.then_inc(cum_ready, 1)
                        else:
                            link(ins)
                    if i >= 3:
                        v = i - 3
                        s, h, qt = v // (AH * SB), v // SB % AH, v % SB
                        dve.wait_ge(ao_psum, v + 1)
                        dve.tensor_scalar(tokA[:, s * SB + qt, h * HD:(h + 1) * HD], ps[:, v % 3, 0:HD],
                                          rinvp[:, v:v + 1], None, ALU.mult).then_inc(ao_done, 1)

                dve.wait_ge(ao_done, N_ATT)
                dve.wait_ge(gla_consts, 16)
                link(dve.memset(attT[:], 0.0))

                def backward_decays():
                    for ht in range(2):
                        for s in range(NSEQ):
                            tok = slice(s * SEQ, (s + 1) * SEQ)
                            ins = dve.tensor_tensor_scan(G[:, ht, tok][:, ::-1], cmask[:], G1[:, ht, tok][:, ::-1], 0.0,
                                                         ALU.mult, ALU.add)
                            if s == 0:
                                link(ins)
                            else:
                                ins.then_inc(cum_ready, 1)
                                dve.wait_ge(cum_ready, 2 + ht + 1)

                def decay_from(d, ht, what):
                    r = d * 2 + ht
                    mid, last = (CH // 2 - 1, CH - 1) if d == 0 else (CH // 2, 0)
                    gc = Gs[d][:, ht, :].rearrange("p (c t) -> p c t", t=CH)
                    dv = dml[:].rearrange("p (c t) -> p c t", t=CH)
                    shape = [P, NSEQ * NCH, CH]
                    if what == 0:
                        if r >= 1:
                            dve.wait_ge(gx_ready, 4 * r)
                        ins = dve.tensor_tensor(dv, gc[:, :, last:last + 1].to_broadcast(shape), gc, ALU.subtract)
                    else:
                        dve.wait_ge(gx_ready, 4 * r + 2)
                        ins = dve.tensor_tensor(dv, gc, gc[:, :, mid:mid + 1].to_broadcast(shape), ALU.subtract)
                    ins.then_inc(dml_ready, 1)

                def scaled(d, ht, m):
                    r = d * 2 + ht
                    n = 4 * r + m
                    q, k = qkG[:, ht, :], qkG[:, 2 + ht, :]
                    dst, src = ((qtil[d][:, ht, :], q), (ktil[:], k), (qhat[d][:, ht, :], q), (khat[d][:, ht, :], k))[m]
                    dve.wait_ge(gx_ready, n + 1)
                    if m == 1 and r >= 1:
                        dve.wait_ge(ktil_psum, 2 * r)
                    dve.tensor_tensor(dst, src, gx[:, m % 2, :], ALU.mult).then_inc(gx_used, 1)
                    dve.wait_ge(gx_used, n + 1)

                def backward_gates(c):
                    if c == 0:
                        decay_from(1, 0, 0)
                        scaled(1, 0, 0)
                    elif c == 1:
                        scaled(1, 0, 1)
                        decay_from(1, 0, 1)
                    elif c == 2:
                        scaled(1, 0, 2)
                    elif c == 3:
                        scaled(1, 0, 3)
                        decay_from(1, 1, 0)
                    elif c == KEYS_AT + 1:
                        scaled(1, 1, 0)
                    elif c == KEYS_AT + 2:
                        scaled(1, 1, 1)
                        decay_from(1, 1, 1)
                    elif c == KEYS_AT + 3:
                        scaled(1, 1, 2)
                    elif c == KEYS_AT + 4:
                        scaled(1, 1, 3)

                def mlstm_gates(c):
                    if c == 0:
                        dve.wait_ge(gx_ready, 16)
                        dve.wait_ge(aL_ready, 4)
                        dve.wait_ge(ktil_psum, 8)
                        dve.tensor_scalar(yf[:], small[64:64 + GROWS, :], vec[64:64 + GROWS, V_GBF:V_GBF + 1], None,
                                          ALU.add).then_inc(yf_ready, 1)
                    elif c == 1:
                        link(dve.tensor_scalar(ri[:], small[0:GROWS, :], vec[0:GROWS, V_GBI:V_GBI + 1], None, ALU.add))
                    elif c == 2:
                        link(dve.memset(Fc[:], 0.0))
                    elif c == 3:
                        link(dve.memset(mm_rows[:], 0.0))
                        link(dve.tensor_copy(Rs[32:64, :], ident[32:64, 64:65].to_broadcast([32, T])))
                    elif c == 4:
                        dve.wait_ge(yf_ready, 1)
                        dve.wait_ge(fl_ready, 1)
                        link(dve.scalar_tensor_tensor(fl[:], yf[:], 0.0, fl[:], ALU.min, ALU.subtract))
                    elif c < 13:
                        d, s, running_max = (c - 5) // 4, (c - 5) // 2 % 2, (c - 5) % 2
                        rows, tok = slice(32 * d, 32 * d + MH), slice(s * SEQ, (s + 1) * SEQ)
                        rev = slice(None, None, -1) if d else slice(None)
                        lf, ig = fl[rows, tok][:, rev], ri[rows, tok][:, rev]
                        if running_max:
                            link(dve.tensor_tensor_scan(mm_rows[rows, tok][:, rev], lf, ig, 0.0, ALU.add, ALU.max))
                        else:
                            link(dve.tensor_tensor_scan(Fc[rows, tok][:, rev], ones[rows, 0:1].to_broadcast([MH, SEQ]),
                                                        lf, 0.0, ALU.mult, ALU.add))
                    elif c == 13:
                        link(dve.tensor_tensor(Rr[:], Fc[:], mm_rows[:], ALU.subtract))
                    else:
                        dve.tensor_tensor(Cr[:], ri[:], Fc[:], ALU.subtract).then_inc(rc_ready, 1)

                def mask_scores(d, i):
                    n = d * TT + i
                    dve.wait_ge(gat_psum, n + 1)
                    if i >= 2:
                        dve.wait_ge(go_psum, n - 1)
                    dve.copy_predicated(attT[:, i % 2, :, :, :],
                                        gam[:, d:d + 1, :].unsqueeze(1).to_broadcast([P, 2, 2, P]),
                                        ps[:, i % 2 * 2:i % 2 * 2 + 2, 0:2 * P].rearrange("p r (q t) -> p r q t", q=2))\
                       .then_inc(gat_ready, 1)

                def take_output(d, i):
                    dve.wait_ge(go_psum, d * TT + i + 1)
                    got = ps[:, 4:6, 0:2 * HD].rearrange("p r (q d) -> p r q d", q=2)
                    acc = oacc[:, tile_of(d, i), :].rearrange("p (q r d) -> p r q d", q=2, r=2)
                    if d == 0:
                        dve.tensor_copy(acc, got).then_inc(go_evac, 1)
                    else:
                        dve.tensor_tensor(acc, acc, got, ALU.add).then_inc(go_evac, 1)

                dve.wait_ge(cum_ready, 2)
                backward_decays()
                for ht in range(2):
                    decay_from(0, ht, 0)
                    scaled(0, ht, 0)
                    scaled(0, ht, 1)
                    decay_from(0, ht, 1)
                    scaled(0, ht, 2)
                    scaled(0, ht, 3)
                for d in range(2):
                    if d == 1:
                        link(dve.memset(attT[:], 0.0))
                    dve.wait_ge(aL_ready, 2 * d + 2)
                    link(dve.memset(st[:, 0, :, :, :], 0.0))
                    for c in range(NCH - 1):
                        ci = step_of(d, c)
                        n = d * (NCH - 1) + c
                        decay = aL[:, d, :, :].rearrange("p h (s c) -> p s h c", s=NSEQ)[:, :, :, ci:ci + 1]
                        link(dve.tensor_tensor(gtmp[:].rearrange("p (s h e) -> p s h e", s=2, h=2), st[:, c, :, :, :],
                                               decay.to_broadcast([P, NSEQ, 2, HD]), ALU.mult))
                        dve.wait_ge(kv_psum, n + 1)
                        dve.tensor_tensor(st[:, c + 1, :, :, :].rearrange("p s h e -> p (s h e)"), gtmp[:],
                                          ps[:, 6 + n % 2, 0:256], ALU.add).then_inc(state_ready, 1)
                        dve.wait_ge(state_ready, n + 1)
                        (backward_gates, mlstm_gates)[d](c)
                        if c == 1:
                            mask_scores(d, 0)
                        for i in range(TT):
                            if TILES_AFTER[i] == c:
                                if i + 1 < TT:
                                    mask_scores(d, i + 1)
                                take_output(d, i)
                    dve.wait_ge(go_evac, (d + 1) * TT)

                dve.wait_ge(R_hi, 1)
                dve.wait_ge(rc_ready, 1)
                dve.tensor_tensor(Rs[64:RROWS, :], Rr[:], Rs[0:GROWS, :].bitcast(F32), ALU.subtract).then_inc(R_split, 1)

                def stack_lo(w):
                    _, h, tok, rows, other = head_rows(w)
                    q, k = qkM[rows, h // 2, tok], qkM[rows, 2 + h // 2, tok]
                    qh, kh = qh2[rows, w % 2, :].bitcast(F32), ks2[rows, w % 2, :].bitcast(F32)
                    dve.wait_ge(stk_hi, 3 * (w + 1))
                    dve.tensor_tensor(ql2[rows, w % 2, :], q, qh, ALU.subtract).then_inc(stk_lo, 1)
                    dve.tensor_tensor(ql2[other, w % 2, :], q, qh, ALU.subtract).then_inc(stk_lo, 1)
                    dve.tensor_tensor(ks2[other, w % 2, :], k, kh, ALU.subtract).then_inc(stk_lo, 1)

                def gla_norm():
                    oa = oacc[:].rearrange("p t (h d) -> p (t h) d", d=HD)
                    link(dve.tensor_tensor(oa, oa, gss[:, 0, :].unsqueeze(2).to_broadcast([P, TT * GH, HD]), ALU.mult))
                    flat = "p t c -> p (t c)"
                    dve.tensor_tensor(gg[:].rearrange(flat), oacc[:].rearrange(flat), gg[:].rearrange(flat),
                                      ALU.mult).then_inc(gla_done, 1)

                for hb in range(2):
                    dve.wait_ge(gsq_ready, hb + 1)
                    dve.tensor_reduce(gss[:, 0, hb * 16:(hb + 1) * 16],
                                      gx[:, hb, :].rearrange("p (a d) -> p a d", d=HD), AX_X, ALU.add)\
                       .then_inc(gss_ready, 1)
                stack_lo(0)
                dve.wait_ge(grms_ready, 1)
                link(dve.reciprocal(gss[:, 0, :], gss[:, 1, :]))
                link(dve.tensor_scalar(gss[:, 0, :], gss[:, 0, :], HD ** -0.5, None, ALU.mult))
                dve.wait_ge(gsig_ready, 1)

                def normalise(w):
                    s, h = w // MH, w % MH
                    num = ps[:, 6:8, 0:SB * (HD + 1)].rearrange("p d (j e) -> p d j e", j=SB)
                    dve.wait_ge(num_psum, w + 1)
                    link(dve.tensor_copy(dn[:].unsqueeze(3), num[:, :, :, HD:HD + 1]))
                    link(dve.scalar_tensor_tensor(rc[:], dn[:], -1.0, dn[:], ALU.mult, ALU.max))
                    link(dve.tensor_tensor(
                        rc[:], rc[:], EM[:, s * SB:(s + 1) * SB, h:h + 33:32].rearrange("p t d -> p d t"), ALU.max))
                    link(dve.reciprocal(rc[:], rc[:]))
                    dve.tensor_tensor(t12[:], num[:, :, :, 0:HD], rc[:].unsqueeze(3).to_broadcast([P, 2, SB, HD]),
                                      ALU.mult).then_inc(ml_evac, 1)
                    dve.wait_ge(ml_evac, w + 1)
                    link(dve.tensor_tensor(hs[:], t12[:, 0, :, :], t12[:, 1, :, :], ALU.add))
                    cs = co[:, s * SB:(s + 1) * SB, h * HD:(h + 1) * HD]
                    dve.wait_ge(msig_ready, 1)
                    link(dve.tensor_tensor(cs, cs, hs[:], ALU.mult))

                for w in range(N_ML):
                    for d in range(2):
                        dve.wait_ge(rb_psum, 2 * w + d + 1)
                        if w >= 1:
                            dve.wait_ge(dt_ready, 2 * SB * w)
                        dve.tensor_tensor(mR[:, d, :].rearrange("p (j t) -> p j t", j=SB),
                                          ps[:, 4 + d, :].rearrange("p (j t) -> p j t", j=SB),
                                          mmask[:, d:d + 1, :].to_broadcast([P, SB, P]), ALU.add).then_inc(mr_ready, 1)
                    if w + 1 < N_ML:
                        stack_lo(w + 1)
                    if w == 0:
                        gla_norm()
                    if w >= 1:
                        normalise(w - 1)
                    for i in range(SB):
                        dve.wait_ge(qk_psum, SB * w + i + 1)
                        for d in range(2):
                            lo, hi = fwd_or_bwd_range(d, i)
                            dve.wait_ge(dt_ready, 2 * SB * w + 2 * i + d + 1)
                            D_t = Dts[w % 2][:, d, i, lo:hi]
                            dve.scalar_tensor_tensor(D_t, ps[:, i, lo:hi], HD ** -0.5, D_t, ALU.mult,
                                                     ALU.mult).then_inc(wt_ready, 1)
                normalise(N_ML - 1)
                dve.wait_ge(gla_done, 1)
                dve.sem_inc(heads_gated, 1)
                for hb in range(2):
                    dve.wait_ge(msq_ready, hb + 1)
                    dve.tensor_reduce(mss[:, 0, hb * 16:(hb + 1) * 16],
                                      Dt0[:, hb, 0:2, :].rearrange("p a b -> p (a b)").rearrange("p (a d) -> p a d", d=HD),
                                      AX_X, ALU.add).then_inc(mss_ready, 1)
                dve.wait_ge(mrms_ready, 1)
                link(dve.reciprocal(mss[:, 0, :], mss[:, 1, :]))
                ca = co[:].rearrange("p t (h d) -> p (t h) d", d=HD)
                dve.tensor_tensor(ca, ca, mss[:, 0, :].unsqueeze(2).to_broadcast([P, TT * MH, HD]), ALU.mult)\
                   .then_inc(ml_done, 1)
                dve.wait_ge(ml_done, 1)

                split_lo(N_IN)
                for tt in range(TT):
                    tok = slice(tt * P, (tt + 1) * P)
                    bank = 4 + tt % 2 * 2
                    dve.wait_ge(mixh_ready, 3 * tt + 1)
                    dve.tensor_tensor(hl[:, 0:4, tok], ps[:, bank, :].rearrange("p (i t) -> p i t", i=4),
                                      hh[:, 0:4, tok].bitcast(F32), ALU.subtract).then_inc(mixl_ready, 1)
                    dve.wait_ge(mixh_ready, 3 * tt + 3)
                    for i, g in enumerate((V_GLAN, V_MLN)):
                        dve.scalar_tensor_tensor(
                            hl[:, 4 + 2 * i:6 + 2 * i, tok],
                            ps[:, bank + 1, 2 * i * P:(2 * i + 2) * P].rearrange("p (i t) -> p i t", i=2),
                            vec[:, g:g + 1], hh[:, 4 + 2 * i:6 + 2 * i, tok].bitcast(F32), ALU.mult,
                            ALU.subtract).then_inc(mixl_ready, 1)
                for u in range(N_IN + 1, N_IN + SPLIT):
                    split_lo(u)
                dve.wait_ge(reloaded, 16)
                for o in range(KT):
                    dve.wait_ge(wo_psum, o + 1)
                    dve.tensor_tensor(x[:, o, :], x[:, o, :], ps[:, o % 3 * 2:o % 3 * 2 + 2, :].rearrange("p s t -> p (s t)"),
                                      ALU.add).then_inc(wo_done, 1)
                    if o >= 1:
                        add_squares(o - 1, sq_ready, sq_used)
                    if o + SPLIT < KT:
                        split_lo(N_IN + SPLIT + o)
                add_squares(KT - 1, sq_ready, sq_used)

                def ffn_lo(kind, j):
                    dve.wait_ge(f_hi[kind], j + 1)
                    dve.tensor_tensor(wlo[:, kind, :, :], raw[:, kind, :].rearrange("p (k c) -> p k c", k=KT),
                                      whi[:, kind, :, :].bitcast(F32), ALU.subtract).then_inc(f_lo[kind], 1)

                for kind in (0, 1):
                    ffn_lo(kind, 0)
                norm(1, V_FFN)

                def conv(acc, pair, taps, init, half, done, j):
                    dve.wait_ge(init, j + 1)
                    dve.scalar_tensor_tensor(acc[:, :, 1:SEQ], ps[:, pair:pair + 2, 0:SEQ - 1], cw[:, taps:taps + 1],
                                             acc[:, :, 1:SEQ], ALU.mult, ALU.add).then_inc(half, 1)
                    dve.wait_ge(half, j + 1)
                    dve.scalar_tensor_tensor(acc[:, :, 0:SEQ - 1], ps[:, pair:pair + 2, 1:SEQ], cw[:, taps + 2:taps + 3],
                                             acc[:, :, 0:SEQ - 1], ALU.mult, ALU.add).then_inc(done, 1)

                def add_down(j, last=False):
                    for o in range(KT):
                        for s in range(NSEQ):
                            dve.wait_ge(d_psum, j * (NSEQ * KT) + (o * NSEQ + s + 1))
                            xs = x[:, o, s * SEQ:(s + 1) * SEQ]
                            dve.tensor_tensor(xs, xs, ps[:, 4 + o % 2 * 2 + s, :], ALU.add).then_inc(d_done, 1)
                        if last and o >= 1:
                            add_squares(o - 1, sq_ready, sq_used, KT)

                def iteration(j, first=False, last=False):
                    conv(accg, 0, 0, g_init, g_half, g_conv, j)
                    if not last:
                        ffn_lo(0, j + 1)
                    if not first:
                        add_down(j - 1)
                    conv(accv, 2, 4, v_init, v_half, v_conv, j)
                    if not last:
                        ffn_lo(1, j + 1)
                    dve.wait_ge(sil_ready, j + 1)
                    dve.wait_ge(v_conv, j + 1)
                    dve.tensor_tensor(accv[:], accv[:], sil[:], ALU.mult).then_inc(act_ready, 1)
                    ffn_lo(2, j)
                    dve.wait_ge(acth_ready, j + 1)
                    dve.tensor_tensor(actl[:], accv[:], acth[:].bitcast(F32), ALU.subtract).then_inc(actl_ready, 1)

                iteration(0, first=True)
                with dve.Fori(1, FT - 1) as j:
                    iteration(j)
                iteration(FT - 1, last=True)
                add_down(FT - 1, last=True)
                add_squares(KT - 1, sq_ready, sq_used, KT)
                diagonals(rms_ready, 2, rinv_ready, diag_ready)
                dve.sem_inc(layer_end, 1)
                dve.wait_ge(layer_go, l + 1)


def axial_tables():
    pos = np.arange(SEQ)
    row = (pos // GRID_W).astype(np.float32)
    col = (pos % GRID_W).astype(np.float32)
    n = HD // 4
    inv = np.power(np.float32(ROPE_THETA), -np.arange(n, dtype=np.float32) / np.float32(n)).astype(np.float32)
    ang = np.stack([row[:, None] * inv, col[:, None] * inv], axis=1)
    c, s = np.cos(ang), np.sin(ang)
    cos = np.stack([c, c], axis=2).reshape(SEQ, HD)
    sin = np.stack([s, -s], axis=2).reshape(SEQ, HD)
    lay = lambda t: t.reshape(SB, P, HD).transpose(1, 0, 2)
    return np.ascontiguousarray(np.stack([lay(cos), lay(sin)])).astype(np.float32)


def masks():
    s, t = np.arange(P)[:, None], np.arange(P)[None, :]
    same = (s // CH) == (t // CH)
    gla = np.stack([same & (s <= t), same & (s >= t)], axis=1).astype(np.uint32)
    chunk = np.broadcast_to((np.arange(SEQ) % CH != 0).astype(np.float32), (P, SEQ))
    ml = np.stack([np.where(s <= t, 0.0, -1e30), np.where(s >= t, 0.0, -1e30)], axis=1).astype(np.float32)
    sel = np.zeros((RROWS, 2 * MH, P), np.float32)
    for d in range(2):
        for h in range(MH):
            sel[32 * d + h, d * MH + h, :] = 1.0
            sel[64 + 32 * d + h, d * MH + h, :] = 1.0
    return gla, np.ascontiguousarray(chunk), ml, sel


def layouts(i):
    f = np.asarray
    x = np.concatenate([f(i["x_prompt"])[0], f(i["x_sample"])[0]], axis=0)
    x_in = np.ascontiguousarray(x.T.reshape(KT, P, T).transpose(1, 0, 2))
    w_in = f(i["w_in"])
    small = np.zeros((DEPTH, D, P), np.float32)
    for d in range(2):
        small[:, :, 32 * d:32 * d + MH] = w_in[:, :, CG + d * MH:CG + (d + 1) * MH]
        small[:, :, BA_ROW[d]:BA_ROW[d] + 16] = w_in[:, :, BA + 16 * d:BA + 16 * (d + 1)]
        small[:, :, 64 + 32 * d:64 + 32 * d + MH] = w_in[:, :, CG + (2 + d) * MH:CG + (3 + d) * MH]
    cols = [c + o for c in TOK_COLS for o in (0, P)] + FEAT_COLS
    unit = lambda w: w.reshape(DEPTH, KT, P, P).transpose(0, 2, 1, 3).reshape(DEPTH, P, UNIT)
    units = [unit(w_in[:, :, c:c + P]) for c in cols] + [unit(small)]
    w_out = f(i["w_out"])
    units += [unit(w_out[:, :, o * P:(o + 1) * P]) for o in range(KT)]
    w_units = np.ascontiguousarray(np.stack(units, axis=1))
    up = f(i["w_up"]).reshape(DEPTH, KT, P, 2, FT, P).transpose(0, 4, 3, 2, 1, 5).reshape(DEPTH, FT, 2, P, UNIT)
    down = f(i["w_down"]).reshape(DEPTH, FT, 1, P, UNIT)
    w_ffn = np.ascontiguousarray(np.concatenate([up, down], axis=2))
    vecs = np.zeros((DEPTH, P, NVEC), np.float32)
    vecs[:, :, V_MIX:V_MIX + KT] = f(i["norm_mix_g"]).reshape(DEPTH, KT, P).transpose(0, 2, 1)
    vecs[:, :, V_FFN:V_FFN + KT] = f(i["norm_ffn_g"]).reshape(DEPTH, KT, P).transpose(0, 2, 1)
    vecs[:, :, V_GLAN] = np.tile(f(i["gla_norm_g"]), (1, 2))
    vecs[:, :, V_MLN] = np.tile(f(i["mlstm_norm_g"]), (1, 2))
    vecs[:, :, V_GB:V_GB + 4] = f(i["gla_gate_b"]).reshape(DEPTH, 4, P).transpose(0, 2, 1)
    gb = f(i["mlstm_gate_b"])
    for d in range(2):
        vecs[:, 32 * d:32 * d + MH, V_GBI] = gb[:, d]
        vecs[:, 64 + 32 * d:64 + 32 * d + MH, V_GBF] = gb[:, 2 + d]
    w2p = np.zeros((DEPTH, P, 2, 256), np.float32)
    for d in range(2):
        w2p[:, BA_ROW[d]:BA_ROW[d] + 16, d, :] = f(i["gla_gate_w2"])[:, d]
    qkg = np.stack([f(i["attn_qn_g"]), f(i["attn_kn_g"])], axis=1)
    qkg = np.ascontiguousarray(np.broadcast_to(qkg[:, None], (DEPTH, P, 2, HD)))
    taps = np.concatenate([f(i["conv_w"]), f(i["conv_b"])[:, None]], axis=1)
    convp = np.ascontiguousarray(taps.reshape(DEPTH, 4, 2, FT, P).transpose(0, 4, 3, 2, 1).reshape(DEPTH, P, FT, 8))
    gla, chunk, ml, sel = masks()
    return {"x_in": x_in, "w_units": w_units, "w_ffn": w_ffn, "vecs": vecs, "w2p": w2p, "qkg": qkg,
            "convp": convp, "rope": axial_tables(), "gmask": gla, "chunkmask": chunk, "lmask": ml,
            "sel": sel, "ident_in": np.eye(P, dtype=np.float32)}


def kernel(**inputs):
    import concourse.bacc as bacc
    from concourse.bass_utils import run_bass_kernel_spmd as run

    arrays = layouts(inputs)
    nc = bacc.Bacc("TRN2", target_bir_lowering=False, num_devices=1)
    args = [nc.dram_tensor(f"d_{n}", a.shape, mybir.dt.from_np(a.dtype), kind="ExternalInput").ap()
            for n, a in arrays.items()]
    out = nc.dram_tensor("d_x_out", (P, KT, T), F32, kind="ExternalOutput").ap()
    build(nc, *args, out)
    r = run(nc, [{f"d_{n}": a for n, a in arrays.items()}], core_ids=[0])
    y = r.results[0]["d_x_out"].transpose(1, 0, 2).reshape(D, T)
    return (np.ascontiguousarray(y[:, 0:SEQ].T)[None], np.ascontiguousarray(y[:, SEQ:T].T)[None])
```
